# Optimizing a Trainium2 kernel written in Bass

```python
import math
import jax
import jax.numpy as jnp
from jax import lax
import numpy as np

D_MODEL = 1024
BATCH = 1
SEQ = 512
DEPTH = 1
DEC_BATCH = 1
DEC_SEQ = 64
PAST_LEN = 512

CHUNK = 64
MIX_WIDTH = D_MODEL
R_WIDTH = MIX_WIDTH // 2
R_HEAD = 64
R_HEADS = R_WIDTH // R_HEAD
DECAY_LORA = 64
AAA_LORA = 64
GATE_LORA = 128
R_PROJ = 3 * R_WIDTH + DECAY_LORA + AAA_LORA + GATE_LORA
R_GN_EPS = R_HEAD * 1e-5
M_WIDTH = MIX_WIDTH - R_WIDTH
M_HEADDIM = 64
M_HEADS = M_WIDTH // M_HEADDIM
M_GROUPS = 2
M_STATE = 64
CONV_W = 4
CONV_DIM = M_WIDTH + 2 * M_GROUPS * M_STATE
M_PROJ = M_WIDTH + CONV_DIM + M_HEADS
IN_PROJ = R_PROJ + M_PROJ
N_KEYS = 128
N_EXPERTS = N_KEYS * N_KEYS
P_HEADS = 8
P_QDIM = 256
P_TOPK = 16
PEER_BLOCK = 256
NORM_EPS = 1e-6

kernel_name = 'hymba_rwkv7_mamba2_peer_stream_step'

def rmsnorm(x, w):
    xf = x.astype(jnp.float32)
    y = xf * lax.rsqrt(jnp.mean(xf * xf, axis=-1, keepdims=True) + NORM_EPS)
    return (y * w.astype(jnp.float32)).astype(x.dtype)

def rwkv7_mixer(p, shift_state, wkv_state, mu, w0, w2, a0, a2, g2, k_k, k_a, r_k, ln_w, ln_b):
    bsz, t, _ = p.shape
    f32 = jnp.float32
    p_prev = jnp.concatenate([shift_state.astype(p.dtype)[:, None, :], p[:, :-1]], axis=1)
    pm = p + (p_prev - p) * mu
    r, k, v, wd, ad, gd = jnp.split(pm, [R_WIDTH, 2 * R_WIDTH, 3 * R_WIDTH, 3 * R_WIDTH + DECAY_LORA,
                                         3 * R_WIDTH + DECAY_LORA + AAA_LORA], axis=-1)
    w_log = -jax.nn.softplus(-(w0 + jnp.tanh(wd) @ w2).astype(f32)) - 0.5
    decay = jnp.exp(-jnp.exp(w_log))
    a = jax.nn.sigmoid((a0 + ad @ a2).astype(f32))
    g = (jax.nn.sigmoid(gd) @ g2).astype(f32)
    heads = lambda z: z.astype(f32).reshape(bsz, t, R_HEADS, R_HEAD)
    kk = heads(k * k_k)
    kk = kk / jnp.maximum(jnp.sqrt(jnp.sum(kk * kk, axis=-1, keepdims=True)), 1e-12)
    k_mod = heads(k.astype(f32) * (1.0 + (a - 1.0) * k_a.astype(f32)))
    rh, vh, wh, ah = heads(r), heads(v), heads(decay), heads(a)
    a_vec = -kk
    b_vec = kk * ah

    def step(S, inp):
        r_t, w_t, k_t, v_t, a_t, b_t = inp
        sa = jnp.einsum('bhvk,bhk->bhv', S, a_t)
        S = S * w_t[:, :, None, :] + sa[..., None] * b_t[:, :, None, :] + v_t[..., None] * k_t[:, :, None, :]
        return S, jnp.einsum('bhvk,bhk->bhv', S, r_t)

    seq_in = tuple(jnp.moveaxis(z, 1, 0) for z in (rh, wh, k_mod, vh, a_vec, b_vec))
    s_final, o = lax.scan(step, wkv_state.astype(f32), seq_in)
    o = jnp.moveaxis(o, 0, 1)
    mean = jnp.mean(o, axis=-1, keepdims=True)
    var = jnp.mean(jnp.square(o - mean), axis=-1, keepdims=True)
    o = ((o - mean) * lax.rsqrt(var + R_GN_EPS)).reshape(bsz, t, R_WIDTH)
    o = o * ln_w.astype(f32) + ln_b.astype(f32)
    bonus = jnp.sum(rh * k_mod * r_k.astype(f32), axis=-1, keepdims=True) * vh
    o = (o + bonus.reshape(bsz, t, R_WIDTH)) * g
    return o.astype(p.dtype), p[:, -1], s_final.astype(p.dtype)

def ssd_chunked(x, dt, A, Bm, Cm, h0):
    bsz, t, nh, hp = x.shape
    L = min(CHUNK, t)
    nc = t // L
    R = nh // M_GROUPS
    xdt = (x * dt[..., None]).reshape(bsz, nc, L, M_GROUPS, R, hp)
    cs = jnp.cumsum((dt * A).reshape(bsz, nc, L, M_GROUPS, R), axis=2)
    Bc = Bm.reshape(bsz, nc, L, M_GROUPS, M_STATE)
    Cc = Cm.reshape(bsz, nc, L, M_GROUPS, M_STATE)
    causal = jnp.tril(jnp.ones((L, L), dtype=bool))[None, None, :, :, None, None]
    seg = cs[:, :, :, None] - cs[:, :, None, :]
    decay_ls = jnp.exp(jnp.where(causal, seg, -jnp.inf))
    cb = jnp.einsum('bclgn,bcsgn->bclsg', Cc, Bc)
    y_diag = jnp.einsum('bclsg,bclsgr,bcsgrp->bclgrp', cb, decay_ls, xdt)
    to_end = jnp.exp(cs[:, :, -1:] - cs)
    chunk_states = jnp.einsum('bclgn,bclgr,bclgrp->bcgrpn', Bc, to_end, xdt)
    chunk_decay = jnp.exp(cs[:, :, -1])

    def step(h, inp):
        dec, st = inp
        return h * dec[..., None, None] + st, h

    h_last, h_in = lax.scan(step, h0.reshape(bsz, M_GROUPS, R, hp, M_STATE),
                            (jnp.moveaxis(chunk_decay, 1, 0), jnp.moveaxis(chunk_states, 1, 0)))
    h_in = jnp.moveaxis(h_in, 0, 1)
    y_off = jnp.einsum('bclgn,bcgrpn,bclgr->bclgrp', Cc, h_in, jnp.exp(cs))
    return (y_diag + y_off).reshape(bsz, t, nh, hp), h_last.reshape(bsz, nh, hp, M_STATE)

def mamba2_mixer(pm, conv_state, ssm_state, conv_w, conv_b, dt_bias, A_log, D, norm_w):
    bsz, t, _ = pm.shape
    f32 = jnp.float32
    z, xbc, dt = jnp.split(pm, [M_WIDTH, M_WIDTH + CONV_DIM], axis=-1)
    xbc_full = jnp.concatenate([conv_state.astype(xbc.dtype), xbc], axis=1)
    conv = lax.conv_general_dilated(xbc_full, conv_w.astype(xbc.dtype)[:, None, :], window_strides=(1,),
                                    padding='VALID', dimension_numbers=('NWC', 'WIO', 'NWC'),
                                    feature_group_count=CONV_DIM)
    xbc_act = jax.nn.silu((conv + conv_b).astype(f32))
    xs, Bm, Cm = jnp.split(xbc_act, [M_WIDTH, M_WIDTH + M_GROUPS * M_STATE], axis=-1)
    xs = xs.reshape(bsz, t, M_HEADS, M_HEADDIM)
    dt = jax.nn.softplus(dt.astype(f32) + dt_bias.astype(f32))
    A = -jnp.exp(A_log.astype(f32))
    y, h_last = ssd_chunked(xs, dt, A, Bm.reshape(bsz, t, M_GROUPS, M_STATE),
                            Cm.reshape(bsz, t, M_GROUPS, M_STATE), ssm_state.astype(f32))
    y = (y + D.astype(f32)[:, None] * xs).reshape(bsz, t, M_WIDTH) * jax.nn.silu(z.astype(f32))
    yg = y.reshape(bsz, t, M_GROUPS, M_WIDTH // M_GROUPS)
    yg = yg * lax.rsqrt(jnp.mean(yg * yg, axis=-1, keepdims=True) + NORM_EPS)
    y = yg.reshape(bsz, t, M_WIDTH) * norm_w.astype(f32)
    return y.astype(pm.dtype), xbc_full[:, -(CONV_W - 1):], h_last.astype(pm.dtype)

def peer_ffn(xn, w_q, sub_keys, u_tab, v_tab):
    bsz, t, _ = xn.shape
    q = (xn @ w_q).reshape(bsz, t, P_HEADS, 2, P_QDIM // 2)
    s = jnp.einsum('bthcd,ckd->bthck', q, sub_keys).astype(jnp.float32)
    sv, si = lax.top_k(s, P_TOPK)
    cand = (sv[..., 0, :, None] + sv[..., 1, None, :]).reshape(bsz, t, P_HEADS, P_TOPK * P_TOPK)
    cand_id = (si[..., 0, :, None] * N_KEYS + si[..., 1, None, :]).reshape(bsz, t, P_HEADS, P_TOPK * P_TOPK)
    top_s, top_pos = lax.top_k(cand, P_TOPK)
    eid = jnp.take_along_axis(cand_id, top_pos, axis=-1)
    gate = jax.nn.softmax(top_s, axis=-1).astype(xn.dtype)
    n = bsz * t
    nb = -(-n // PEER_BLOCK)
    pad = nb * PEER_BLOCK - n
    xt = jnp.pad(xn.reshape(n, D_MODEL), ((0, pad), (0, 0))).reshape(nb, PEER_BLOCK, D_MODEL)
    ei = jnp.pad(eid.reshape(n, P_HEADS * P_TOPK), ((0, pad), (0, 0))).reshape(nb, PEER_BLOCK, P_HEADS * P_TOPK)
    gt = jnp.pad(gate.reshape(n, P_HEADS * P_TOPK), ((0, pad), (0, 0))).reshape(nb, PEER_BLOCK, P_HEADS * P_TOPK)

    def block(args):
        xb, eb, gb = args
        hid = jnp.einsum('td,ted->te', xb, u_tab[eb])
        return jnp.einsum('te,ted->td', jax.nn.gelu(hid, approximate=False) * gb, v_tab[eb])

    out = lax.map(block, (xt, ei, gt))
    return out.reshape(nb * PEER_BLOCK, D_MODEL)[:n].reshape(bsz, t, D_MODEL)

def trunk_layer(x, shift_st, wkv_st, conv_st, ssm_st, norm1_w, w_in, rwkv_mu, rwkv_w0, rwkv_w2, rwkv_a0,
                rwkv_a2, rwkv_g2, rwkv_k_k, rwkv_k_a, rwkv_r_k, rwkv_ln_w, rwkv_ln_b, mamba_conv_w,
                mamba_conv_b, mamba_dt_bias, mamba_A_log, mamba_D, mamba_norm_w, w_out, norm2_w, peer_w_q,
                peer_sub_keys, peer_u, peer_v):
    proj = rmsnorm(x, norm1_w) @ w_in
    o_r, new_shift, new_wkv = rwkv7_mixer(proj[..., :R_PROJ], shift_st, wkv_st, rwkv_mu, rwkv_w0, rwkv_w2,
                                          rwkv_a0, rwkv_a2, rwkv_g2, rwkv_k_k, rwkv_k_a, rwkv_r_k,
                                          rwkv_ln_w, rwkv_ln_b)
    o_m, new_conv, new_ssm = mamba2_mixer(proj[..., R_PROJ:], conv_st, ssm_st, mamba_conv_w, mamba_conv_b,
                                          mamba_dt_bias, mamba_A_log, mamba_D, mamba_norm_w)
    h = x + jnp.concatenate([o_r, o_m], axis=-1) @ w_out
    h = h + peer_ffn(rmsnorm(h, norm2_w), peer_w_q, peer_sub_keys, peer_u, peer_v)
    return h, new_shift, new_wkv, new_conv, new_ssm

def setup_inputs(seed: int = 0) -> dict:
    key = jax.random.key(seed)
    ks = jax.random.split(key, 40)
    nrm = lambda k, shape, scale: jax.random.normal(k, shape, jnp.float32) * scale
    dt0 = jnp.exp(jax.random.uniform(ks[20], (DEPTH, M_HEADS), jnp.float32) * (math.log(0.1) - math.log(0.001))
                  + math.log(0.001))
    return {
        'x_prompt': nrm(ks[0], (BATCH, SEQ, D_MODEL), 1.0),
        'x_sample': nrm(ks[1], (DEC_BATCH, DEC_SEQ, D_MODEL), 1.0),
        'state_rwkv_shift': nrm(ks[2], (DEPTH, DEC_BATCH, R_PROJ), 1.0),
        'state_rwkv_wkv': nrm(ks[3], (DEPTH, DEC_BATCH, R_HEADS, R_HEAD, R_HEAD), 0.5),
        'state_mamba_conv': nrm(ks[4], (DEPTH, DEC_BATCH, CONV_W - 1, CONV_DIM), 1.0),
        'state_mamba_ssm': nrm(ks[5], (DEPTH, DEC_BATCH, M_HEADS, M_HEADDIM, M_STATE), 0.5),
        'norm1_w': 1.0 + nrm(ks[6], (DEPTH, D_MODEL), 0.01),
        'w_in': nrm(ks[7], (DEPTH, D_MODEL, IN_PROJ), D_MODEL ** -0.5),
        'rwkv_mu': jax.random.uniform(ks[8], (DEPTH, R_PROJ), jnp.float32, 0.2, 0.8),
        'rwkv_w0': nrm(ks[9], (DEPTH, R_WIDTH), 0.5),
        'rwkv_w2': nrm(ks[10], (DEPTH, DECAY_LORA, R_WIDTH), 0.5 * DECAY_LORA ** -0.5),
        'rwkv_a0': nrm(ks[11], (DEPTH, R_WIDTH), 0.5),
        'rwkv_a2': nrm(ks[12], (DEPTH, AAA_LORA, R_WIDTH), 0.5 * AAA_LORA ** -0.5),
        'rwkv_g2': nrm(ks[13], (DEPTH, GATE_LORA, R_WIDTH), GATE_LORA ** -0.5),
        'rwkv_k_k': 0.85 + nrm(ks[14], (DEPTH, R_WIDTH), 0.1),
        'rwkv_k_a': 1.0 + nrm(ks[15], (DEPTH, R_WIDTH), 0.1),
        'rwkv_r_k': nrm(ks[16], (DEPTH, R_HEADS, R_HEAD), 0.1),
        'rwkv_ln_w': 1.0 + nrm(ks[17], (DEPTH, R_WIDTH), 0.01),
        'rwkv_ln_b': nrm(ks[18], (DEPTH, R_WIDTH), 0.01),
        'mamba_conv_w': nrm(ks[19], (DEPTH, CONV_W, CONV_DIM), CONV_W ** -0.5),
        'mamba_conv_b': nrm(ks[21], (DEPTH, CONV_DIM), 0.01),
        'mamba_dt_bias': dt0 + jnp.log(-jnp.expm1(-dt0)),
        'mamba_A_log': jnp.log(jax.random.uniform(ks[22], (DEPTH, M_HEADS), jnp.float32, 1.0, 16.0)),
        'mamba_D': 1.0 + nrm(ks[23], (DEPTH, M_HEADS), 0.1),
        'mamba_norm_w': 1.0 + nrm(ks[24], (DEPTH, M_WIDTH), 0.01),
        'w_out': nrm(ks[25], (DEPTH, MIX_WIDTH, D_MODEL), MIX_WIDTH ** -0.5),
        'norm2_w': 1.0 + nrm(ks[26], (DEPTH, D_MODEL), 0.01),
        'peer_w_q': nrm(ks[27], (DEPTH, D_MODEL, P_HEADS * P_QDIM), D_MODEL ** -0.5),
        'peer_sub_keys': nrm(ks[28], (DEPTH, 2, N_KEYS, P_QDIM // 2), (P_QDIM // 2) ** -0.5),
        'peer_u': nrm(ks[29], (DEPTH, N_EXPERTS, D_MODEL), D_MODEL ** -0.5),
        'peer_v': nrm(ks[30], (DEPTH, N_EXPERTS, D_MODEL), 0.3),
        'final_norm_w': 1.0 + nrm(ks[31], (D_MODEL,), 0.01),
    }

def reference(x_prompt, x_sample, state_rwkv_shift, state_rwkv_wkv, state_mamba_conv, state_mamba_ssm,
              norm1_w, w_in, rwkv_mu, rwkv_w0, rwkv_w2, rwkv_a0, rwkv_a2, rwkv_g2, rwkv_k_k, rwkv_k_a,
              rwkv_r_k, rwkv_ln_w, rwkv_ln_b, mamba_conv_w, mamba_conv_b, mamba_dt_bias, mamba_A_log, mamba_D,
              mamba_norm_w, w_out, norm2_w, peer_w_q, peer_sub_keys, peer_u, peer_v, final_norm_w):
    layer_weights = (norm1_w, w_in, rwkv_mu, rwkv_w0, rwkv_w2, rwkv_a0, rwkv_a2, rwkv_g2, rwkv_k_k, rwkv_k_a,
                     rwkv_r_k, rwkv_ln_w, rwkv_ln_b, mamba_conv_w, mamba_conv_b, mamba_dt_bias, mamba_A_log,
                     mamba_D, mamba_norm_w, w_out, norm2_w, peer_w_q, peer_sub_keys, peer_u, peer_v)
    bp = x_prompt.shape[0]
    dtp = x_prompt.dtype
    z_shift = jnp.zeros((bp, R_PROJ), dtp)
    z_wkv = jnp.zeros((bp, R_HEADS, R_HEAD, R_HEAD), dtp)
    z_conv = jnp.zeros((bp, CONV_W - 1, CONV_DIM), dtp)
    z_ssm = jnp.zeros((bp, M_HEADS, M_HEADDIM, M_STATE), dtp)
    hp, hs = x_prompt, x_sample
    new_p = ([], [], [], [])
    new_s = ([], [], [], [])
    for l in range(DEPTH):
        lw = [w[l] for w in layer_weights]
        hp, *sp = trunk_layer(hp, z_shift, z_wkv, z_conv, z_ssm, *lw)
        hs, *ss = trunk_layer(hs, state_rwkv_shift[l], state_rwkv_wkv[l], state_mamba_conv[l],
                              state_mamba_ssm[l], *lw)
        for acc, val in zip(new_p, sp):
            acc.append(val)
        for acc, val in zip(new_s, ss):
            acc.append(val)
    y_prompt = rmsnorm(hp, final_norm_w)
    y_sample = rmsnorm(hs, final_norm_w)
    return (y_prompt, y_sample,
            jnp.stack(new_p[0]), jnp.stack(new_p[1]), jnp.stack(new_p[2]), jnp.stack(new_p[3]),
            jnp.stack(new_s[0]), jnp.stack(new_s[1]), jnp.stack(new_s[2]), jnp.stack(new_s[3]))


_drawn_inputs = setup_inputs


def setup_inputs(seed=0):
    import zlib

    import numpy as np

    out = dict(_drawn_inputs(seed))
    spreads = {}
    factors = {'norm1_w': 3.377,
     'rwkv_ln_w': 51.864,
     'rwkv_ln_b': 53.966,
     'mamba_conv_b': 12.968,
     'mamba_norm_w': 35.98,
     'norm2_w': 29.451,
     'final_norm_w': 33.661,
     'mamba_D': 8.0}
    for name, (base, spread) in spreads.items():
        noise = np.random.default_rng([zlib.crc32(name.encode()), seed]).standard_normal(out[name].shape)
        drawn = base * np.exp(spread * noise) if base else spread * noise
        out[name] = jnp.asarray(drawn.astype(out[name].dtype))
    for name, factor in factors.items():
        out[name] = (out[name] * factor).astype(out[name].dtype)
    return out
```

```python
from contextlib import ExitStack

import numpy as np

import concourse.bass as bass
from concourse import mybir

F32 = mybir.dt.float32
F32R = mybir.dt.float32r
U32 = mybir.dt.uint32
ALU = mybir.AluOpType
ACT = mybir.ActivationFunctionType
AX_X = mybir.AxisListType.X

P = 128
D_MODEL = 1024
SEQ = 512
DEC_SEQ = 64
TOK = SEQ + DEC_SEQ
HALF = TOK // 2
DT = D_MODEL // P
R_WIDTH = 512
M_WIDTH = 512
HEADS = 8
HD = 64
R_PROJ = 1792
CONV_DIM = 768
CONV_W = 4
RT = R_PROJ // P
XT_ = CONV_DIM // P
ZT = M_WIDTH // P
NCT = RT + XT_ + ZT + 1
N_KEYS = 128
P_HEADS = 8
TOPK = 16
SEL = P_HEADS * TOPK
NORM_EPS = 1e-6
GN_EPS = HD * 1e-5
DECAY_SCALE = -float(np.exp(-0.5))
LOWEST = -3.0e38
RWIN = SEQ + 1 + DEC_SEQ
XWIN = SEQ + CONV_W - 1 + DEC_SEQ
TILES = [(0, P, 0, 0), (P, P, P, P), (2 * P, P, 2 * P, 2 * P), (3 * P, P, 3 * P, 3 * P),
         (SEQ, DEC_SEQ, SEQ + 1, SEQ + CONV_W - 1)]
NT = len(TILES)
LEVELS = 7
JJ = 4
NG = N_KEYS // JJ
TB = 32

C_ID, C_ONE, C_TRI, C_REV, C_DINC, C_DEXC = (P * n for n in range(6))
C_MS, C_LT0, C_LEV = (P * n for n in range(6, 9))
C_DCOL = C_LEV + P * LEVELS
C_N = C_DCOL + 2


def shape_constants():
    c = np.zeros((P, C_N), np.float32)
    s = np.arange(P)[:, None]
    t = np.arange(P)[None, :]
    c[:, C_ID:C_ID + P] = s == t
    c[:, C_ONE:C_ONE + P] = 1
    c[:, C_TRI:C_TRI + P] = s <= t
    c[:, C_REV:C_REV + P] = s > t
    mid = (s <= HD - 1)
    c[:, C_DINC:C_DINC + P] = DECAY_SCALE * ((s <= t).astype(np.float32) - mid)
    c[:, C_DEXC:C_DEXC + P] = DECAY_SCALE * ((s < t).astype(np.float32) - mid)
    c[:, C_MS:C_MS + P] = s < t
    for n in range(LEVELS):
        b = 1 << n
        m = ((s // (2 * b) == t // (2 * b)) & (s // b > t // b)) | (s == t)
        c[:, C_LEV + P * n:C_LEV + P * (n + 1)] = m if n else m & (s != t)
        if n == 0:
            c[:, C_LT0:C_LT0 + P] = m.T
    c[:, C_DCOL] = DECAY_SCALE * mid[:, 0]
    c[:, C_DCOL + 1] = DECAY_SCALE * (~mid[:, 0])
    return c


def bc(ap, axis, shape):
    return ap.unsqueeze(axis).broadcast_to(shape)


def three_products(pe, out, ah, al, bh, bl, first, last):
    pe.matmul(out, ah, bh, start=first, stop=False)
    pe.matmul(out, ah, bl, start=False, stop=False)
    return pe.matmul(out, al, bh, start=False, stop=last)


class Acts:

    def __init__(self, core, ctx, name):
        self.x = core.sb(name + "_x", [P, DT, TOK], ctx=ctx)
        self.hi = core.sb(name + "_hi", [P, DT, TOK], F32R, ctx=ctx)
        self.lo = core.sb(name + "_lo", [P, DT, TOK], F32R, ctx=ctx)


class Core:

    def __init__(self, nc, ctx, a):
        self.nc, self.ctx, self.a = nc, ctx, a
        self.psum = ctx.enter_context(nc.psum_tensor("banks", [P, 8, 512], F32))
        self.ident = self.sb("ident", [P, P])
        self.ones = self.sb("ones", [P, P])
        self.norms = self.sb("norms", [P, 3, DT])

    def sb(self, name, shape, dt=F32, ctx=None):
        return (ctx or self.ctx).enter_context(self.nc.sbuf_tensor(name, shape, dt))

    def sem(self, name):
        return self.ctx.enter_context(self.nc.semaphore(name))

    def bank(self, n):
        return self.psum[:, n % 8, :]


class Chain:

    def __init__(self, eng, sem):
        self.eng, self.sem, self.n = eng, sem, 0

    def __call__(self, ins):
        ins.then_inc(self.sem, 1)
        self.n += 1
        self.eng.wait_ge(self.sem, self.n)


class Gemm:

    def __init__(self, core, ctx, name, acts, count, dram, banks=(0, 1, 2, 3)):
        self.acts = acts
        self.core, self.count, self.dram, self.banks = core, count, dram, banks
        self.raw = core.sb(name + "_raw", [P, 3, DT * P], ctx=ctx)
        self.wh = core.sb(name + "_wh", [P, 2, DT * P], F32R, ctx=ctx)
        self.wl = core.sb(name + "_wl", [P, 2, DT * P], F32R, ctx=ctx)
        self.loaded = [core.sem(f"{name}_loaded{n}") for n in range(3)]
        self.high = core.sem(name + "_high")
        self.low = core.sem(name + "_low")
        self.done = core.sem(name + "_done")
        self.taken = core.sem(name + "_taken")

    def load(self, sp, c):
        if c >= 3:
            sp.wait_ge(self.low, c - 2)
        sp.dma_start(self.raw[:, c % 3, :], self.dram[c]).then_inc(self.loaded[c % 3], 16)

    def split_high(self, act, c):
        act.wait_ge(self.loaded[c % 3], 16 * (c // 3 + 1))
        if c >= 2:
            act.wait_ge(self.done, c - 1)
        act.activation(self.wh[:, c % 2, :], self.raw[:, c % 3, :], ACT.Copy).then_inc(self.high, 1)

    def split_low(self, pool, c):
        pool.wait_ge(self.high, c + 1)
        pool.tensor_tensor(self.wl[:, c % 2, :], self.raw[:, c % 3, :],
                           self.wh[:, c % 2, :].bitcast(F32), ALU.subtract).then_inc(self.low, 1)

    def multiply(self, pe, c):
        pe.wait_ge(self.low, c + 1)
        if c >= 2:
            pe.wait_ge(self.taken, c - 1)
        for half in range(2):
            out = self.core.psum[:, self.banks[2 * (c % 2) + half], 0:HALF]
            cols = slice(half * HALF, (half + 1) * HALF)
            for dt in range(DT):
                w = slice(dt * P, (dt + 1) * P)
                ins = three_products(pe, out, self.wh[:, c % 2, w], self.wl[:, c % 2, w],
                                     self.acts.hi[:, dt, cols], self.acts.lo[:, dt, cols],
                                     dt == 0, dt == DT - 1)
        ins.then_inc(self.done, 1)

    def out(self, c, half):
        return self.core.psum[:, self.banks[2 * (c % 2) + half], 0:HALF]


class Norm:

    def __init__(self, core, ctx, name, acts, which, halves, bank):
        self.acts = acts
        self.core, self.which, self.halves, self.b = core, which, halves, bank
        self.sq = core.sb(name + "_sq", [P, 2, TOK], ctx=ctx)
        self.mean = core.sb(name + "_mean", [P, TOK], ctx=ctx)
        self.root = core.sb(name + "_root", [P, TOK], ctx=ctx)
        self.inv = core.sb(name + "_inv", [P, TOK], ctx=ctx)
        self.ny = 2 if halves else DT
        self.y = core.sb(name + "_y", [P, self.ny, TOK], ctx=ctx)
        self.squared = core.sem(name + "_squared")
        self.summed = core.sem(name + "_summed")
        self.meaned = core.sem(name + "_meaned")
        self.rooted = core.sem(name + "_rooted")
        self.scaled = core.sem(name + "_scaled")
        self.high = core.sem(name + "_high")
        self.low = core.sem(name + "_low")

    def act_squares(self, act, ready=None):
        for dt in range(DT):
            if ready is not None:
                act.wait_ge(*ready(dt))
            if dt >= 2:
                act.wait_ge(self.summed, dt - 1)
            act.activation(self.sq[:, dt % 2, :], self.acts.x[:, dt, :], ACT.Square).then_inc(self.squared, 1)

    def pe_sums(self, pe):
        for dt in range(DT):
            pe.wait_ge(self.squared, dt + 1)
            for half in range(2):
                ins = pe.matmul(self.core.psum[:, self.b + half, 0:HALF], self.core.ones[:, :],
                                self.sq[:, dt % 2, half * HALF:(half + 1) * HALF],
                                start=dt == 0, stop=dt == DT - 1)
            ins.then_inc(self.summed, 1)

    def act_root(self, act):
        act.wait_ge(self.meaned, 2)
        act.activation(self.root[:, :], self.mean[:, :], ACT.Sqrt).then_inc(self.rooted, 1)

    def act_high(self, act):
        for dt in range(DT):
            act.wait_ge(self.scaled, dt + 2)
            act.activation(self.acts.hi[:, dt, :], self.y[:, dt % 2, :], ACT.Copy).then_inc(self.high, 1)

    def dve(self, dve):
        dve.wait_ge(self.summed, DT)
        for half in range(2):
            cols = slice(half * HALF, (half + 1) * HALF)
            dve.tensor_scalar(self.mean[:, cols], self.core.psum[:, self.b + half, 0:HALF],
                              1.0 / D_MODEL, NORM_EPS, ALU.mult, ALU.add).then_inc(self.meaned, 1)
        dve.wait_ge(self.rooted, 1)
        dve.reciprocal(self.inv[:, :], self.root[:, :]).then_inc(self.scaled, 1)
        dve.wait_ge(self.scaled, 1)
        for dt in range(DT):
            if dt >= self.ny:
                dve.wait_ge(self.low, dt - 1)
            dve.scalar_tensor_tensor(out=self.y[:, dt % self.ny, :], in0=self.acts.x[:, dt, :],
                                     scalar=self.core.norms[:, self.which, dt:dt + 1],
                                     in1=self.inv[:, :], op0=ALU.mult, op1=ALU.mult).then_inc(self.scaled, 1)
            if self.halves:
                dve.wait_ge(self.high, dt + 1)
                dve.tensor_tensor(self.acts.lo[:, dt, :], self.y[:, dt % 2, :],
                                  self.acts.hi[:, dt, :].bitcast(F32), ALU.subtract).then_inc(self.low, 1)


def project_in(core):
    nc, a = core.nc, core.a
    with ExitStack() as ctx:
        acts = Acts(core, ctx, "in")
        norm = Norm(core, ctx, "n1", acts, 0, True, 4)
        gemm = Gemm(core, ctx, "in", acts, NCT, a["w_in"])
        out = core.sb("row_out", [P, 3, XWIN], ctx=ctx)
        pr = core.sb("pr", [P, 2, RWIN + 1], ctx=ctx)
        px = core.sb("px", [P, 2, XWIN + CONV_W - 1], ctx=ctx)
        tmp = core.sb("tmp1", [P, 2, XWIN], ctx=ctx)
        par = core.sb("par1", [P, 3 * RT + XT_ * (CONV_W + 1 + CONV_W - 1)], ctx=ctx)
        mu, shift_in, = par[:, 0:RT], par[:, RT:2 * RT]
        cw = par[:, 3 * RT:3 * RT + XT_ * CONV_W].rearrange("p (x k) -> p x k", k=CONV_W)
        cb = par[:, 3 * RT + XT_ * CONV_W:3 * RT + XT_ * (CONV_W + 1)]
        cst = par[:, 3 * RT + XT_ * (CONV_W + 1):].rearrange("p (x k) -> p x k", k=CONV_W - 1)
        shift_out = core.sb("shift_out", [P, RT, 2], ctx=ctx)
        conv_out = core.sb("conv_out", [P, XT_, 2, CONV_W - 1], ctx=ctx)
        dtp = core.sb("dtp", [8, 4], ctx=ctx)
        dts = core.sb("dts", [8, 3, TOK], ctx=ctx)
        dto = core.sb("dt_out", [8, 2, TOK], ctx=ctx)
        x_in = core.sem("x_in")
        ones_in = core.sem("ones_in")
        par_in = core.sem("par_in")
        zeroed = core.sem("pads_zeroed")
        copied = core.sem("row_copied")
        mixed = core.sem("row_mixed")
        conved = core.sem("row_conved")
        tails = core.sem("tails_copied")
        silued = core.sem("row_silued")
        dtc = core.sem("dt_act")
        dtv = core.sem("dt_dve")
        stored = core.sem("tails_stored")
        sent = [core.sem(f"row_sent{n}") for n in range(3)]
        dchain = core.sem("dve_chain1")
        achain = core.sem("act_chain1")

        with nc.Block() as block:
            @block.sync
            def _(sp):
                sp.dma_start(core.ones[:, :], a["consts"][:, C_ONE:C_ONE + P]).then_inc(ones_in, 16)
                sp.dma_start(acts.x[:, :, :], a["x"]).then_inc(x_in, 16)
                for c in range(3):
                    gemm.load(sp, c)
                sp.dma_start(core.ident[:, :], a["consts"][:, C_ID:C_ID + P]).then_inc(par_in, 16)
                sp.dma_start(core.norms[:, :, :], a["norms"]).then_inc(par_in, 16)
                sp.dma_start(par[:, :], a["par1"]).then_inc(par_in, 16)
                sp.dma_start(dtp[:, 0:2], a["dtp"]).then_inc(par_in, 16)
                for c in range(NCT - 1):
                    if c + 3 < NCT:
                        gemm.load(sp, c + 3)
                    if c < RT:
                        sp.wait_ge(mixed, c + 1)
                        dst = a["pm"][:, c, :]
                    elif c < RT + XT_:
                        sp.wait_ge(silued, c - RT + 1)
                        dst = a["xbc"][:, c - RT, :]
                    else:
                        sp.wait_ge(gemm.taken, c + 1)
                        dst = a["z"][:, c - RT - XT_, :]
                    sp.dma_start(dst, out[:, c % 3, 0:dst.shape[1]]).then_inc(sent[c % 3], 16)
                sp.wait_ge(dtv, 1)
                sp.dma_start(a["dt"], dto[:, :, :]).then_inc(stored, 16)
                sp.wait_ge(tails, RT + XT_)
                sp.wait_ge(mixed, RT + XT_)
                sp.dma_start(a["shift_out"], shift_out[:, :, :]).then_inc(stored, 16)
                sp.dma_start(a["conv_out"], conv_out[:, :, :, :]).then_inc(stored, 16)
                sp.wait_ge(stored, 48)
                for n in range(3):
                    sp.wait_ge(sent[n], 16 * ((NCT - 1) // 3))

            @block.gpsimd
            def _(pool):
                pool.memset(pr[:, :, 0:1], 0.0).then_inc(zeroed, 1)
                pool.memset(px[:, :, 0:CONV_W - 1], 0.0).then_inc(zeroed, 1)
                for c in range(NCT):
                    gemm.split_low(pool, c)

            @block.tensor
            def _(pe):
                pe.wait_ge(ones_in, 16)
                norm.pe_sums(pe)
                pe.wait_ge(norm.low, DT)
                for c in range(NCT):
                    gemm.multiply(pe, c)

            @block.scalar
            def _(act):
                link = Chain(act, achain)
                norm.act_squares(act, ready=lambda dt: (x_in, 16))
                norm.act_root(act)
                gemm.split_high(act, 0)
                gemm.split_high(act, 1)
                norm.act_high(act)
                act.wait_ge(par_in, 64)
                act.wait_ge(zeroed, 2)

                def row_free(c):
                    if c >= 3:
                        act.wait_ge(sent[c % 3], 16 * (c // 3))

                link(act.activation(dtp[:, 2:3], dtp[:, 1:2], ACT.Exp))

                def silu(x):
                    act.wait_ge(conved, x + 1)
                    row_free(RT + x)
                    act.activation(out[:, (RT + x) % 3, :], tmp[:, 1, :], ACT.Silu, bias=cb[:, x:x + 1]).then_inc(silued, 1)

                for c in range(NCT):
                    act.wait_ge(gemm.done, c + 1)
                    a0, a1 = gemm.out(c, 0), gemm.out(c, 1)
                    n1 = SEQ - HALF
                    if c < RT:
                        if c >= 2:
                            act.wait_ge(mixed, c - 1)
                        row = pr[:, c % 2, :]
                        act.activation(row[:, SEQ + 1:SEQ + 2], shift_in[:, c:c + 1], ACT.Copy).then_inc(copied, 1)
                        act.activation(row[:, 1:1 + HALF], a0, ACT.Copy).then_inc(copied, 1)
                        act.activation(row[:, 1 + HALF:1 + SEQ], a1[:, 0:n1], ACT.Copy).then_inc(copied, 1)
                        act.activation(row[:, SEQ + 2:], a1[:, n1:], ACT.Copy).then_inc(gemm.taken, 1)
                    elif c < RT + XT_:
                        x = c - RT
                        if x >= 2:
                            act.wait_ge(mixed, c - 1)
                        row = px[:, x % 2, :]
                        g = CONV_W - 1
                        act.activation(row[:, g + SEQ:g + SEQ + g], cst[:, x, :], ACT.Copy).then_inc(copied, 1)
                        act.activation(row[:, g:g + HALF], a0, ACT.Copy).then_inc(copied, 1)
                        act.activation(row[:, g + HALF:g + SEQ], a1[:, 0:n1], ACT.Copy).then_inc(copied, 1)
                        act.activation(row[:, g + SEQ + g:], a1[:, n1:], ACT.Copy).then_inc(gemm.taken, 1)
                        if x >= 1:
                            silu(x - 1)
                    elif c < RT + XT_ + ZT:
                        if c == RT + XT_:
                            silu(XT_ - 1)
                        row_free(c)
                        act.activation(out[:, c % 3, 0:HALF], a0, ACT.Silu).then_inc(copied, 1)
                        act.activation(out[:, c % 3, HALF:TOK], a1, ACT.Silu).then_inc(gemm.taken, 1)
                    else:
                        act.activation(dts[:, 0, 0:HALF], a0[0:8, :], ACT.Identity, bias=dtp[:, 0:1]).then_inc(dtc, 1)
                        act.activation(dts[:, 0, HALF:], a1[0:8, :], ACT.Identity, bias=dtp[:, 0:1]).then_inc(gemm.taken, 1)
                        act.wait_ge(gemm.taken, NCT)
                        link(act.activation(dts[:, 1, :], dts[:, 0, :], ACT.Abs))
                        link(act.activation(dts[:, 2, :], dts[:, 1, :], ACT.Exp, scale=-1.0))
                        act.activation(dts[:, 1, :], dts[:, 2, :], ACT.Ln, bias=1.0).then_inc(dtc, 1)
                    if c + 2 < NCT:
                        gemm.split_high(act, c + 2)

            @block.vector
            def _(dve):
                link = Chain(dve, dchain)
                dve.wait_ge(par_in, 64)
                norm.dve(dve)
                dve.wait_ge(zeroed, 2)
                for c in range(RT):
                    dve.wait_ge(gemm.taken, c + 1)
                    row = pr[:, c % 2, :]
                    link(dve.tensor_tensor(tmp[:, 0, 0:RWIN], row[:, 0:RWIN], row[:, 1:], ALU.subtract))
                    dve.tensor_copy(shift_out[:, c, :], row[:, SEQ:SEQ + 2 + DEC_SEQ:DEC_SEQ + 1]).then_inc(tails, 1)
                    if c >= 3:
                        dve.wait_ge(sent[c % 3], 16 * (c // 3))
                    dve.scalar_tensor_tensor(out=out[:, c % 3, 0:RWIN], in0=tmp[:, 0, 0:RWIN], scalar=mu[:, c:c + 1],
                                             in1=row[:, 1:], op0=ALU.mult, op1=ALU.add).then_inc(mixed, 1)
                    dve.wait_ge(mixed, c + 1)
                for x in range(XT_):
                    c = RT + x
                    dve.wait_ge(gemm.taken, c + 1)
                    row = px[:, x % 2, :]
                    dve.tensor_copy(conv_out[:, x, 0, :], row[:, SEQ:SEQ + CONV_W - 1]).then_inc(tails, 1)
                    link(dve.tensor_scalar(tmp[:, 0, :], row[:, 0:XWIN], cw[:, x, 0:1], None, ALU.mult))
                    if x >= 1:
                        dve.wait_ge(silued, x)
                    link(dve.scalar_tensor_tensor(out=tmp[:, 1, :], in0=row[:, 1:1 + XWIN], scalar=cw[:, x, 1:2],
                                                  in1=tmp[:, 0, :], op0=ALU.mult, op1=ALU.add))
                    link(dve.scalar_tensor_tensor(out=tmp[:, 0, :], in0=row[:, 2:2 + XWIN], scalar=cw[:, x, 2:3],
                                                  in1=tmp[:, 1, :], op0=ALU.mult, op1=ALU.add))
                    dve.scalar_tensor_tensor(out=tmp[:, 1, :], in0=row[:, 3:3 + XWIN], scalar=cw[:, x, 3:4],
                                             in1=tmp[:, 0, :], op0=ALU.mult, op1=ALU.add).then_inc(conved, 1)
                    dve.wait_ge(conved, x + 1)
                    dve.tensor_copy(conv_out[:, x, 1, :], row[:, XWIN:XWIN + CONV_W - 1]).then_inc(mixed, 1)
                dve.wait_ge(mixed, RT + XT_)
                dve.wait_ge(dtc, 2)
                link(dve.tensor_scalar(dts[:, 0, :], dts[:, 0, :], 0.0, None, ALU.max))
                link(dve.tensor_tensor(dto[:, 0, :], dts[:, 0, :], dts[:, 1, :], ALU.add))
                dve.tensor_scalar(dto[:, 1, :], dto[:, 0, :], dtp[:, 2:3], -1.0, ALU.mult, ALU.mult).then_inc(dtv, 1)


def mixer_jobs():
    jobs = []
    for i in range(NT):
        top = LEVELS if TILES[i][1] == P else LEVELS - 1
        one = [("k", "act"), ("r", "act"), ("v", "act"), ("w", "dve"), ("a", "dve"), ("g", "act"),
               ("mx", "act"), ("mb", "act"), ("mz", "act"), ("cinc", "act"), ("cexc", "act"), ("dec", "act"),
               ("cs", "dve"), ("cb0", "dve"), ("cb1", "dve"), ("cst0", "dve"), ("cst1", "dve"),
               ("bT", "act"), ("kT", "act"), ("aT", "act"), ("rT", "act")]
        for e in range(2):
            one += [(f"ab{e}", "dve"), (f"m{e}", "dve"), (f"ak{e}", "dve"), (f"rb{e}", "dve"), (f"rk{e}", "dve")]
        for n in range(1, top):
            one += [(f"q{n}{e}", "dve") for e in range(2)]
            for e in range(2):
                one += [(f"x{n}{e}", "act")] * (n < top - 1) + [(f"t{n}{e}", "dve")]
            if n == 1:
                one += [("yo0", "dve"), ("yo1", "dve")]
            if n == 2:
                one += [("yd", "dve")]
            if n == 3:
                one += [("st", "dve")]
        one += [("y0", "act"), ("y1", "act"), ("u0", "act"), ("u1", "act"), ("o0", "act"), ("o1", "act"),
                ("s", "dve"), ("om", "act"), ("or", "act")]
        jobs += [(name, i, taker) for name, taker in one]
    return jobs


class Banks:

    def __init__(self, core, jobs):
        self.core = core
        self.done = core.sem("banks_done")
        self.taken = {"act": core.sem("banks_taken_act"), "dve": core.sem("banks_taken_dve")}
        self.number, self.order, count = {}, [], {"act": 0, "dve": 0}
        for n, (name, i, taker) in enumerate(jobs):
            count[taker] += 1
            self.number[name, i] = n
            self.order.append((self.taken[taker], count[taker]))

    def start(self, pe, name, i):
        n = self.number[name, i]
        if n >= 8:
            pe.wait_ge(*self.order[n - 8])
        return self.core.bank(n)

    def finish(self, ins):
        ins.then_inc(self.done, 1)

    def get(self, eng, name, i):
        n = self.number[name, i]
        eng.wait_ge(self.done, n + 1)
        return self.core.bank(n)

    def took(self, ins, name, i):
        ins.then_inc(self.order[self.number[name, i]][0], 1)

    def wait_taken(self, eng, name, i):
        eng.wait_ge(*self.order[self.number[name, i]])


def mix(core):
    nc, a = core.nc, core.a
    with ExitStack() as ctx:
        def sb(name, *shape, dt=F32):
            return core.sb(name, list(shape), dt, ctx)

        cst = sb("shape_constants", P, C_N)
        rows = sb("param_rows", P, 8, R_WIDTH)
        heads_row = sb("mamba_D", P, HEADS)
        w2 = sb("w2", P, R_WIDTH)
        g2 = sb("g2", P, R_WIDTH)
        kt, rt, vt, gt = (sb(n, P, HEADS, HD) for n in ("k_tok", "r_tok", "v_tok", "g_tok"))
        wa = sb("wa_sigmoid", P, 2, R_WIDTH)
        einc, eneg, eexc = (sb(n, P, HEADS, HD) for n in ("e_inc", "e_neg", "e_exc"))
        dec = sb("decay_cols", P, 4, 2)
        kk, km = sb("kk", P, HEADS, HD), sb("k_mod", P, HEADS, HD)
        bh, kh, ah, rh = (sb(n, P, R_WIDTH) for n in ("b_hat", "k_hat", "a_hat", "r_hat"))
        bT, kT, aT, rT = (sb(n, P, 4, P) for n in ("b_hatT", "k_hatT", "a_hatT", "r_hatT"))
        mT, ak, rb, rk = (sb(n, P, 2, 4, P) for n in ("mT", "akT", "rbT", "rkT"))
        xx, xt = sb("inv", P, 2, 4, P), sb("invT", P, 2, 4, P)
        pq = sb("level", P, 2, 4, P)
        s0m = sb("s_mid", P, 4, HD)
        st = sb("wkv_states", P, 5, 4, HD)
        ys, us = sb("y_sol", P, 2, 4, HD), sb("u_sol", P, 2, 4, HD)
        os_ = sb("o_tok", P, HEADS, HD)
        t0, t1 = sb("tmp_a", P, HEADS, HD), sb("tmp_b", P, HEADS, HD)
        small = sb("small", P, 8, HEADS)
        mxt, mzt = sb("mx_tok", P, HEADS, HD), sb("mz_tok", P, HEADS, HD)
        mbt = sb("mb_tok", P, P + 2 * HEADS)
        dab = sb("dA_rows", P, HEADS, P)
        cb = sb("cb_masked", P, 2, P)
        csv = sb("cs_cols", P, 2, HEADS)
        ecs = sb("cs_exp", P, 2, HEADS)
        hdec = sb("h_decay", P, 4)
        seg = sb("segments", P, HEADS, P)
        xdt, xw = sb("xdt", P, HEADS, HD), sb("xw", P, HEADS, HD)
        ht = sb("ssm_states", P, 5, 4, HD)
        ym, t2 = sb("y_mamba", P, HEADS, HD), sb("tmp_c", P, HEADS, HD)
        msmall = sb("msmall", P, 4, HEADS)

        pm_in, xbc_in = sb("pm_in", P, 2, RT, P), sb("xbc_in", P, 2, XT_, P)
        z_in, dt_in = sb("z_in", P, 2, ZT, P), sb("dt_in", 8, 2, 2, P)
        oT = sb("oT", P, DT, P)

        b = Banks(core, mixer_jobs())
        rows_in = [core.sem(f"tile_rows_in{n}") for n in range(2)]
        inner = core.sem("inner_acts")
        sent = core.sem("o_sent")
        par_in = core.sem("mix_params_in")
        zeroed = core.sem("states_zeroed")
        row_switch = core.sem("row_switch")
        tanhs = core.sem("wa_sigmoids")
        cs_half = core.sem("cs_copied")
        states = core.sem("states_ready")
        hats = core.sem("hats")
        mt_rdy = core.sem("mT_ready")
        x_rdy = core.sem("inv_first")
        s0_rdy = core.sem("s_mid_ready")
        exps = core.sem("exps_ready")
        dab_rdy = core.sem("dA_rows_ready")
        seg_exp = core.sem("segments_exp")
        l_rdy = core.sem("weights_ready")
        cse = core.sem("cs_exps")
        xdt_rdy = core.sem("xdt_ready")
        roots_in = core.sem("root_args")
        roots = core.sem("roots_out")
        out_rdy = core.sem("outputs_ready")
        bonus = core.sem("bonus_products")
        dchain, achain, pchain = core.sem("dve_chain2"), core.sem("act_chain2"), core.sem("pool_chain2")
        stored = core.sem("states_stored")
        into = [1, 0, 1, 2, 4]
        frm = [0, 1, 0, 1, 3]

        def tile_over(eng, i):
            b.wait_taken(eng, "or", i)
            b.wait_taken(eng, "s", i)
            eng.wait_ge(states, i + 1)
            eng.wait_ge(out_rdy, 2 * (i + 1))
            eng.wait_ge(bonus, i + 1)

        def fence(eng, i):
            if i:
                tile_over(eng, i - 1)

        with nc.Block() as block:
            @block.sync
            def _(sp):
                for dst, src in ((cst[:, :], a["consts"]), (rows[:, :, :], a["rows"]),
                                 (heads_row[:, :], a["mamba_D"]), (w2[:, :], a["w2"]), (g2[:, :], a["g2"]),
                                 (st[:, 3, :, :], a["wkv_in"]), (ht[:, 3, :, :], a["ssm_in"])):
                    sp.dma_start(dst, src).then_inc(par_in, 16)

                def load(i):
                    tok, T, rc, xc = TILES[i]
                    if i >= 2:
                        tile_over(sp, i - 2)
                    for dst, src in ((pm_in[:, i % 2, :, 0:T], a["pm"][:, :, rc:rc + T]),
                                     (xbc_in[:, i % 2, :, 0:T], a["xbc"][:, :, xc:xc + T]),
                                     (z_in[:, i % 2, :, 0:T], a["z"][:, :, tok:tok + T]),
                                     (dt_in[:, i % 2, :, 0:T], a["dt"][:, :, tok:tok + T])):
                        sp.dma_start(dst, src).then_inc(rows_in[i % 2], 16)

                load(0)
                load(1)
                for i, (tok, T, rc, xc) in enumerate(TILES):
                    b.wait_taken(sp, "or", i)
                    sp.dma_start(a["o"][:, :, tok:tok + T], oT[:, :, 0:T]).then_inc(sent, 16)
                    if i + 2 < NT:
                        load(i + 2)
                tile_over(sp, 3)
                sp.dma_start(a["wkv_out"][:, 0], st[:, 2, :, :]).then_inc(stored, 16)
                sp.dma_start(a["ssm_out"][:, 0], ht[:, 2, :, :]).then_inc(stored, 16)
                tile_over(sp, 4)
                sp.dma_start(a["wkv_out"][:, 1], st[:, 4, :, :]).then_inc(stored, 16)
                sp.dma_start(a["ssm_out"][:, 1], ht[:, 4, :, :]).then_inc(stored, 16)
                sp.wait_ge(stored, 64)
                sp.wait_ge(sent, 16 * NT)

            @block.tensor
            def _(pe):
                pe.wait_ge(par_in, 7 * 16)
                pe.wait_ge(zeroed, 2)
                ident = core.ident
                link = Chain(pe, row_switch)

                def apart(ins, e, T):
                    if T < P and e == 1:
                        link(ins)

                for i, (tok, T, rc, xc) in enumerate(TILES):
                    fence(pe, i)
                    pmi, xbi, zi, dti = (x[:, i % 2] for x in (pm_in, xbc_in, z_in, dt_in))
                    pe.wait_ge(rows_in[i % 2], 64 * (i // 2 + 1))
                    top = LEVELS if T == P else LEVELS - 1

                    def turned(name, srcs, cols=P):
                        o = b.start(pe, name, i)
                        for n, src in enumerate(srcs):
                            ins = pe.transpose(o[0:T, n * P:n * P + src.shape[0]], src, ident[0:src.shape[0], 0:src.shape[0]])
                        b.finish(ins)

                    turned("k", [pmi[:, 4 + n, 0:T] for n in range(4)])
                    turned("r", [pmi[:, n, 0:T] for n in range(4)])
                    turned("v", [pmi[:, 8 + n, 0:T] for n in range(4)])
                    pe.wait_ge(inner, 2 * (i + 1))
                    for name, lhs, rhs in (("w", pmi[0:HD, RT - 2, 0:T], w2[0:HD, :]),
                                           ("a", pmi[HD:P, RT - 2, 0:T], w2[HD:P, :]),
                                           ("g", pmi[:, RT - 1, 0:T], g2[:, :])):
                        o = b.start(pe, name, i)
                        b.finish(pe.matmul(o[0:T, :], lhs, rhs, start=True, stop=True))
                    turned("mx", [xbi[:, n, 0:T] for n in range(4)])
                    o = b.start(pe, "mb", i)
                    pe.transpose(o[0:T, 0:P], xbi[:, 4, 0:T], ident[:, :])
                    pe.transpose(o[0:T, P:P + 8], dti[:, 0, 0:T], ident[0:8, 0:8])
                    b.finish(pe.transpose(o[0:T, P + 8:P + 16], dti[:, 1, 0:T], ident[0:8, 0:8]))
                    turned("mz", [zi[:, n, 0:T] for n in range(4)])
                    pe.wait_ge(tanhs, 2 * (i + 1))
                    for name, m in (("cinc", C_DINC), ("cexc", C_DEXC)):
                        o = b.start(pe, name, i)
                        b.finish(pe.matmul(o[0:T, :], cst[0:T, m:m + T], wa[0:T, 0, :], start=True, stop=True))
                    o = b.start(pe, "dec", i)
                    for n in range(4):
                        ins = pe.matmul(o[:, 2 * n:2 * n + 2], wa[0:T, 0, n * P:(n + 1) * P],
                                        cst[0:T, C_DCOL:C_DCOL + 2], start=True, stop=True)
                    b.finish(ins)
                    b.wait_taken(pe, "mb", i)
                    o = b.start(pe, "cs", i)
                    da = mbt[0:T, P + 8:P + 16]
                    pe.matmul(o[0:T, 0:8], cst[0:T, C_TRI:C_TRI + T], da, start=True, stop=True)
                    pe.matmul(o[0:T, 8:16], cst[0:T, C_REV:C_REV + T], da, start=True, stop=True)
                    b.finish(pe.matmul(o[:, 16:24], core.ones[0:T, :], da, start=True, stop=True))
                    for g in range(2):
                        o = b.start(pe, f"cb{g}", i)
                        gs = slice(g * HD, (g + 1) * HD)
                        b.finish(pe.matmul(o[0:T, 0:T], xbi[gs, 4, 0:T], xbi[gs, 5, 0:T], start=True, stop=True))
                    pe.wait_ge(dab_rdy, i + 1)
                    for g in range(2):
                        o = b.start(pe, f"cst{g}", i)
                        for h in range(4):
                            ins = pe.matmul(o[0:T, h * T:(h + 1) * T], dab[0:T, 4 * g + h, 0:T],
                                            cst[0:T, C_TRI:C_TRI + T], start=True, stop=True)
                        b.finish(ins)
                    for n, (name, src) in enumerate((("bT", bh), ("kT", kh), ("aT", ah), ("rT", rh))):
                        pe.wait_ge(hats, 4 * i + n + 1)
                        o = b.start(pe, name, i)
                        for q in range(4):
                            ins = pe.transpose(o[:, q * T:(q + 1) * T], src[0:T, q * P:(q + 1) * P], ident[0:T, 0:T])
                        b.finish(ins)
                    for name in ("bT", "kT", "aT", "rT"):
                        b.wait_taken(pe, name, i)
                    for e in range(2):
                        es = slice(e * HD, (e + 1) * HD)
                        for name, lhs, rhs in ((f"ab{e}", bT, aT), (f"m{e}", aT, bT), (f"ak{e}", kT, aT),
                                               (f"rb{e}", bT, rT), (f"rk{e}", kT, rT)):
                            o = b.start(pe, name, i)
                            for q in range(4):
                                ins = pe.matmul(o[0:T, q * T:(q + 1) * T], lhs[es, q, 0:T], rhs[es, q, 0:T],
                                                start=True, stop=True)
                            b.finish(ins)
                    for n in range(1, top):
                        for e in range(2):
                            if n == 1:
                                pe.wait_ge(x_rdy, 4 * i + 2 * e + 2)
                            else:
                                b.wait_taken(pe, f"x{n - 1}{e}", i)
                                b.wait_taken(pe, f"t{n - 1}{e}", i)
                            o = b.start(pe, f"q{n}{e}", i)
                            for q in range(4):
                                ins = pe.matmul(o[0:T, q * T:(q + 1) * T], mT[0:T, e, q, 0:T], xx[0:T, e, q, 0:T],
                                                start=True, stop=True)
                            b.finish(ins)
                        for e in range(2):
                            b.wait_taken(pe, f"q{n}{e}", i)
                            if n < top - 1:
                                o = b.start(pe, f"x{n}{e}", i)
                                for q in range(4):
                                    ins = pe.matmul(o[0:T, q * T:(q + 1) * T], xt[0:T, e, q, 0:T], pq[0:T, e, q, 0:T],
                                                    start=True, stop=True)
                                b.finish(ins)
                            o = b.start(pe, f"t{n}{e}", i)
                            for q in range(4):
                                ins = pe.matmul(o[0:T, q * T:(q + 1) * T], pq[0:T, e, q, 0:T], xt[0:T, e, q, 0:T],
                                                start=True, stop=True)
                            b.finish(ins)
                        if n == 1:
                            if i not in (0, 4):
                                b.wait_taken(pe, "st", i - 1)
                            for g in range(2):
                                gs = slice(g * HD, (g + 1) * HD)
                                o = b.start(pe, f"yo{g}", i)
                                b.finish(pe.matmul(o[0:T, 0:4 * HD], xbi[gs, 5, 0:T], ht[gs, frm[i], :, :],
                                                   start=True, stop=True))
                        if n == 2:
                            pe.wait_ge(l_rdy, 2 * (i + 1))
                            pe.wait_ge(xdt_rdy, 2 * (i + 1))
                            o = b.start(pe, "yd", i)
                            for h in range(HEADS):
                                ins = pe.matmul(o[0:T, h * HD:(h + 1) * HD], seg[0:T, h, 0:T], xdt[0:T, h, :],
                                                start=True, stop=True)
                            b.finish(ins)
                        if n == 3:
                            o = b.start(pe, "st", i)
                            for g in range(2):
                                gs = slice(g * HD, (g + 1) * HD)
                                ins = pe.matmul(o[gs, 0:4 * HD], mbt[0:T, gs], xw[0:T, 4 * g:4 * g + 4, :],
                                                start=True, stop=True)
                            b.finish(ins)
                    pe.wait_ge(s0_rdy, i + 1)
                    for e in range(2):
                        es = slice(e * HD, (e + 1) * HD)
                        b.wait_taken(pe, f"ak{e}", i)
                        o = b.start(pe, f"y{e}", i)
                        for q in range(4):
                            oo = o[0:T, q * HD:(q + 1) * HD]
                            apart(pe.matmul(oo, aT[es, q, 0:T], s0m[es, q, :], start=True, stop=False), e, T)
                            ins = pe.matmul(oo, ak[0:T, e, q, 0:T], vt[0:T, 2 * q + e, :], start=False, stop=True)
                            if q < 3:
                                apart(ins, e, T)
                        b.finish(ins)
                    for e in range(2):
                        b.wait_taken(pe, f"y{e}", i)
                        b.wait_taken(pe, f"t{top - 1}{e}", i)
                        o = b.start(pe, f"u{e}", i)
                        for q in range(4):
                            ins = pe.matmul(o[0:T, q * HD:(q + 1) * HD], xt[0:T, e, q, 0:T], ys[0:T, e, q, :],
                                            start=True, stop=True)
                        b.finish(ins)
                    for e in range(2):
                        es = slice(e * HD, (e + 1) * HD)
                        b.wait_taken(pe, f"u{e}", i)
                        o = b.start(pe, f"o{e}", i)
                        for q in range(4):
                            oo = o[0:T, q * HD:(q + 1) * HD]
                            apart(pe.matmul(oo, rT[es, q, 0:T], s0m[es, q, :], start=True, stop=False), e, T)
                            pe.matmul(oo, rk[0:T, e, q, 0:T], vt[0:T, 2 * q + e, :], start=False, stop=False)
                            ins = pe.matmul(oo, rb[0:T, e, q, 0:T], us[0:T, e, q, :], start=False, stop=True)
                            if q < 3:
                                apart(ins, e, T)
                        b.finish(ins)
                    o = b.start(pe, "s", i)
                    for h in range(HEADS):
                        q, e = h // 2, h % 2
                        hs = slice(h * HD, (h + 1) * HD)
                        oo = o[e * HD:(e + 1) * HD, q * HD:(q + 1) * HD]
                        pe.matmul(oo, bh[0:T, hs], us[0:T, e, q, :], start=True, stop=False)
                        ins = pe.matmul(oo, kh[0:T, hs], vt[0:T, h, :], start=False, stop=True)
                    b.finish(ins)
                    for n, (name, src) in enumerate((("om", ym), ("or", os_))):
                        pe.wait_ge(out_rdy, 2 * i + n + 1)
                        flat = src[:, :, :].rearrange("p h d -> p (h d)")
                        o = b.start(pe, name, i)
                        for q in range(4):
                            ins = pe.transpose(o[:, q * T:(q + 1) * T], flat[0:T, q * P:(q + 1) * P], ident[0:T, 0:T])
                        b.finish(ins)

            @block.scalar
            def _(act):
                link = Chain(act, achain)
                act.wait_ge(par_in, 7 * 16)
                for i, (tok, T, rc, xc) in enumerate(TILES):
                    fence(act, i)
                    top = LEVELS if T == P else LEVELS - 1

                    def take(name, dst, cols, func=ACT.Copy, **kw):
                        src = b.get(act, name, i)[0:dst.shape[0], 0:cols]
                        if len(dst.shape) == 3:
                            src = src.rearrange("p (h d) -> p h d", d=dst.shape[2])
                        b.took(act.activation(dst, src, func, **kw), name, i)

                    act.wait_ge(rows_in[i % 2], 64 * (i // 2 + 1))
                    wd, gd = pm_in[0:HD, i % 2, RT - 2, 0:T], pm_in[:, i % 2, RT - 1, 0:T]
                    act.activation(wd, wd, ACT.Tanh).then_inc(inner, 1)
                    act.activation(gd, gd, ACT.Sigmoid).then_inc(inner, 1)
                    take("k", kt[0:T], 512)
                    take("r", rt[0:T], 512)
                    take("v", vt[0:T], 512)
                    take("g", gt[0:T], 512)
                    take("mx", mxt[0:T], 512)
                    take("mb", mbt[0:T, :], P + 16)
                    take("mz", mzt[0:T], 512)
                    for n in range(2):
                        b.wait_taken(act, ("w", "a")[n], i)
                        act.activation(wa[0:T, n, :], wa[0:T, n, :], ACT.Sigmoid).then_inc(tanhs, 1)
                    o = b.get(act, "cinc", i)
                    o3 = o[0:T, :].rearrange("p (h d) -> p h d", d=HD)
                    act.activation(eneg[0:T], o3, ACT.Exp, scale=-1.0).then_inc(exps, 1)
                    b.took(act.activation(einc[0:T], o3, ACT.Exp), "cinc", i)
                    take("cexc", eexc[0:T], 512, ACT.Exp)
                    take("dec", dec[:, :, :], 8, ACT.Exp)
                    b.wait_taken(act, "cs", i)
                    act.activation(ecs[0:T], csv[0:T], ACT.Exp).then_inc(cse, 1)
                    act.activation(hdec[0:HD, :], msmall[0:HD, 0, 0:4], ACT.Exp).then_inc(cse, 1)
                    act.activation(hdec[HD:P, :], msmall[HD:P, 0, 4:8], ACT.Exp).then_inc(cse, 1)
                    for g in range(2):
                        b.wait_taken(act, f"cst{g}", i)
                        act.activation(seg[0:T, 4 * g:4 * g + 4, 0:T], seg[0:T, 4 * g:4 * g + 4, 0:T], ACT.Exp).then_inc(seg_exp, 1)
                    act.wait_ge(roots_in, 3 * i + 1)
                    act.activation(small[0:T, 1, :], small[0:T, 0, :], ACT.Sqrt).then_inc(roots, 1)
                    for name, dst in (("bT", bT), ("kT", kT), ("aT", aT), ("rT", rT)):
                        take(name, dst[:, :, 0:T], 4 * T)
                    for n in range(1, top - 1):
                        for e in range(2):
                            take(f"x{n}{e}", xx[0:T, e, :, 0:T], 4 * T)
                    act.wait_ge(roots_in, 3 * i + 2)
                    act.activation(msmall[0:T, 3, 0:2], msmall[0:T, 2, 0:2], ACT.Sqrt).then_inc(roots, 1)
                    for e in range(2):
                        take(f"y{e}", ys[0:T, e], 4 * HD)
                    for e in range(2):
                        take(f"u{e}", us[0:T, e], 4 * HD)
                    for e in range(2):
                        take(f"o{e}", os_[0:T, e::2, :], 4 * HD)
                    act.wait_ge(roots_in, 3 * i + 3)
                    act.activation(small[0:T, 5, :], small[0:T, 4, :], ACT.Sqrt).then_inc(roots, 1)
                    if i:
                        act.wait_ge(sent, 16 * i)
                    take("om", oT[:, 4:8, 0:T], 4 * T)
                    take("or", oT[:, 0:4, 0:T], 4 * T)

            @block.gpsimd
            def _(pool):
                pool.memset(st[:, 0, :, :], 0.0).then_inc(zeroed, 1)
                pool.memset(ht[:, 0, :, :], 0.0).then_inc(zeroed, 1)
                pool.wait_ge(par_in, 7 * 16)
                link = Chain(pool, pchain)
                for i, (tok, T, rc, xc) in enumerate(TILES):
                    fence(pool, i)
                    b.wait_taken(pool, "mb", i)
                    pool.tensor_copy(dab[0:T, :, 0:T], bc(mbt[0:T, P + 8:P + 16], 2, [T, HEADS, T])).then_inc(dab_rdy, 1)
                    pool.wait_ge(hats, 4 * i + 2)
                    b.wait_taken(pool, "r", i)
                    link(pool.tensor_tensor(t1[0:T], rt[0:T], km[0:T], ALU.mult))
                    pool.tensor_tensor(t1[0:T], t1[0:T], rows[0:T, 4, :].rearrange("p (h d) -> p h d", d=HD), ALU.mult).then_inc(bonus, 1)

            @block.vector
            def _(dve):
                link = Chain(dve, dchain)
                dve.wait_ge(par_in, 7 * 16)
                dve.wait_ge(zeroed, 2)
                TT, STT, TS = dve.tensor_tensor, dve.scalar_tensor_tensor, dve.tensor_scalar

                def row(n, T):
                    return rows[0:T, n, :].rearrange("p (h d) -> p h d", d=HD)

                for i, (tok, T, rc, xc) in enumerate(TILES):
                    fence(dve, i)
                    top = LEVELS if T == P else LEVELS - 1

                    def h3(ap):
                        return ap.rearrange("p (h d) -> p h d", d=HD)

                    def per_head(ap):
                        return bc(ap, 2, [T, HEADS, HD])

                    def mask4(c):
                        return bc(cst[0:T, c:c + T], 1, [T, 4, T])

                    for n, name in enumerate(("w", "a")):
                        o = b.get(dve, name, i)[0:T, :]
                        ins = TT(wa[0:T, n, :], o, rows[0:T, n, :], ALU.add)
                        b.took(ins, name, i)
                    b.wait_taken(dve, "k", i)
                    link(TT(kk[0:T], kt[0:T], row(2, T), ALU.mult))
                    link(TT(t0[0:T], kk[0:T], kk[0:T], ALU.mult))
                    dve.tensor_reduce(small[0:T, 0, :], t0[0:T], AX_X, ALU.add).then_inc(roots_in, 1)
                    o = b.get(dve, "cs", i)
                    dve.tensor_copy(csv[0:T], o[0:T, 0:16].rearrange("p (a h) -> p a h", h=HEADS)).then_inc(cs_half, 1)
                    b.took(dve.tensor_copy(msmall[:, 0, :], o[:, 16:24]), "cs", i)
                    b.wait_taken(dve, "cs", i)
                    for g in range(2):
                        o = b.get(dve, f"cb{g}", i)
                        b.took(TT(cb[0:T, g, 0:T], o[0:T, 0:T], cst[0:T, C_TRI:C_TRI + T], ALU.mult), f"cb{g}", i)
                    for g in range(2):
                        o = b.get(dve, f"cst{g}", i)
                        for h in range(4):
                            ins = TS(seg[0:T, 4 * g + h, 0:T], o[0:T, h * T:(h + 1) * T],
                                     csv[0:T, 0, 4 * g + h:4 * g + h + 1], 0.0, ALU.subtract, ALU.min)
                        b.took(ins, f"cst{g}", i)
                    b.wait_taken(dve, "mb", i)
                    TT(xdt[0:T], mxt[0:T], per_head(mbt[0:T, P:P + 8]), ALU.mult).then_inc(xdt_rdy, 1)
                    dve.wait_ge(tanhs, 2 * (i + 1))
                    link(STT(out=t0[0:T], in0=h3(wa[0:T, 1, :]), scalar=1.0, in1=row(3, T), op0=ALU.subtract, op1=ALU.mult))
                    link(STT(out=km[0:T], in0=t0[0:T], scalar=1.0, in1=kt[0:T], op0=ALU.add, op1=ALU.mult))
                    dve.wait_ge(roots, 3 * i + 1)
                    link(TS(small[0:T, 2, :], small[0:T, 1, :], 1e-12, None, ALU.max))
                    link(dve.reciprocal(small[0:T, 3, :], small[0:T, 2, :]))
                    link(TT(kk[0:T], kk[0:T], per_head(small[0:T, 3, :]), ALU.mult))
                    link(TT(t0[0:T], kk[0:T], h3(wa[0:T, 1, :]), ALU.mult))
                    b.wait_taken(dve, "dec", i)
                    TT(h3(bh[0:T, :]), t0[0:T], eneg[0:T], ALU.mult).then_inc(hats, 1)
                    TT(h3(kh[0:T, :]), km[0:T], eneg[0:T], ALU.mult).then_inc(hats, 1)
                    STT(out=h3(ah[0:T, :]), in0=kk[0:T], scalar=-1.0, in1=eexc[0:T], op0=ALU.mult, op1=ALU.mult).then_inc(hats, 1)
                    TT(h3(rh[0:T, :]), rt[0:T], einc[0:T], ALU.mult).then_inc(hats, 1)
                    TT(s0m[:], st[:, frm[i]], bc(dec[:, :, 0], 2, [P, 4, HD]), ALU.mult).then_inc(s0_rdy, 1)
                    for g in range(2):
                        dve.wait_ge(seg_exp, 2 * i + g + 1)
                        sg = seg[0:T, 4 * g:4 * g + 4, 0:T]
                        TT(sg, sg, bc(cb[0:T, g, 0:T], 1, [T, 4, T]), ALU.mult).then_inc(l_rdy, 1)
                    dve.wait_ge(cse, 3 * (i + 1))
                    dve.wait_ge(xdt_rdy, 2 * i + 1)
                    TT(xw[0:T], xdt[0:T], per_head(ecs[0:T, 1, :]), ALU.mult).then_inc(xdt_rdy, 1)
                    for e in range(2):
                        def masked(name, dst, mask):
                            o = b.get(dve, f"{name}{e}", i)[0:T, 0:4 * T].rearrange("p (q t) -> p q t", t=T)
                            b.took(TT(dst, o, mask4(mask), ALU.mult), f"{name}{e}", i)
                        one = bc(core.ident[0:T, 0:T], 1, [T, 4, T])
                        masked("ab", mT[0:T, e, :, 0:T], C_MS)
                        masked("m", xx[0:T, e, :, 0:T], C_LEV)
                        b.wait_taken(dve, f"ab{e}", i)
                        b.wait_taken(dve, f"m{e}", i)
                        link(TT(mT[0:T, e, :, 0:T], mT[0:T, e, :, 0:T], one, ALU.add))
                        TT(xt[0:T, e, :, 0:T], mT[0:T, e, :, 0:T], mask4(C_LT0), ALU.mult).then_inc(x_rdy, 1)
                        TT(xx[0:T, e, :, 0:T], xx[0:T, e, :, 0:T], one, ALU.add).then_inc(x_rdy, 1)
                        masked("ak", ak[0:T, e, :, 0:T], C_MS)
                        masked("rb", rb[0:T, e, :, 0:T], C_TRI)
                        masked("rk", rk[0:T, e, :, 0:T], C_TRI)
                    for n in range(1, top):
                        for e in range(2):
                            o = b.get(dve, f"q{n}{e}", i)[0:T, 0:4 * T].rearrange("p (q t) -> p q t", t=T)
                            b.took(TT(pq[0:T, e, :, 0:T], o, mask4(C_LEV + n * P), ALU.mult), f"q{n}{e}", i)
                        for e in range(2):
                            o = b.get(dve, f"t{n}{e}", i)[0:T, 0:4 * T].rearrange("p (q t) -> p q t", t=T)
                            b.took(dve.tensor_copy(xt[0:T, e, :, 0:T], o), f"t{n}{e}", i)
                        if n == 1:
                            for g in range(2):
                                o = b.get(dve, f"yo{g}", i)[0:T, 0:4 * HD]
                                b.took(TT(ym[0:T, 4 * g:4 * g + 4, :], h3(o), bc(ecs[0:T, 0, 4 * g:4 * g + 4], 2, [T, 4, HD]),
                                          ALU.mult), f"yo{g}", i)
                            link(TT(t2[0:T], mxt[0:T], per_head(heads_row[0:T, :]), ALU.mult))
                        if n == 2:
                            o = b.get(dve, "yd", i)[0:T, :]
                            b.wait_taken(dve, "yo1", i)
                            b.took(TT(ym[0:T], h3(o), ym[0:T], ALU.add), "yd", i)
                            b.wait_taken(dve, "yd", i)
                            link(TT(ym[0:T], ym[0:T], t2[0:T], ALU.add))
                            link(TT(ym[0:T], ym[0:T], mzt[0:T], ALU.mult))
                            link(TT(t2[0:T], ym[0:T], ym[0:T], ALU.mult))
                            link(dve.tensor_reduce(msmall[0:T, 1, 0:2],
                                                   t2[0:T].rearrange("p (g h) d -> p g (h d)", g=2), AX_X, ALU.add))
                            TS(msmall[0:T, 2, 0:2], msmall[0:T, 1, 0:2], 1.0 / 256, NORM_EPS, ALU.mult, ALU.add).then_inc(roots_in, 1)
                        if n == 3:
                            o = b.get(dve, "st", i)[:, 0:4 * HD]
                            hn = ht[:, into[i]]
                            link(TT(t2[:, 0:4, :], ht[:, frm[i]], bc(hdec[:, :], 2, [P, 4, HD]), ALU.mult))
                            b.took(TT(hn, h3(o), t2[:, 0:4, :], ALU.add), "st", i)
                            b.wait_taken(dve, "st", i)
                    dve.wait_ge(roots, 3 * i + 2)
                    link(dve.reciprocal(msmall[0:T, 1, 0:2], msmall[0:T, 3, 0:2]))
                    y2 = ym[0:T].rearrange("p (g h) d -> p g (h d)", g=2)
                    link(TT(y2, y2, bc(msmall[0:T, 1, 0:2], 2, [T, 2, 4 * HD]), ALU.mult))
                    TT(ym[0:T], ym[0:T], row(7, T), ALU.mult).then_inc(out_rdy, 1)
                    dve.wait_ge(bonus, i + 1)
                    link(dve.tensor_reduce(small[0:T, 6, :], t1[0:T], AX_X, ALU.add))
                    b.wait_taken(dve, "o1", i)
                    link(dve.tensor_reduce(small[0:T, 0, :], os_[0:T], AX_X, ALU.add))
                    link(TS(small[0:T, 1, :], small[0:T, 0, :], 1.0 / HD, None, ALU.mult))
                    link(TT(os_[0:T], os_[0:T], per_head(small[0:T, 1, :]), ALU.subtract))
                    link(TT(t0[0:T], os_[0:T], os_[0:T], ALU.mult))
                    link(dve.tensor_reduce(small[0:T, 2, :], t0[0:T], AX_X, ALU.add))
                    TS(small[0:T, 4, :], small[0:T, 2, :], 1.0 / HD, GN_EPS, ALU.mult, ALU.add).then_inc(roots_in, 1)
                    link(TT(t1[0:T], vt[0:T], per_head(small[0:T, 6, :]), ALU.mult))
                    o = b.get(dve, "s", i)[:, 0:4 * HD]
                    b.took(TT(t2[:, 0:4, :], h3(o), s0m[:], ALU.add), "s", i)
                    b.wait_taken(dve, "s", i)
                    TT(st[:, into[i]], t2[:, 0:4, :], bc(dec[:, :, 1], 2, [P, 4, HD]), ALU.mult).then_inc(states, 1)
                    dve.wait_ge(roots, 3 * i + 3)
                    link(dve.reciprocal(small[0:T, 0, :], small[0:T, 5, :]))
                    link(TT(os_[0:T], os_[0:T], per_head(small[0:T, 0, :]), ALU.mult))
                    link(TT(os_[0:T], os_[0:T], row(5, T), ALU.mult))
                    link(TT(os_[0:T], os_[0:T], row(6, T), ALU.add))
                    link(TT(os_[0:T], os_[0:T], t1[0:T], ALU.add))
                    TT(os_[0:T], os_[0:T], gt[0:T], ALU.mult).then_inc(out_rdy, 1)


def project_out(core, acts):
    nc, a = core.nc, core.a
    with ExitStack() as ctx:
        norm = Norm(core, ctx, "n2", acts, 1, True, 4)
        gemm = Gemm(core, ctx, "wout", acts, DT, a["w_out"])
        om = core.sb("mixed_o", [P, DT, TOK], ctx=ctx)
        x_in, o_in = core.sem("res_in"), core.sem("o_in")
        high, low, added = core.sem("o_high"), core.sem("o_low"), core.sem("res_added")

        with nc.Block() as block:
            @block.sync
            def _(sp):
                sp.dma_start(om[:, :, :], a["o"]).then_inc(o_in, 16)
                sp.dma_start(acts.x[:, :, :], a["x"]).then_inc(x_in, 16)
                for c in range(DT):
                    gemm.load(sp, c)

            @block.gpsimd
            def _(pool):
                for c in range(DT):
                    gemm.split_low(pool, c)

            @block.tensor
            def _(pe):
                pe.wait_ge(low, DT)
                for c in range(DT):
                    gemm.multiply(pe, c)
                norm.pe_sums(pe)

            @block.scalar
            def _(act):
                act.wait_ge(o_in, 16)
                for dt in range(DT):
                    act.activation(acts.hi[:, dt, :], om[:, dt, :], ACT.Copy).then_inc(high, 1)
                for c in range(DT):
                    gemm.split_high(act, c)
                norm.act_squares(act, ready=lambda dt: (gemm.taken, dt + 1))
                norm.act_root(act)
                norm.act_high(act)

            @block.vector
            def _(dve):
                for dt in range(DT):
                    dve.wait_ge(high, dt + 1)
                    dve.tensor_tensor(acts.lo[:, dt, :], om[:, dt, :], acts.hi[:, dt, :].bitcast(F32),
                                      ALU.subtract).then_inc(low, 1)
                dve.wait_ge(x_in, 16)
                for c in range(DT):
                    dve.wait_ge(gemm.done, c + 1)
                    for half in range(2):
                        x = acts.x[:, c, half * HALF:(half + 1) * HALF]
                        ins = dve.tensor_tensor(x, gemm.out(c, half), x, ALU.add)
                        ins.then_inc((added, gemm.taken)[half], 1)
                dve.wait_ge(gemm.taken, DT)
                norm.dve(dve)


def route(core, acts, sel):
    nc, a = core.nc, core.a
    with ExitStack() as ctx:
        def sb(name, *shape, dt=F32):
            return core.sb(name, list(shape), dt, ctx)

        NC = 2 * P_HEADS
        gemm = Gemm(core, ctx, "q", acts, NC, a["w_q"])
        keys = sb("sub_keysT", P, 2, N_KEYS)
        ranks = sb("ranks", P, TOPK)
        qT = sb("qT", P, 2, TOK)
        sc = sb("scores", P, 2, NT, N_KEYS)
        left = sb("scores_left", P, NT, N_KEYS)
        val = sb("top_values", P, 2, NT, TOPK)
        idx = sb("top_index", P, 2, NT, TOPK, dt=U32)
        idf = sb("top_index_f", P, 2, NT, TOPK)
        cand = sb("candidates", P, NT, TOPK * TOPK)
        cleft = sb("candidates_left", P, NT, TOPK * TOPK)
        tv = sb("pick_values", P, NT, TOPK)
        tp = sb("pick_pos", P, NT, TOPK, dt=U32)
        rk = sb("pick_rank", P, 2, NT, TOPK, dt=U32)
        rkf = sb("pick_rank_f", P, 2, NT, TOPK)
        gsum = sb("gate_sum", P, NT, 2)
        picks = sb("picks", P, NT, 3, SEL)
        par_in = core.sem("route_in")
        s_done, s_taken, s_half = core.sem("scores_done"), core.sem("scores_taken"), core.sem("scores_copied")
        ranked, zeroed = core.sem("ranked"), core.sem("scores_zeroed")
        e_in, e_out = core.sem("gate_args"), core.sem("gate_exps")
        picked, turned, sel_out = core.sem("picked"), core.sem("picks_turned"), core.sem("picks_out")
        q_half = core.sem("q_copied")
        dchain = core.sem("dve_chain4")

        with nc.Block() as block:
            @block.sync
            def _(sp):
                sp.dma_start(keys[:, :, :], a["keysT"]).then_inc(par_in, 16)
                sp.dma_start(ranks[:, :], a["ranks"][:, 0:TOPK]).then_inc(par_in, 16)
                for c in range(NC):
                    gemm.load(sp, c)

            @block.gpsimd
            def _(pool):
                pool.memset(sc[:, :, NT - 1, :], 0.0).then_inc(zeroed, 1)
                for c in range(NC):
                    gemm.split_low(pool, c)

            @block.tensor
            def _(pe):
                def scores(c):
                    pe.wait_ge(gemm.taken, c + 1)
                    if c >= 2:
                        pe.wait_ge(s_taken, c - 1)
                    for n, (tok, T, _, _) in enumerate(TILES):
                        bank = core.bank(4 + 2 * (c % 2) + n // 4)
                        ins = pe.matmul(bank[0:T, (n % 4) * P:(n % 4 + 1) * P], qT[:, c % 2, tok:tok + T],
                                        keys[:, c % 2, :], start=True, stop=True)
                    ins.then_inc(s_done, 1)

                pe.wait_ge(par_in, 32)
                for c in range(NC):
                    gemm.multiply(pe, c)
                    if c:
                        scores(c - 1)
                scores(NC - 1)
                for n, (tok, T, _, _) in enumerate(TILES):
                    pe.wait_ge(picked, 3 * P_HEADS)
                    if n >= 2:
                        pe.wait_ge(sel_out, n - 1)
                    for k in range(3):
                        ins = pe.transpose(core.psum[:, n % 2, k * P:k * P + T], picks[0:T, n, k, :],
                                           core.ident[0:T, 0:T])
                    ins.then_inc(turned, 1)

            @block.scalar
            def _(act):
                def take_scores(c):
                    act.wait_ge(s_done, c + 1)
                    act.wait_ge(zeroed, 1)
                    if c >= 2:
                        act.wait_ge(ranked, c - 1)
                    bank = core.bank(4 + 2 * (c % 2))
                    act.activation(sc[:, c % 2, 0:4, :], bank.rearrange("p (n k) -> p n k", n=4), ACT.Copy).then_inc(s_half, 1)
                    bank = core.bank(5 + 2 * (c % 2))
                    act.activation(sc[0:DEC_SEQ, c % 2, 4, :], bank[0:DEC_SEQ, 0:P], ACT.Copy).then_inc(s_taken, 1)

                def gate_exp(h):
                    act.wait_ge(e_in, h + 1)
                    act.activation(tv[:, :, :], tv[:, :, :], ACT.Exp).then_inc(e_out, 1)

                gemm.split_high(act, 0)
                for c in range(NC):
                    if c + 1 < NC:
                        gemm.split_high(act, c + 1)
                    act.wait_ge(gemm.done, c + 1)
                    if c >= 2:
                        act.wait_ge(s_done, c - 1)
                    act.activation(qT[:, c % 2, 0:HALF], gemm.out(c, 0), ACT.Copy).then_inc(q_half, 1)
                    act.activation(qT[:, c % 2, HALF:], gemm.out(c, 1), ACT.Copy).then_inc(gemm.taken, 1)
                    if c:
                        take_scores(c - 1)
                    if c >= 4 and c % 2 == 0:
                        gate_exp(c // 2 - 2)
                take_scores(NC - 1)
                gate_exp(P_HEADS - 2)
                gate_exp(P_HEADS - 1)
                for n, (tok, T, _, _) in enumerate(TILES):
                    act.wait_ge(turned, n + 1)
                    act.activation(sel[:, :, tok:tok + T],
                                   core.psum[:, n % 2, 0:3 * P].rearrange("p (k t) -> p k t", k=3)[:, :, 0:T],
                                   ACT.Copy).then_inc(sel_out, 1)

            @block.vector
            def _(dve):
                link = Chain(dve, dchain)

                def top16(values, index, source, rest, read=None):
                    for n in range(NT):
                        ins = dve.max(values[:, n, 0:8], source[:, n, :])
                    link(ins)
                    for n in range(NT):
                        dve.match_replace(rest[:, n, :], values[:, n, 0:8], source[:, n, :], LOWEST)
                        ins = dve.max_index(index[:, n, 0:8], values[:, n, 0:8], source[:, n, :])
                    if read is None:
                        link(ins)
                    else:
                        ins.then_inc(read[0], 1)
                        dve.wait_ge(*read)
                    for n in range(NT):
                        ins = dve.max(values[:, n, 8:16], rest[:, n, :])
                    link(ins)
                    for n in range(NT):
                        ins = dve.max_index(index[:, n, 8:16], values[:, n, 8:16], rest[:, n, :])
                    link(ins)

                dve.wait_ge(par_in, 32)
                for h in range(P_HEADS):
                    for side in range(2):
                        c = 2 * h + side
                        dve.wait_ge(s_taken, c + 1)
                        top16(val[:, side], idx[:, side], sc[:, side], left, read=(ranked, c + 1))
                    link(dve.tensor_copy(idf[:, :, :, :], idx[:, :, :, :]))
                    c4 = cand[:, :, :].rearrange("p n (a b) -> p n a b", a=TOPK)
                    grid = [P, NT, TOPK, TOPK]
                    link(dve.tensor_tensor(c4, bc(val[:, 0], 3, grid), bc(val[:, 1], 2, grid), ALU.add))
                    top16(tv, tp, cand, cleft)
                    link(dve.tensor_copy(gsum[:, :, 1:2], tv[:, :, 0:1]))
                    dve.tensor_tensor(tv[:, :, :], tv[:, :, :], gsum[:, :, 1:2].broadcast_to([P, NT, TOPK]),
                                      ALU.subtract).then_inc(e_in, 1)
                    link(dve.tensor_scalar(rk[:, 0], tp[:, :, :], 4, None, ALU.logical_shift_right))
                    link(dve.tensor_scalar(rk[:, 1], tp[:, :, :], TOPK - 1, None, ALU.bitwise_and))
                    link(dve.tensor_copy(rkf[:, :, :, :], rk[:, :, :, :]))
                    hs = slice(h * TOPK, (h + 1) * TOPK)
                    e4 = cleft[:, :, :].rearrange("p n (a b) -> p n a b", a=TOPK)
                    rr = ranks[:, :].unsqueeze(1).unsqueeze(1).broadcast_to(grid)
                    for side in range(2):
                        link(dve.tensor_tensor(e4, bc(rkf[:, side], 3, grid), rr, ALU.is_equal))
                        link(dve.tensor_tensor(e4, e4, bc(idf[:, side], 2, grid), ALU.mult))
                        dve.tensor_reduce(picks[:, :, side, hs], e4, AX_X, ALU.add).then_inc(picked, 1)
                        dve.wait_ge(picked, 3 * h + side + 1)
                    dve.wait_ge(e_out, h + 1)
                    link(dve.tensor_reduce(gsum[:, :, 0], tv[:, :, :], AX_X, ALU.add))
                    link(dve.reciprocal(gsum[:, :, 1], gsum[:, :, 0]))
                    dve.tensor_tensor(picks[:, :, 2, hs], tv[:, :, :], gsum[:, :, 1:2].broadcast_to([P, NT, TOPK]),
                                      ALU.mult).then_inc(picked, 1)
                    dve.wait_ge(picked, 3 * h + 3)


def spread_gates(core, sel):
    nc, a = core.nc, core.a
    with ExitStack() as ctx:
        FOUR, SLOTS, PER = 4, 4, 2 * TB // 4
        iota = core.sb("iota", [P, N_KEYS], ctx=ctx)
        cur = core.sb("cur_picks", [P, 3, 2 * TB], ctx=ctx)
        onea = core.sb("onehot_first", [P, SLOTS * FOUR, N_KEYS], ctx=ctx)
        oneb = core.sb("gated_second", [P, SLOTS * FOUR, N_KEYS], ctx=ctx)
        stage = core.sb("gate_stage", [P, 2, NG, TB, JJ], ctx=ctx)
        iota_in = core.sem("iota_in")
        onehots = core.sem("onehots_ready")
        bank_done = core.sem("gates_done")
        staged = core.sem("gates_staged")
        sent = [core.sem(f"gates_sent{n}") for n in range(2)]
        copied = core.sem("picks_copied")
        steps = TOK // (2 * TB)

        with nc.Block() as block:
            @block.sync
            def _(sp):
                sp.dma_start(iota[:, :], a["ranks"]).then_inc(iota_in, 16)
                with sp.Fori(0, steps) as it:
                    for b in range(2):
                        sp.wait_ge(staged, it * PER + 8 * (b + 1) + 8)
                        dst = a["gates"][:, :, bass.ds(it * (2 * TB) + b * TB, TB), :].rearrange("g p t j -> p g (t j)")
                        sp.dma_start(dst, stage[:, b].rearrange("p g t j -> p g (t j)")).then_inc(sent[b], 16)
                for b in range(2):
                    sp.wait_ge(sent[b], 16 * (steps + 1))

            @block.tensor
            def _(pe):
                with pe.Fori(0, steps) as it:
                    for g in range(PER):
                        pe.wait_ge(onehots, it * PER + g + 2)
                        pe.wait_ge(staged, it * PER + g + 1)
                        for t in range(FOUR):
                            s = (g % SLOTS) * FOUR + t
                            ins = pe.matmul(core.psum[:, g % 8, t * P:(t + 1) * P], onea[:, s, :], oneb[:, s, :],
                                            start=True, stop=True)
                        ins.then_inc(bank_done, 1)

            @block.scalar
            def _(act):
                act.sem_inc(staged, 8)
                act.sem_inc(sent[0], 16)
                act.sem_inc(sent[1], 16)
                with act.Fori(0, steps) as it:
                    for g in range(PER):
                        b, r = g // 8, g % 8
                        if r == 0:
                            act.wait_ge(sent[b], 16 * it + 16)
                        act.wait_ge(bank_done, it * PER + g + 1 + SLOTS)
                        src = core.psum[:, g % 8, :].rearrange("p (t g j) -> p g t j", t=FOUR, j=JJ)
                        act.activation(stage[:, b, :, r * FOUR:(r + 1) * FOUR, :], src, ACT.Copy).then_inc(staged, 1)

            @block.vector
            def _(dve):
                dve.wait_ge(iota_in, 16)
                dve.sem_inc(onehots, 1)
                dve.sem_inc(bank_done, SLOTS)
                with dve.Fori(0, steps) as it:
                    dve.wait_ge(onehots, it * PER + 1)
                    dve.tensor_copy(cur[:, :, :], sel[:, :, bass.ds(it * (2 * TB), 2 * TB)]).then_inc(copied, 1)
                    dve.wait_ge(copied, it + 1)
                    for g in range(PER):
                        dve.wait_ge(bank_done, it * PER + g + 1)
                        for t in range(FOUR):
                            s, k = (g % SLOTS) * FOUR + t, g * FOUR + t
                            dve.tensor_scalar(onea[:, s, :], iota[:, :], cur[:, 0, k:k + 1], None, ALU.is_equal)
                            ins = dve.tensor_scalar(oneb[:, s, :], iota[:, :], cur[:, 1, k:k + 1], cur[:, 2, k:k + 1],
                                                    ALU.is_equal, ALU.mult)
                        ins.then_inc(onehots, 1)


def experts(core, acts):
    nc, a = core.nc, core.a
    with ExitStack() as ctx:
        def sb(name, *shape, dt=F32):
            return core.sb(name, list(shape), dt, ctx)

        OUTS = 2 * DT
        u_raw = sb("u_raw", P, 2, 2, DT * P)
        v_raw = sb("v_raw", P, JJ, D_MODEL)
        gates = sb("gates_in", P, 2, TOK, JJ)
        uh, ul = sb("u_high", P, 2, DT * P, dt=F32R), sb("u_low", P, 2, DT * P, dt=F32R)
        vh, vl = sb("v_high", P, JJ, D_MODEL, dt=F32R), sb("v_low", P, JJ, D_MODEL, dt=F32R)
        act_out = sb("gelu_out", P, 2, TOK)
        prod = sb("gated", P, 2, TOK)
        wh, wl = sb("w_high", P, 2, JJ, TOK, dt=F32R), sb("w_low", P, 2, JJ, TOK, dt=F32R)
        u_in = [core.sem(f"u_in{n}") for n in range(2)]
        g_in = [core.sem(f"gates_in{n}") for n in range(2)]
        v_in = core.sem("v_in")
        u_high, u_low = core.sem("u_high_done"), core.sem("u_low_done")
        v_high, v_low = core.sem("v_high_done"), core.sem("v_low_done")
        hid_done = core.sem("hidden_done")
        gelu_half = core.sem("gelu_half")
        gelu_done = core.sem("gelu_done")
        prod_done = core.sem("gated_done")
        w_high = core.sem("w_high_done")
        w_low = core.sem("w_low_done")
        out_done = core.sem("out_done")
        out_added = core.sem("out_added")
        O2 = 2 * OUTS

        def step(f, before=None, after=None):
            def run(eng):
                if before:
                    before(eng)
                f(eng, 0, 0, first=True, last=False)
                with eng.Fori(0, NG // 2 - 1) as it:
                    f(eng, it * 2 + 1, 1, first=False, last=False)
                    f(eng, it * 2 + 2, 0, first=False, last=False)
                f(eng, NG - 1, 1, first=False, last=True)
                if after:
                    after(eng)
            return run

        def load_v(sp, g):
            sp.dma_start(v_raw[:, :, :], a["v"][bass.ds(g, 1)].rearrange("o p j d -> p (o j) d")).then_inc(v_in, 16)

        def sp_run(sp):
            for s in range(2):
                sp.dma_start(u_raw[:, s], a["u"][0, :, 2 * s:2 * s + 2]).then_inc(u_in[s], 16)
            sp.dma_start(gates[:, 0], a["gates"][0]).then_inc(g_in[0], 16)
            for s in range(2):
                sp.wait_ge(u_low, 2 * s + 2)
                sp.dma_start(u_raw[:, s], a["u"][1, :, 2 * s:2 * s + 2]).then_inc(u_in[s], 16)
            sp.dma_start(gates[:, 1], a["gates"][1]).then_inc(g_in[1], 16)
            load_v(sp, 0)
            with sp.Fori(0, NG // 2 - 1) as it:
                for n in range(2):
                    g = it * 2 + 2 + n
                    for s in range(2):
                        sp.wait_ge(u_low, g * JJ + 2 * s - 2)
                        sp.dma_start(u_raw[:, s], a["u"][bass.ds(g, 1), :, 2 * s:2 * s + 2].rearrange(
                            "o p j n -> p (o j) n")).then_inc(u_in[s], 16)
                    sp.wait_ge(prod_done, g * JJ - 2)
                    sp.dma_start(gates[:, n], a["gates"][bass.ds(g, 1)].rearrange(
                        "o p t j -> p (o t) j")).then_inc(g_in[n], 16)
                    sp.wait_ge(v_low, g * JJ - JJ)
                    load_v(sp, g - 1)
            sp.wait_ge(v_low, (NG - 1) * JJ)
            load_v(sp, NG - 1)

        def split_u_high(act, n, g, jj):
            act.wait_ge(u_in[jj // 2], g * 16 + 16)
            act.activation(uh[:, jj % 2], u_raw[:, jj // 2, jj % 2], ACT.Copy).then_inc(u_high, 1)

        def split_v_high(act, g, jj):
            if jj == 0:
                act.wait_ge(v_in, g * 16 + 16)
                act.wait_ge(out_done, g * OUTS + O2)
            act.activation(vh[:, jj], v_raw[:, jj], ACT.Copy).then_inc(v_high, 1)

        def split_v_low(dve, g, jj):
            dve.wait_ge(v_high, g * JJ + jj + 1)
            dve.tensor_tensor(vl[:, jj], v_raw[:, jj], vh[:, jj].bitcast(F32), ALU.subtract).then_inc(v_low, 1)

        def hidden(pe, g):
            for jj in range(JJ):
                n = g * JJ + jj
                pe.wait_ge(u_low, n + 1)
                pe.wait_ge(gelu_done, n + 1)
                for half in range(2):
                    o = core.psum[:, 2 * (jj % 2) + half, 0:HALF]
                    cols = slice(half * HALF, (half + 1) * HALF)
                    for dt in range(DT):
                        w = slice(dt * P, (dt + 1) * P)
                        ins = three_products(pe, o, uh[:, jj % 2, w], ul[:, jj % 2, w],
                                             acts.hi[:, dt, cols], acts.lo[:, dt, cols], dt == 0, dt == DT - 1)
                ins.then_inc(hid_done, 1)

        def out(pe, g, par):
            pe.wait_ge(v_low, g * JJ + JJ)
            pe.wait_ge(w_low, g * JJ + JJ + 2)
            for k in range(OUTS):
                dt, half = k // 2, k % 2
                pe.wait_ge(out_added, g * OUTS + k + 1)
                o = core.psum[:, 4 + k % 4, 0:HALF]
                w, cols = slice(dt * P, (dt + 1) * P), slice(half * HALF, (half + 1) * HALF)
                for jj in range(JJ):
                    ins = three_products(pe, o, vh[:, jj, w], vl[:, jj, w], wh[:, par, jj, cols],
                                         wl[:, par, jj, cols], jj == 0, jj == JJ - 1)
                ins.then_inc(out_done, 1)

        def pe_group(pe, g, par, first, last):
            hidden(pe, g)
            if not first:
                out(pe, g - 1, 1 - par)

        def act_group(act, g, par, first, last):
            for jj in range(JJ):
                n = g * JJ + jj
                act.wait_ge(hid_done, n + 1)
                act.wait_ge(prod_done, n + 1)
                for half in range(2):
                    ins = act.activation(act_out[:, jj % 2, half * HALF:(half + 1) * HALF],
                                         core.psum[:, 2 * (jj % 2) + half, 0:HALF], ACT.Gelu)
                    ins.then_inc((gelu_half, gelu_done)[half], 1)
                if not (last and jj >= 2):
                    split_u_high(act, n + 2, g + (jj + 2) // JJ, (jj + 2) % JJ)
                if not first:
                    split_v_high(act, g - 1, jj)
                act.wait_ge(prod_done, n + 3)
                if jj == 0:
                    act.wait_ge(out_done, g * OUTS)
                act.activation(wh[:, par, jj, :], prod[:, jj % 2, :], ACT.Copy).then_inc(w_high, 1)

        def dve_group(dve, g, par, first, last):
            for jj in range(JJ):
                n = g * JJ + jj
                dve.wait_ge(gelu_done, n + 3)
                if jj == 0:
                    dve.wait_ge(g_in[par], 8 * (g - par) + 16)
                dve.wait_ge(w_low, n + 1)
                dve.tensor_tensor(prod[:, jj % 2, :], act_out[:, jj % 2, :], gates[:, par, :, jj],
                                  ALU.mult).then_inc(prod_done, 1)
                if not first:
                    split_v_low(dve, g - 1, jj)
                dve.wait_ge(w_high, n + 1)
                dve.tensor_tensor(wl[:, par, jj, :], prod[:, jj % 2, :], wh[:, par, jj, :].bitcast(F32),
                                  ALU.subtract).then_inc(w_low, 1)
            if not first:
                add_out(dve, g - 1)

        def add_out(dve, g):
            for k in range(OUTS):
                x = acts.x[:, k // 2, (k % 2) * HALF:(k % 2 + 1) * HALF]
                dve.wait_ge(out_done, g * OUTS + k + 1 + O2)
                dve.tensor_tensor(x, core.psum[:, 4 + k % 4, 0:HALF], x, ALU.add).then_inc(out_added, 1)

        def act_before(act):
            act.sem_inc(gelu_done, 2)
            split_u_high(act, 0, 0, 0)
            split_u_high(act, 1, 0, 1)

        def act_after(act):
            for jj in range(JJ):
                split_v_high(act, NG - 1, jj)

        def dve_before(dve):
            dve.sem_inc(prod_done, 2)
            dve.sem_inc(w_low, 2)
            dve.sem_inc(out_added, 4)

        def dve_after(dve):
            for jj in range(JJ):
                split_v_low(dve, NG - 1, jj)
            add_out(dve, NG - 1)

        with nc.Block() as block:
            @block.sync
            def _(sp):
                sp_run(sp)

            @block.gpsimd
            def _(pool):
                with pool.Fori(0, NG) as g:
                    for jj in range(JJ):
                        pool.wait_ge(u_high, g * JJ + jj + 1)
                        pool.tensor_tensor(ul[:, jj % 2], u_raw[:, jj // 2, jj % 2], uh[:, jj % 2].bitcast(F32),
                                           ALU.subtract).then_inc(u_low, 1)

            @block.tensor
            def _(pe):
                pe.sem_inc(out_done, O2)
                step(pe_group)(pe)
                out(pe, NG - 1, 1)

            @block.scalar
            def _(act):
                step(act_group, act_before, act_after)(act)

            @block.vector
            def _(dve):
                step(dve_group, dve_before, dve_after)(dve)


def finish(core, acts):
    nc, a = core.nc, core.a
    with ExitStack() as ctx:
        norm = Norm(core, ctx, "n3", acts, 2, False, 0)
        stored = core.sem("y_stored")
        with nc.Block() as block:
            @block.sync
            def _(sp):
                for dt in range(DT):
                    sp.wait_ge(norm.scaled, dt + 2)
                    sp.dma_start(a["y"][:, dt, :], norm.y[:, dt, :]).then_inc(stored, 16)
                sp.wait_ge(stored, 16 * DT)

            @block.tensor
            def _(pe):
                norm.pe_sums(pe)

            @block.scalar
            def _(act):
                norm.act_squares(act)
                norm.act_root(act)

            @block.vector
            def _(dve):
                norm.dve(dve)


def build(nc, a):
    with ExitStack() as ctx:
        core = Core(nc, ctx, a)
        project_in(core)
        mix(core)
        acts = Acts(core, ctx, "res")
        with ExitStack() as inner:
            sel = core.sb("picks_by_token", [P, 3, TOK], ctx=inner)
            project_out(core, acts)
            route(core, acts, sel)
            spread_gates(core, sel)
        experts(core, acts)
        finish(core, acts)



_OUT = {
    "y": (P, DT, TOK), "shift_out": (P, RT, 2), "conv_out": (P, XT_, 2, CONV_W - 1),
    "wkv_out": (P, 2, 4, HD), "ssm_out": (P, 2, 4, HD),
}
_SCRATCH = {
    "pm": (P, RT, RWIN), "xbc": (P, XT_, XWIN), "z": (P, ZT, TOK), "dt": (8, 2, TOK), "o": (P, DT, TOK),
    "gates": (NG, P, TOK, JJ),
}


def lay_out(inp):
    f = {k: np.asarray(v) for k, v in inp.items()}

    def chan(x):
        x = np.asarray(x)
        x = x.reshape(x.shape[:-1] + (x.shape[-1] // P, P))
        return np.ascontiguousarray(np.moveaxis(np.moveaxis(x, -1, 0), -1, 1))

    def weight_tiles(w):
        r, c = w.shape
        return np.ascontiguousarray(w.reshape(r // P, P, c // P, P).transpose(2, 1, 0, 3).reshape(c // P, P, r))

    def rows(x):
        return np.broadcast_to(np.asarray(x).reshape(-1), (P, np.asarray(x).size))

    x = np.concatenate([f["x_prompt"][0], f["x_sample"][0]], 0)
    w_in = f["w_in"][0]
    z0, x0, d0 = R_PROJ, R_PROJ + M_WIDTH, R_PROJ + M_WIDTH + CONV_DIM
    pad = np.zeros((D_MODEL, P - HEADS), w_in.dtype)
    w_in = np.concatenate([w_in[:, :R_PROJ], w_in[:, x0:d0], w_in[:, z0:x0], w_in[:, d0:], pad], 1)
    shift = f["state_rwkv_shift"][0, 0]
    par1 = np.concatenate([
        chan(f["rwkv_mu"][0]), chan(shift), np.zeros((P, RT), np.float32),
        chan(f["mamba_conv_w"][0]).reshape(P, -1), chan(f["mamba_conv_b"][0]),
        chan(f["state_mamba_conv"][0, 0]).reshape(P, -1)], 1)

    def pair_states(s):
        return np.ascontiguousarray(s.reshape(4, 2, HD, HD).transpose(1, 3, 0, 2).reshape(P, 4, HD))

    def group_states(s):
        return np.ascontiguousarray(s.reshape(2, 4, HD, HD).transpose(0, 3, 1, 2).reshape(P, 4, HD))

    u = f["peer_u"][0].reshape(N_KEYS, NG, JJ, DT, P).transpose(1, 4, 2, 3, 0).reshape(NG, P, JJ, DT * P)
    v = f["peer_v"][0].reshape(N_KEYS, NG, JJ, D_MODEL).transpose(1, 0, 2, 3)
    return {
        "x": chan(x), "w_in": weight_tiles(w_in), "w_out": weight_tiles(f["w_out"][0]),
        "w_q": weight_tiles(f["peer_w_q"][0]), "consts": shape_constants(),
        "ranks": np.broadcast_to(np.arange(P, dtype=np.float32), (P, P)),
        "norms": np.stack([chan(f["norm1_w"][0]), chan(f["norm2_w"][0]), chan(f["final_norm_w"])], 1),
        "par1": par1, "dtp": np.stack([f["mamba_dt_bias"][0], f["mamba_A_log"][0]], 1),
        "rows": np.stack([rows(f[k]) for k in ("rwkv_w0", "rwkv_a0", "rwkv_k_k", "rwkv_k_a", "rwkv_r_k",
                                               "rwkv_ln_w", "rwkv_ln_b", "mamba_norm_w")], 1),
        "mamba_D": rows(f["mamba_D"]), "w2": np.concatenate([f["rwkv_w2"][0], f["rwkv_a2"][0]], 0),
        "g2": f["rwkv_g2"][0], "wkv_in": pair_states(f["state_rwkv_wkv"][0, 0]),
        "ssm_in": group_states(f["state_mamba_ssm"][0, 0]),
        "keysT": np.ascontiguousarray(f["peer_sub_keys"][0].transpose(2, 0, 1)),
        "u": u, "v": v,
    }


def kernel(**inputs):
    import concourse.bacc as bacc
    from concourse.bass_utils import run_bass_kernel_spmd

    nc = bacc.Bacc("TRN2", target_bir_lowering=False, num_devices=1)
    arrays = {"arg_" + k: np.ascontiguousarray(v) for k, v in lay_out(inputs).items()}
    a = {k[4:]: nc.dram_tensor(k, v.shape, F32, kind="ExternalInput").ap() for k, v in arrays.items()}
    a.update({k: nc.dram_tensor("out_" + k, s, F32, kind="ExternalOutput").ap() for k, s in _OUT.items()})
    a.update({k: nc.dram_tensor("scratch_" + k, s, F32, kind="Internal").ap() for k, s in _SCRATCH.items()})
    build(nc, a)
    r = run_bass_kernel_spmd(nc, [arrays], core_ids=[0]).results[0]
    y = np.asarray(r["out_y"]).transpose(2, 1, 0).reshape(TOK, D_MODEL)
    shift = np.asarray(r["out_shift_out"]).transpose(2, 1, 0).reshape(2, R_PROJ)
    conv = np.asarray(r["out_conv_out"]).transpose(2, 3, 1, 0).reshape(2, CONV_W - 1, CONV_DIM)
    wkv = np.asarray(r["out_wkv_out"]).reshape(2, HD, 2, 4, HD).transpose(2, 3, 0, 4, 1).reshape(2, HEADS, HD, HD)
    ssm = np.asarray(r["out_ssm_out"]).reshape(2, HD, 2, 4, HD).transpose(2, 0, 3, 4, 1).reshape(2, HEADS, HD, HD)
    outs = [y[None, :SEQ], y[None, SEQ:]]
    for n in range(2):
        outs += [shift[None, n:n + 1], wkv[None, n:n + 1], conv[None, n:n + 1], ssm[None, n:n + 1]]
    return tuple(np.ascontiguousarray(o) for o in outs)
```

```python
from contextlib import ExitStack

import numpy as np

import concourse.bass as bass
from concourse import mybir

F32 = mybir.dt.float32
F32R = mybir.dt.float32r
U32 = mybir.dt.uint32
ALU = mybir.AluOpType
ACT = mybir.ActivationFunctionType
AX_X = mybir.AxisListType.X

P = 128
D_MODEL = 1024
SEQ = 512
DEC_SEQ = 64
TOK = SEQ + DEC_SEQ
HALF = TOK // 2
DT = D_MODEL // P
R_WIDTH = 512
M_WIDTH = 512
HEADS = 8
HD = 64
R_PROJ = 1792
CONV_DIM = 768
CONV_W = 4
RT = R_PROJ // P
XT_ = CONV_DIM // P
ZT = M_WIDTH // P
NCT = RT + XT_ + ZT + 1
N_KEYS = 128
P_HEADS = 8
TOPK = 16
SEL = P_HEADS * TOPK
NORM_EPS = 1e-6
GN_EPS = HD * 1e-5
DECAY_SCALE = -float(np.exp(-0.5))
LOWEST = -3.0e38
RWIN = SEQ + 1 + DEC_SEQ
XWIN = SEQ + CONV_W - 1 + DEC_SEQ
TILES = [(0, P, 0, 0), (P, P, P, P), (2 * P, P, 2 * P, 2 * P), (3 * P, P, 3 * P, 3 * P),
         (SEQ, DEC_SEQ, SEQ + 1, SEQ + CONV_W - 1)]
NT = len(TILES)
LEVELS = 7
JJ = 4
NG = N_KEYS // JJ
TB = 32
G_STEPS = TOK // (2 * TB)
AHEAD5 = 2 * G_STEPS
AHEAD4 = 30
NH = NG - (AHEAD4 + AHEAD5) // JJ
KEY4, KEY5 = NH * JJ, NH * JJ + AHEAD4

C_ID, C_ONE, C_TRI, C_REV, C_DINC, C_DEXC = (P * n for n in range(6))
C_MS, C_LT0, C_LEV = (P * n for n in range(6, 9))
C_DCOL = C_LEV + P * LEVELS
C_N = C_DCOL + 2


def shape_constants():
    c = np.zeros((P, C_N), np.float32)
    s = np.arange(P)[:, None]
    t = np.arange(P)[None, :]
    c[:, C_ID:C_ID + P] = s == t
    c[:, C_ONE:C_ONE + P] = 1
    c[:, C_TRI:C_TRI + P] = s <= t
    c[:, C_REV:C_REV + P] = s > t
    mid = (s <= HD - 1)
    c[:, C_DINC:C_DINC + P] = DECAY_SCALE * ((s <= t).astype(np.float32) - mid)
    c[:, C_DEXC:C_DEXC + P] = DECAY_SCALE * ((s < t).astype(np.float32) - mid)
    c[:, C_MS:C_MS + P] = s < t
    for n in range(LEVELS):
        b = 1 << n
        m = ((s // (2 * b) == t // (2 * b)) & (s // b > t // b)) | (s == t)
        c[:, C_LEV + P * n:C_LEV + P * (n + 1)] = m if n else m & (s != t)
        if n == 0:
            c[:, C_LT0:C_LT0 + P] = m.T
    c[:, C_DCOL] = DECAY_SCALE * mid[:, 0]
    c[:, C_DCOL + 1] = DECAY_SCALE * (~mid[:, 0])
    return c


def bc(ap, axis, shape):
    return ap.unsqueeze(axis).broadcast_to(shape)


def three_products(pe, out, ah, al, bh, bl, first, last):
    pe.matmul(out, ah, bh, start=first, stop=False)
    pe.matmul(out, ah, bl, start=False, stop=False)
    return pe.matmul(out, al, bh, start=False, stop=last)


class Acts:

    def __init__(self, core, ctx, name):
        self.x = core.sb(name + "_x", [P, DT, TOK], ctx=ctx)
        self.hi = core.sb(name + "_hi", [P, DT, TOK], F32R, ctx=ctx)
        self.lo = core.sb(name + "_lo", [P, DT, TOK], F32R, ctx=ctx)


class Core:

    def __init__(self, nc, ctx, a):
        self.nc, self.ctx, self.a = nc, ctx, a
        self.psum = ctx.enter_context(nc.psum_tensor("banks", [P, 8, 512], F32))
        self.ident = self.sb("ident", [P, P])
        self.ones = self.sb("ones", [P, P])
        self.norms = self.sb("norms", [P, 3, DT])
        self.chains = {name: Chain(self.sem(name + "_chain")) for name in ("pe", "act", "pool", "dve")}

    def sb(self, name, shape, dt=F32, ctx=None):
        return (ctx or self.ctx).enter_context(self.nc.sbuf_tensor(name, shape, dt))

    def sem(self, name):
        return self.ctx.enter_context(self.nc.semaphore(name))

    def bank(self, n):
        return self.psum[:, n % 8, :]


class Chain:

    def __init__(self, sem):
        self.sem, self.n = sem, 0

    def on(self, eng):
        self.eng = eng
        return self

    def __call__(self, ins):
        ins.then_inc(self.sem, 1)
        self.n += 1
        self.eng.wait_ge(self.sem, self.n)


class Gemm:

    def __init__(self, core, ctx, name, acts, count, dram, banks=(0, 1, 2, 3)):
        self.acts = acts
        self.core, self.count, self.dram, self.banks = core, count, dram, banks
        self.raw = core.sb(name + "_raw", [P, 3, DT * P], ctx=ctx)
        self.wh = core.sb(name + "_wh", [P, 2, DT * P], F32R, ctx=ctx)
        self.wl = core.sb(name + "_wl", [P, 2, DT * P], F32R, ctx=ctx)
        self.loaded = [core.sem(f"{name}_loaded{n}") for n in range(3)]
        self.high = core.sem(name + "_high")
        self.low = core.sem(name + "_low")
        self.done = core.sem(name + "_done")
        self.taken = core.sem(name + "_taken")

    def load(self, sp, c):
        if c >= 3:
            sp.wait_ge(self.low, c - 2)
        sp.dma_start(self.raw[:, c % 3, :], self.dram[c]).then_inc(self.loaded[c % 3], 16)

    def split_high(self, act, c):
        act.wait_ge(self.loaded[c % 3], 16 * (c // 3 + 1))
        if c >= 2:
            act.wait_ge(self.done, c - 1)
        act.activation(self.wh[:, c % 2, :], self.raw[:, c % 3, :], ACT.Copy).then_inc(self.high, 1)

    def split_low(self, pool, c):
        pool.wait_ge(self.high, c + 1)
        pool.tensor_tensor(self.wl[:, c % 2, :], self.raw[:, c % 3, :],
                           self.wh[:, c % 2, :].bitcast(F32), ALU.subtract).then_inc(self.low, 1)

    def multiply(self, pe, c):
        pe.wait_ge(self.low, c + 1)
        if c >= 2:
            pe.wait_ge(self.taken, c - 1)
        for half in range(2):
            out = self.core.psum[:, self.banks[2 * (c % 2) + half], 0:HALF]
            cols = slice(half * HALF, (half + 1) * HALF)
            for dt in range(DT):
                w = slice(dt * P, (dt + 1) * P)
                ins = three_products(pe, out, self.wh[:, c % 2, w], self.wl[:, c % 2, w],
                                     self.acts.hi[:, dt, cols], self.acts.lo[:, dt, cols],
                                     dt == 0, dt == DT - 1)
        ins.then_inc(self.done, 1)

    def out(self, c, half):
        return self.core.psum[:, self.banks[2 * (c % 2) + half], 0:HALF]


class Norm:

    def __init__(self, core, ctx, name, acts, which, halves, bank):
        self.acts = acts
        self.core, self.which, self.halves, self.b = core, which, halves, bank
        self.sq = core.sb(name + "_sq", [P, 2, TOK], ctx=ctx)
        self.mean = core.sb(name + "_mean", [P, TOK], ctx=ctx)
        self.root = core.sb(name + "_root", [P, TOK], ctx=ctx)
        self.inv = core.sb(name + "_inv", [P, TOK], ctx=ctx)
        self.ny = 2 if halves else DT
        self.y = core.sb(name + "_y", [P, self.ny, TOK], ctx=ctx)
        self.squared = core.sem(name + "_squared")
        self.summed = core.sem(name + "_summed")
        self.meaned = core.sem(name + "_meaned")
        self.rooted = core.sem(name + "_rooted")
        self.scaled = core.sem(name + "_scaled")
        if halves:
            self.high = core.sem(name + "_high")
            self.low = core.sem(name + "_low")

    def act_squares(self, act, ready=None):
        for dt in range(DT):
            if ready is not None:
                act.wait_ge(*ready(dt))
            if dt >= 2:
                act.wait_ge(self.summed, dt - 1)
            act.activation(self.sq[:, dt % 2, :], self.acts.x[:, dt, :], ACT.Square).then_inc(self.squared, 1)

    def pe_sums(self, pe):
        for dt in range(DT):
            pe.wait_ge(self.squared, dt + 1)
            for half in range(2):
                ins = pe.matmul(self.core.psum[:, self.b + half, 0:HALF], self.core.ones[:, :],
                                self.sq[:, dt % 2, half * HALF:(half + 1) * HALF],
                                start=dt == 0, stop=dt == DT - 1)
            ins.then_inc(self.summed, 1)

    def act_root(self, act):
        act.wait_ge(self.meaned, 2)
        act.activation(self.root[:, :], self.mean[:, :], ACT.Sqrt).then_inc(self.rooted, 1)

    def act_high(self, act):
        for dt in range(DT):
            act.wait_ge(self.scaled, dt + 2)
            act.activation(self.acts.hi[:, dt, :], self.y[:, dt % 2, :], ACT.Copy).then_inc(self.high, 1)

    def dve(self, dve):
        dve.wait_ge(self.summed, DT)
        for half in range(2):
            cols = slice(half * HALF, (half + 1) * HALF)
            dve.tensor_scalar(self.mean[:, cols], self.core.psum[:, self.b + half, 0:HALF],
                              1.0 / D_MODEL, NORM_EPS, ALU.mult, ALU.add).then_inc(self.meaned, 1)
        dve.wait_ge(self.rooted, 1)
        dve.reciprocal(self.inv[:, :], self.root[:, :]).then_inc(self.scaled, 1)
        dve.wait_ge(self.scaled, 1)
        for dt in range(DT):
            if dt >= self.ny:
                dve.wait_ge(self.low, dt - 1)
            dve.scalar_tensor_tensor(out=self.y[:, dt % self.ny, :], in0=self.acts.x[:, dt, :],
                                     scalar=self.core.norms[:, self.which, dt:dt + 1],
                                     in1=self.inv[:, :], op0=ALU.mult, op1=ALU.mult).then_inc(self.scaled, 1)
            if self.halves:
                dve.wait_ge(self.high, dt + 1)
                dve.tensor_tensor(self.acts.lo[:, dt, :], self.y[:, dt % 2, :],
                                  self.acts.hi[:, dt, :].bitcast(F32), ALU.subtract).then_inc(self.low, 1)


def project_in(core):
    nc, a = core.nc, core.a
    with ExitStack() as ctx:
        acts = Acts(core, ctx, "in")
        norm = Norm(core, ctx, "n1", acts, 0, True, 4)
        gemm = Gemm(core, ctx, "in", acts, NCT, a["w_in"])
        out = core.sb("row_out", [P, 3, XWIN], ctx=ctx)
        pr = core.sb("pr", [P, 2, RWIN + 1], ctx=ctx)
        px = core.sb("px", [P, 2, XWIN + CONV_W - 1], ctx=ctx)
        tmp = core.sb("tmp1", [P, 2, XWIN], ctx=ctx)
        par = core.sb("par1", [P, 3 * RT + XT_ * (CONV_W + 1 + CONV_W - 1)], ctx=ctx)
        mu, shift_in, = par[:, 0:RT], par[:, RT:2 * RT]
        cw = par[:, 3 * RT:3 * RT + XT_ * CONV_W].rearrange("p (x k) -> p x k", k=CONV_W)
        cb = par[:, 3 * RT + XT_ * CONV_W:3 * RT + XT_ * (CONV_W + 1)]
        cst = par[:, 3 * RT + XT_ * (CONV_W + 1):].rearrange("p (x k) -> p x k", k=CONV_W - 1)
        shift_out = core.sb("shift_out", [P, RT, 2], ctx=ctx)
        conv_out = core.sb("conv_out", [P, XT_, 2, CONV_W - 1], ctx=ctx)
        dtp = core.sb("dtp", [8, 4], ctx=ctx)
        dts = core.sb("dts", [8, 3, TOK], ctx=ctx)
        dto = core.sb("dt_out", [8, 2, TOK], ctx=ctx)
        x_in = core.sem("x_in")
        ones_in = core.sem("ones_in")
        par_in = core.sem("par_in")
        zeroed = core.sem("pads_zeroed")
        mixed = core.sem("row_mixed")
        conved = core.sem("row_conved")
        tails = core.sem("tails_copied")
        silued = core.sem("row_silued")
        dtc = core.sem("dt_act")
        dtv = core.sem("dt_dve")
        stored = core.sem("tails_stored")
        sent = [core.sem(f"row_sent{n}") for n in range(3)]

        with nc.Block() as block:
            @block.sync
            def _(sp):
                sp.dma_start(core.ones[:, :], a["consts"][:, C_ONE:C_ONE + P]).then_inc(ones_in, 16)
                sp.dma_start(acts.x[:, :, :], a["x"]).then_inc(x_in, 16)
                for c in range(3):
                    gemm.load(sp, c)
                sp.dma_start(core.ident[:, :], a["consts"][:, C_ID:C_ID + P]).then_inc(par_in, 16)
                sp.dma_start(core.norms[:, :, :], a["norms"]).then_inc(par_in, 16)
                sp.dma_start(par[:, :], a["par1"]).then_inc(par_in, 16)
                sp.dma_start(dtp[:, 0:2], a["dtp"]).then_inc(par_in, 16)
                for c in range(NCT - 1):
                    if c + 3 < NCT:
                        gemm.load(sp, c + 3)
                    if c < RT:
                        sp.wait_ge(mixed, c + 1)
                        dst = a["pm"][:, c, :]
                    elif c < RT + XT_:
                        sp.wait_ge(silued, c - RT + 1)
                        dst = a["xbc"][:, c - RT, :]
                    else:
                        sp.wait_ge(gemm.taken, c + 1)
                        dst = a["z"][:, c - RT - XT_, :]
                    sp.dma_start(dst, out[:, c % 3, 0:dst.shape[1]]).then_inc(sent[c % 3], 16)
                sp.wait_ge(dtv, 1)
                sp.dma_start(a["dt"], dto[:, :, :]).then_inc(stored, 16)
                sp.wait_ge(tails, RT + XT_)
                sp.wait_ge(mixed, RT + XT_)
                sp.dma_start(a["shift_out"], shift_out[:, :, :]).then_inc(stored, 16)
                sp.dma_start(a["conv_out"], conv_out[:, :, :, :]).then_inc(stored, 16)
                sp.wait_ge(stored, 48)
                for n in range(3):
                    sp.wait_ge(sent[n], 16 * ((NCT - 1) // 3))

            @block.gpsimd
            def _(pool):
                pool.memset(pr[:, :, 0:1], 0.0).then_inc(zeroed, 1)
                pool.memset(px[:, :, 0:CONV_W - 1], 0.0).then_inc(zeroed, 1)
                for c in range(NCT):
                    gemm.split_low(pool, c)

            @block.tensor
            def _(pe):
                pe.wait_ge(ones_in, 16)
                norm.pe_sums(pe)
                pe.wait_ge(norm.low, DT)
                for c in range(NCT):
                    gemm.multiply(pe, c)

            @block.scalar
            def _(act):
                link = core.chains["act"].on(act)
                norm.act_squares(act, ready=lambda dt: (x_in, 16))
                norm.act_root(act)
                gemm.split_high(act, 0)
                gemm.split_high(act, 1)
                norm.act_high(act)
                act.wait_ge(par_in, 64)
                act.wait_ge(zeroed, 2)

                def row_free(c):
                    if c >= 3:
                        act.wait_ge(sent[c % 3], 16 * (c // 3))

                link(act.activation(dtp[:, 2:3], dtp[:, 1:2], ACT.Exp))

                def silu(x):
                    act.wait_ge(conved, x + 1)
                    row_free(RT + x)
                    act.activation(out[:, (RT + x) % 3, :], tmp[:, 1, :], ACT.Silu, bias=cb[:, x:x + 1]).then_inc(silued, 1)

                for c in range(NCT):
                    act.wait_ge(gemm.done, c + 1)
                    a0, a1 = gemm.out(c, 0), gemm.out(c, 1)
                    n1 = SEQ - HALF
                    if c < RT:
                        if c >= 2:
                            act.wait_ge(mixed, c - 1)
                        row = pr[:, c % 2, :]
                        act.activation(row[:, SEQ + 1:SEQ + 2], shift_in[:, c:c + 1], ACT.Copy)
                        act.activation(row[:, 1:1 + HALF], a0, ACT.Copy)
                        act.activation(row[:, 1 + HALF:1 + SEQ], a1[:, 0:n1], ACT.Copy)
                        act.activation(row[:, SEQ + 2:], a1[:, n1:], ACT.Copy).then_inc(gemm.taken, 1)
                    elif c < RT + XT_:
                        x = c - RT
                        if x >= 2:
                            act.wait_ge(mixed, c - 1)
                        row = px[:, x % 2, :]
                        g = CONV_W - 1
                        act.activation(row[:, g + SEQ:g + SEQ + g], cst[:, x, :], ACT.Copy)
                        act.activation(row[:, g:g + HALF], a0, ACT.Copy)
                        act.activation(row[:, g + HALF:g + SEQ], a1[:, 0:n1], ACT.Copy)
                        act.activation(row[:, g + SEQ + g:], a1[:, n1:], ACT.Copy).then_inc(gemm.taken, 1)
                        if x >= 1:
                            silu(x - 1)
                    elif c < RT + XT_ + ZT:
                        if c == RT + XT_:
                            silu(XT_ - 1)
                        row_free(c)
                        act.activation(out[:, c % 3, 0:HALF], a0, ACT.Silu)
                        act.activation(out[:, c % 3, HALF:TOK], a1, ACT.Silu).then_inc(gemm.taken, 1)
                    else:
                        act.activation(dts[:, 0, 0:HALF], a0[0:8, :], ACT.Identity, bias=dtp[:, 0:1]).then_inc(dtc, 1)
                        act.activation(dts[:, 0, HALF:], a1[0:8, :], ACT.Identity, bias=dtp[:, 0:1]).then_inc(gemm.taken, 1)
                        act.wait_ge(gemm.taken, NCT)
                        link(act.activation(dts[:, 1, :], dts[:, 0, :], ACT.Abs))
                        link(act.activation(dts[:, 2, :], dts[:, 1, :], ACT.Exp, scale=-1.0))
                        act.activation(dts[:, 1, :], dts[:, 2, :], ACT.Ln, bias=1.0).then_inc(dtc, 1)
                    if c + 2 < NCT:
                        gemm.split_high(act, c + 2)

            @block.vector
            def _(dve):
                link = core.chains["dve"].on(dve)
                dve.wait_ge(par_in, 64)
                norm.dve(dve)
                dve.wait_ge(zeroed, 2)
                for c in range(RT):
                    dve.wait_ge(gemm.taken, c + 1)
                    row = pr[:, c % 2, :]
                    link(dve.tensor_tensor(tmp[:, 0, 0:RWIN], row[:, 0:RWIN], row[:, 1:], ALU.subtract))
                    dve.tensor_copy(shift_out[:, c, :], row[:, SEQ:SEQ + 2 + DEC_SEQ:DEC_SEQ + 1]).then_inc(tails, 1)
                    if c >= 3:
                        dve.wait_ge(sent[c % 3], 16 * (c // 3))
                    dve.scalar_tensor_tensor(out=out[:, c % 3, 0:RWIN], in0=tmp[:, 0, 0:RWIN], scalar=mu[:, c:c + 1],
                                             in1=row[:, 1:], op0=ALU.mult, op1=ALU.add).then_inc(mixed, 1)
                    dve.wait_ge(mixed, c + 1)
                for x in range(XT_):
                    c = RT + x
                    dve.wait_ge(gemm.taken, c + 1)
                    row = px[:, x % 2, :]
                    dve.tensor_copy(conv_out[:, x, 0, :], row[:, SEQ:SEQ + CONV_W - 1]).then_inc(tails, 1)
                    link(dve.tensor_scalar(tmp[:, 0, :], row[:, 0:XWIN], cw[:, x, 0:1], None, ALU.mult))
                    if x >= 1:
                        dve.wait_ge(silued, x)
                    link(dve.scalar_tensor_tensor(out=tmp[:, 1, :], in0=row[:, 1:1 + XWIN], scalar=cw[:, x, 1:2],
                                                  in1=tmp[:, 0, :], op0=ALU.mult, op1=ALU.add))
                    link(dve.scalar_tensor_tensor(out=tmp[:, 0, :], in0=row[:, 2:2 + XWIN], scalar=cw[:, x, 2:3],
                                                  in1=tmp[:, 1, :], op0=ALU.mult, op1=ALU.add))
                    dve.scalar_tensor_tensor(out=tmp[:, 1, :], in0=row[:, 3:3 + XWIN], scalar=cw[:, x, 3:4],
                                             in1=tmp[:, 0, :], op0=ALU.mult, op1=ALU.add).then_inc(conved, 1)
                    dve.wait_ge(conved, x + 1)
                    dve.tensor_copy(conv_out[:, x, 1, :], row[:, XWIN:XWIN + CONV_W - 1]).then_inc(mixed, 1)
                dve.wait_ge(mixed, RT + XT_)
                dve.wait_ge(dtc, 2)
                link(dve.tensor_scalar(dts[:, 0, :], dts[:, 0, :], 0.0, None, ALU.max))
                link(dve.tensor_tensor(dto[:, 0, :], dts[:, 0, :], dts[:, 1, :], ALU.add))
                dve.tensor_scalar(dto[:, 1, :], dto[:, 0, :], dtp[:, 2:3], -1.0, ALU.mult, ALU.mult).then_inc(dtv, 1)


def tile_parts():
    parts = [(f"A{n}", 0) for n in range(1, 6)]
    between = {1: ("C1", "A1"), 2: ("C2", "A2"), 3: ("C3", "A3"), 4: ("A4", "C4"), 5: ("A5",)}
    for i in range(NT):
        parts.append(("B1", i))
        for n in range(1, last_level(i) + 1):
            parts.append((f"L{n}", i))
            for name in between.get(n, ()):
                j = i + 1 if name[0] == "A" else i - 1
                if 0 <= j < NT:
                    parts.append((name, j))
        parts.append(("B5", i))
    return parts + [(f"C{n}", NT - 1) for n in range(1, 5)]


def last_level(i):
    return LEVELS - 1 if TILES[i][1] == P else LEVELS - 2


def mixer_jobs():
    jobs = []
    for part, i in tile_parts():
        one = {
            "A1": [("k", "act"), ("w", "dve"), ("a", "dve"), ("r", "act"), ("v", "act"), ("g", "act"),
                   ("mb", "act"), ("mx", "act"), ("mz", "act")],
            "A2": [("cinc", "act"), ("cexc", "act"), ("dec", "act"), ("cs", "dve"), ("cb0", "dve"), ("cb1", "dve")],
            "A4": [("cst0", "dve"), ("cst1", "dve")],
            "B1": [("bT", "act"), ("kT", "act"), ("aT", "act"), ("rT", "act")]
                  + [(f"{name}{e}", "dve") for name in ("ab", "m") for e in range(2)]
                  + [(f"{name}{e}", "dve") for e in range(2) for name in ("ak", "rb", "rk")],
            "B5": [("y0", "act"), ("y1", "act"), ("u0", "act"), ("u1", "act"), ("o0", "act"), ("o1", "act"),
                   ("s", "dve"), ("om", "act")],
            "C4": [("or", "act")],
        }.get(part, [])
        if part[0] == "L":
            n = int(part[1])
            one = [(f"q{n}{e}", "dve") for e in range(2)]
            for e in range(2):
                one += [(f"x{n}{e}", "act")] * (n < last_level(i)) + [(f"t{n}{e}", "act")]
            one += {1: [("yo0", "dve"), ("yo1", "dve")], 2: [("yd", "dve")], 3: [("st", "dve")]}.get(n, [])
        jobs += [(name, i, taker) for name, taker in one]
    return jobs


class Banks:

    def __init__(self, core, jobs):
        self.core = core
        self.done = core.sem("banks_done")
        self.taken = {"act": core.sem("banks_taken_act"), "dve": core.sem("banks_taken_dve")}
        self.number, self.order, count = {}, [], {"act": 0, "dve": 0}
        for n, (name, i, taker) in enumerate(jobs):
            count[taker] += 1
            self.number[name, i] = n
            self.order.append((self.taken[taker], count[taker]))

    def start(self, pe, name, i):
        n = self.number[name, i]
        if n >= 8:
            pe.wait_ge(*self.order[n - 8])
        return self.core.bank(n)

    def finish(self, ins):
        ins.then_inc(self.done, 1)

    def get(self, eng, name, i):
        n = self.number[name, i]
        eng.wait_ge(self.done, n + 1)
        return self.core.bank(n)

    def took(self, ins, name, i):
        ins.then_inc(self.order[self.number[name, i]][0], 1)

    def wait_taken(self, eng, name, i):
        eng.wait_ge(*self.order[self.number[name, i]])


def mix(core):
    nc, a = core.nc, core.a
    with ExitStack() as ctx:
        def sb(name, *shape, dt=F32):
            return core.sb(name, list(shape), dt, ctx)

        cst = sb("shape_constants", P, C_N)
        rows = sb("param_rows", P, 8, R_WIDTH)
        heads_row = sb("mamba_D", P, HEADS)
        w2 = sb("w2", P, R_WIDTH)
        g2 = sb("g2", P, R_WIDTH)
        kt, rt = (sb(n, P, HEADS, HD) for n in ("k_tok", "r_tok"))
        vt2, gt3 = sb("v_tok", P, 2, HEADS, HD), sb("g_tok", P, 3, HEADS, HD)
        wa = sb("wa_sigmoid", P, 2, R_WIDTH)
        einc, eneg, eexc = (sb(n, P, HEADS, HD) for n in ("e_inc", "e_neg", "e_exc"))
        dec2 = sb("decay_cols", P, 2, 4, 2)
        kk, km = sb("kk", P, HEADS, HD), sb("k_mod", P, HEADS, HD)
        bh2, kh2 = (sb(n, P, 2, R_WIDTH) for n in ("b_hat", "k_hat"))
        ah, rh = (sb(n, P, R_WIDTH) for n in ("a_hat", "r_hat"))
        bT, kT, aT, rT = (sb(n, P, 4, P) for n in ("b_hatT", "k_hatT", "a_hatT", "r_hatT"))
        mT, ak, rb, rk = (sb(n, P, 2, 4, P) for n in ("mT", "akT", "rbT", "rkT"))
        xx, xt = sb("inv", P, 2, 4, P), sb("invT", P, 2, 4, P)
        pq = sb("level", P, 2, 4, P)
        s0m = sb("s_mid", P, 4, HD)
        st = sb("wkv_states", P, 5, 4, HD)
        ys, us = sb("y_sol", P, 2, 4, HD), sb("u_sol", P, 2, 4, HD)
        os_ = sb("o_tok", P, HEADS, HD)
        t0, t1, t3, t4 = (sb(n, P, HEADS, HD) for n in ("tmp_a", "bonus_prod", "tmp_b", "bonus_v"))
        small, small_b = sb("small", P, 4, HEADS), sb("small_b", P, 8, HEADS)
        bonus2 = sb("bonus", P, 2, HEADS)
        mxt2, mzt2 = sb("mx_tok", P, 2, HEADS, HD), sb("mz_tok", P, 2, HEADS, HD)
        mbt2 = sb("mb_tok", P, 2, P + 2 * HEADS)
        dab = sb("dA_rows", P, HEADS, P)
        cb = sb("cb_masked", P, 2, P)
        csv = sb("cs_cols", P, 2, HEADS)
        ecs2 = sb("cs_exp", P, 2, 2, HEADS)
        hdec2 = sb("h_decay", P, 2, 4)
        seg2 = sb("segments", P, 2, HEADS, P)
        xdt2, xw2 = sb("xdt", P, 2, HEADS, HD), sb("xw", P, 2, HEADS, HD)
        ht = sb("ssm_states", P, 5, 4, HD)
        ym, t2 = sb("y_mamba", P, HEADS, HD), sb("tmp_c", P, HEADS, HD)
        t5 = sb("state_tmp", P, 4, HD)
        msmall = sb("msmall", P, 4, HEADS)

        pm_in, xbc_in = sb("pm_in", P, 2, RT, P), sb("xbc_in", P, 2, XT_, P)
        z_in, dt_in = sb("z_in", P, 2, ZT, P), sb("dt_in", 8, 2, 2, P)
        oT = sb("oT", P, DT, P)

        b = Banks(core, mixer_jobs())
        rows_in = [core.sem(f"tile_rows_in{n}") for n in range(2)]
        inner = core.sem("inner_acts")
        sent = core.sem("o_sent")
        par_in = core.sem("mix_params_in")
        zeroed = core.sem("states_zeroed")
        tanhs = core.sem("wa_sigmoids")
        states = core.sem("states_ready")
        hats = core.sem("hats")
        mt_rdy = core.sem("mT_ready")
        x_rdy = core.sem("inv_first")
        s0_rdy = core.sem("s_mid_ready")
        exps = core.sem("exps_ready")
        dab_rdy = core.sem("dA_rows_ready")
        seg_exp = core.sem("segments_exp")
        l_rdy = core.sem("weights_ready")
        cse = core.sem("cs_exps")
        xdt_rdy = core.sem("xdt_ready")
        kmod = core.sem("k_mod_ready")
        knorm_in, knorm = core.sem("key_norm_arg"), core.sem("key_norm")
        mnorm_in, mnorm = core.sem("mamba_norm_arg"), core.sem("mamba_norm")
        gnorm_in, gnorm = core.sem("group_norm_arg"), core.sem("group_norm")
        bonus_sum = core.sem("bonus_summed")
        ksq = core.sem("key_squared")
        skip = core.sem("skip_ready")
        ysq = core.sem("mamba_squared")
        om_rdy, or_rdy = core.sem("mamba_out_ready"), core.sem("rwkv_out_ready")
        bonus, bonus_v = core.sem("bonus_products"), core.sem("bonus_times_v")
        yinv, ginv = core.sem("mamba_inverse_root"), core.sem("group_inverse_root")
        stored = core.sem("states_stored")
        into = [1, 0, 1, 2, 4]
        frm = [0, 1, 0, 1, 3]

        def b_over(eng, i):
            b.wait_taken(eng, "s", i)
            b.wait_taken(eng, "om", i)
            eng.wait_ge(states, i + 1)
            eng.wait_ge(bonus_v, i + 1)

        def a_over(eng, i):
            eng.wait_ge(hats, 4 * (i + 1))
            eng.wait_ge(l_rdy, 2 * (i + 1))
            eng.wait_ge(xdt_rdy, 2 * (i + 1))
            eng.wait_ge(bonus_sum, i + 1)

        def a_fence(eng, i):
            if i:
                a_over(eng, i - 1)
            if i >= 2:
                b_over(eng, i - 2)
            if i >= 3:
                b.wait_taken(eng, "or", i - 3)

        def b_fence(eng, i):
            if i:
                b_over(eng, i - 1)

        def run_parts(parts):
            for part, i in tile_parts():
                if part in parts:
                    parts[part](i, *TILES[i])

        with nc.Block() as block:
            @block.sync
            def _(sp):
                for dst, src in ((cst[:, :], a["consts"]), (rows[:, :, :], a["rows"]),
                                 (heads_row[:, :], a["mamba_D"]), (w2[:, :], a["w2"]), (g2[:, :], a["g2"]),
                                 (st[:, 3, :, :], a["wkv_in"]), (ht[:, 3, :, :], a["ssm_in"])):
                    sp.dma_start(dst, src).then_inc(par_in, 16)

                def load(i):
                    tok, T, rc, xc = TILES[i]
                    for dst, src in ((pm_in[:, i % 2, :, 0:T], a["pm"][:, :, rc:rc + T]),
                                     (xbc_in[:, i % 2, :, 0:T], a["xbc"][:, :, xc:xc + T]),
                                     (z_in[:, i % 2, :, 0:T], a["z"][:, :, tok:tok + T]),
                                     (dt_in[:, i % 2, :, 0:T], a["dt"][:, :, tok:tok + T])):
                        sp.dma_start(dst, src).then_inc(rows_in[i % 2], 16)

                load(0)
                load(1)
                for i, (tok, T, rc, xc) in enumerate(TILES):
                    b_over(sp, i)
                    if i + 2 < NT:
                        load(i + 2)
                    b.wait_taken(sp, "or", i)
                    sp.dma_start(a["o"][:, :, tok:tok + T], oT[:, :, 0:T]).then_inc(sent, 16)
                sp.dma_start(a["wkv_out"][:, 0], st[:, 2, :, :]).then_inc(stored, 16)
                sp.dma_start(a["ssm_out"][:, 0], ht[:, 2, :, :]).then_inc(stored, 16)
                sp.dma_start(a["wkv_out"][:, 1], st[:, 4, :, :]).then_inc(stored, 16)
                sp.dma_start(a["ssm_out"][:, 1], ht[:, 4, :, :]).then_inc(stored, 16)
                sp.wait_ge(stored, 64)
                sp.wait_ge(sent, 16 * NT)

            @block.tensor
            def _(pe):
                pe.wait_ge(par_in, 7 * 16)
                pe.wait_ge(zeroed, 2)
                ident = core.ident
                link = core.chains["pe"].on(pe)

                def apart(ins, e, T):
                    if T < P and e == 1:
                        link(ins)

                def rows_of(i, T):
                    return (x[:, i % 2, :, 0:T] for x in (pm_in, xbc_in, z_in, dt_in))

                def turned(name, i, T, srcs):
                    o = b.start(pe, name, i)
                    for n, src in enumerate(srcs):
                        ins = pe.transpose(o[0:T, n * P:n * P + src.shape[0]], src,
                                           ident[0:src.shape[0], 0:src.shape[0]])
                    b.finish(ins)

                def four(name, i, T, lhs, rhs):
                    o = b.start(pe, name, i)
                    for q in range(4):
                        ins = pe.matmul(o[0:T, q * T:(q + 1) * T], lhs(q), rhs(q), start=True, stop=True)
                    b.finish(ins)

                def a1(i, tok, T, rc, xc):
                    a_fence(pe, i)
                    pmi, xbi, zi, dti = rows_of(i, T)
                    pe.wait_ge(rows_in[i % 2], 64 * (i // 2 + 1))
                    turned("k", i, T, [pmi[:, 4 + n] for n in range(4)])
                    pe.wait_ge(inner, 2 * (i + 1))
                    for name, lhs, rhs in (("w", pmi[0:HD, RT - 2], w2[0:HD, :]), ("a", pmi[HD:P, RT - 2], w2[HD:P, :])):
                        o = b.start(pe, name, i)
                        b.finish(pe.matmul(o[0:T, :], lhs, rhs, start=True, stop=True))
                    turned("r", i, T, [pmi[:, n] for n in range(4)])
                    turned("v", i, T, [pmi[:, 8 + n] for n in range(4)])
                    o = b.start(pe, "g", i)
                    b.finish(pe.matmul(o[0:T, :], pmi[:, RT - 1], g2[:, :], start=True, stop=True))
                    o = b.start(pe, "mb", i)
                    pe.transpose(o[0:T, 0:P], xbi[:, 4], ident[:, :])
                    pe.transpose(o[0:T, P:P + 8], dti[:, 0], ident[0:8, 0:8])
                    b.finish(pe.transpose(o[0:T, P + 8:P + 16], dti[:, 1], ident[0:8, 0:8]))
                    turned("mx", i, T, [xbi[:, n] for n in range(4)])
                    turned("mz", i, T, [zi[:, n] for n in range(4)])

                def a2(i, tok, T, rc, xc):
                    pmi, xbi, zi, dti = rows_of(i, T)
                    mbt = mbt2[:, i % 2]
                    pe.wait_ge(tanhs, 2 * (i + 1))
                    for name, m in (("cinc", C_DINC), ("cexc", C_DEXC)):
                        o = b.start(pe, name, i)
                        b.finish(pe.matmul(o[0:T, :], cst[0:T, m:m + T], wa[0:T, 0, :], start=True, stop=True))
                    o = b.start(pe, "dec", i)
                    for n in range(4):
                        ins = pe.matmul(o[:, 2 * n:2 * n + 2], wa[0:T, 0, n * P:(n + 1) * P],
                                        cst[0:T, C_DCOL:C_DCOL + 2], start=True, stop=True)
                    b.finish(ins)
                    b.wait_taken(pe, "mb", i)
                    o = b.start(pe, "cs", i)
                    da = mbt[0:T, P + 8:P + 16]
                    pe.matmul(o[0:T, 0:8], cst[0:T, C_TRI:C_TRI + T], da, start=True, stop=True)
                    pe.matmul(o[0:T, 8:16], cst[0:T, C_REV:C_REV + T], da, start=True, stop=True)
                    b.finish(pe.matmul(o[:, 16:24], core.ones[0:T, :], da, start=True, stop=True))
                    for g in range(2):
                        o = b.start(pe, f"cb{g}", i)
                        gs = slice(g * HD, (g + 1) * HD)
                        b.finish(pe.matmul(o[0:T, 0:T], xbi[gs, 4], xbi[gs, 5], start=True, stop=True))

                def a4(i, tok, T, rc, xc):
                    pe.wait_ge(dab_rdy, i + 1)
                    for g in range(2):
                        four(f"cst{g}", i, T, lambda h: dab[0:T, 4 * g + h, 0:T], lambda h: cst[0:T, C_TRI:C_TRI + T])

                def b1(i, tok, T, rc, xc):
                    b_fence(pe, i)
                    for n, (name, src) in enumerate((("bT", bh2[:, i % 2]), ("kT", kh2[:, i % 2]), ("aT", ah), ("rT", rh))):
                        pe.wait_ge(hats, 4 * i + n + 1)
                        o = b.start(pe, name, i)
                        for q in range(4):
                            ins = pe.transpose(o[:, q * T:(q + 1) * T], src[0:T, q * P:(q + 1) * P], ident[0:T, 0:T])
                        b.finish(ins)
                    b.wait_taken(pe, "aT", i)

                    def score(name, e, lhs, rhs):
                        es = slice(e * HD, (e + 1) * HD)
                        four(f"{name}{e}", i, T, lambda q: lhs[es, q, 0:T], lambda q: rhs[es, q, 0:T])

                    for name, lhs, rhs in (("ab", bT, aT), ("m", aT, bT)):
                        for e in range(2):
                            score(name, e, lhs, rhs)
                    b.wait_taken(pe, "rT", i)
                    for e in range(2):
                        for name, lhs, rhs in (("ak", kT, aT), ("rb", bT, rT), ("rk", kT, rT)):
                            score(name, e, lhs, rhs)

                def level(n):
                    def run(i, tok, T, rc, xc):
                        last = last_level(i)
                        xbi = xbc_in[:, i % 2, :, 0:T]
                        for e in range(2):
                            if n == 1:
                                pe.wait_ge(x_rdy, 4 * i + 2 * e + 2)
                            else:
                                b.wait_taken(pe, f"x{n - 1}{e}", i)
                            four(f"q{n}{e}", i, T, lambda q: mT[0:T, e, q, 0:T], lambda q: xx[0:T, e, q, 0:T])
                        for e in range(2):
                            b.wait_taken(pe, f"q{n}{e}", i)
                            if n > 1:
                                b.wait_taken(pe, f"t{n - 1}{e}", i)
                            if n < last:
                                four(f"x{n}{e}", i, T, lambda q: xt[0:T, e, q, 0:T], lambda q: pq[0:T, e, q, 0:T])
                            four(f"t{n}{e}", i, T, lambda q: pq[0:T, e, q, 0:T], lambda q: xt[0:T, e, q, 0:T])
                        if n == 1:
                            if i not in (0, 4):
                                b.wait_taken(pe, "st", i - 1)
                            for g in range(2):
                                gs = slice(g * HD, (g + 1) * HD)
                                o = b.start(pe, f"yo{g}", i)
                                b.finish(pe.matmul(o[0:T, 0:4 * HD], xbi[gs, 5], ht[gs, frm[i], :, :],
                                                   start=True, stop=True))
                        if n == 2:
                            pe.wait_ge(l_rdy, 2 * (i + 1))
                            pe.wait_ge(xdt_rdy, 2 * (i + 1))
                            o = b.start(pe, "yd", i)
                            for h in range(HEADS):
                                ins = pe.matmul(o[0:T, h * HD:(h + 1) * HD], seg2[0:T, i % 2, h, 0:T],
                                                xdt2[0:T, i % 2, h, :], start=True, stop=True)
                            b.finish(ins)
                        if n == 3:
                            o = b.start(pe, "st", i)
                            for g in range(2):
                                gs = slice(g * HD, (g + 1) * HD)
                                ins = pe.matmul(o[gs, 0:4 * HD], mbt2[0:T, i % 2, gs], xw2[0:T, i % 2, 4 * g:4 * g + 4, :],
                                                start=True, stop=True)
                            b.finish(ins)
                    return run

                def b5(i, tok, T, rc, xc):
                    vt, bh, kh = vt2[:, i % 2], bh2[:, i % 2], kh2[:, i % 2]
                    last = last_level(i)
                    pe.wait_ge(s0_rdy, i + 1)
                    for e in range(2):
                        es = slice(e * HD, (e + 1) * HD)
                        b.wait_taken(pe, f"ak{e}", i)
                        o = b.start(pe, f"y{e}", i)
                        for q in range(4):
                            oo = o[0:T, q * HD:(q + 1) * HD]
                            apart(pe.matmul(oo, aT[es, q, 0:T], s0m[es, q, :], start=True, stop=False), e, T)
                            ins = pe.matmul(oo, ak[0:T, e, q, 0:T], vt[0:T, 2 * q + e, :], start=False, stop=True)
                            if q < 3:
                                apart(ins, e, T)
                        b.finish(ins)
                    for e in range(2):
                        b.wait_taken(pe, f"y{e}", i)
                        b.wait_taken(pe, f"t{last}{e}", i)
                        o = b.start(pe, f"u{e}", i)
                        for q in range(4):
                            ins = pe.matmul(o[0:T, q * HD:(q + 1) * HD], xt[0:T, e, q, 0:T], ys[0:T, e, q, :],
                                            start=True, stop=True)
                        b.finish(ins)
                    for e in range(2):
                        es = slice(e * HD, (e + 1) * HD)
                        b.wait_taken(pe, f"u{e}", i)
                        o = b.start(pe, f"o{e}", i)
                        for q in range(4):
                            oo = o[0:T, q * HD:(q + 1) * HD]
                            apart(pe.matmul(oo, rT[es, q, 0:T], s0m[es, q, :], start=True, stop=False), e, T)
                            pe.matmul(oo, rk[0:T, e, q, 0:T], vt[0:T, 2 * q + e, :], start=False, stop=False)
                            ins = pe.matmul(oo, rb[0:T, e, q, 0:T], us[0:T, e, q, :], start=False, stop=True)
                            if q < 3:
                                apart(ins, e, T)
                        b.finish(ins)
                    o = b.start(pe, "s", i)
                    for h in range(HEADS):
                        q, e = h // 2, h % 2
                        hs = slice(h * HD, (h + 1) * HD)
                        oo = o[e * HD:(e + 1) * HD, q * HD:(q + 1) * HD]
                        pe.matmul(oo, bh[0:T, hs], us[0:T, e, q, :], start=True, stop=False)
                        ins = pe.matmul(oo, kh[0:T, hs], vt[0:T, h, :], start=False, stop=True)
                    b.finish(ins)
                    pe.wait_ge(om_rdy, i + 1)
                    outs("om", i, T, ym)

                def outs(name, i, T, src):
                    flat = src[:, :, :].rearrange("p h d -> p (h d)")
                    o = b.start(pe, name, i)
                    for q in range(4):
                        ins = pe.transpose(o[:, q * T:(q + 1) * T], flat[0:T, q * P:(q + 1) * P], ident[0:T, 0:T])
                    b.finish(ins)

                def c4(i, tok, T, rc, xc):
                    pe.wait_ge(or_rdy, i + 1)
                    outs("or", i, T, os_)

                run_parts({"A1": a1, "A2": a2, "A4": a4, "B1": b1, "B5": b5, "C4": c4,
                           **{f"L{n}": level(n) for n in range(1, LEVELS)}})

            @block.scalar
            def _(act):
                act.wait_ge(par_in, 7 * 16)

                def take(name, i, dst, cols, func=ACT.Copy, **kw):
                    src = b.get(act, name, i)[0:dst.shape[0], 0:cols]
                    if len(dst.shape) == 3:
                        src = src.rearrange("p (h d) -> p h d", d=dst.shape[2])
                    b.took(act.activation(dst, src, func, **kw), name, i)

                def a1(i, tok, T, rc, xc):
                    a_fence(act, i)
                    vt, gt, mxt, mzt, mbt = vt2[:, i % 2], gt3[:, i % 3], mxt2[:, i % 2], mzt2[:, i % 2], mbt2[:, i % 2]
                    act.wait_ge(rows_in[i % 2], 64 * (i // 2 + 1))
                    wd, gd = pm_in[0:HD, i % 2, RT - 2, 0:T], pm_in[:, i % 2, RT - 1, 0:T]
                    act.activation(wd, wd, ACT.Tanh).then_inc(inner, 1)
                    act.activation(gd, gd, ACT.Sigmoid).then_inc(inner, 1)
                    take("k", i, kt[0:T], 512)
                    for n in range(2):
                        b.wait_taken(act, ("w", "a")[n], i)
                        act.activation(wa[0:T, n, :], wa[0:T, n, :], ACT.Sigmoid).then_inc(tanhs, 1)
                    take("r", i, rt[0:T], 512)
                    take("v", i, vt[0:T], 512)
                    take("g", i, gt[0:T], 512)
                    take("mb", i, mbt[0:T, :], P + 16)
                    take("mx", i, mxt[0:T], 512)
                    take("mz", i, mzt[0:T], 512)

                def a2(i, tok, T, rc, xc):
                    o = b.get(act, "cinc", i)
                    o3 = o[0:T, :].rearrange("p (h d) -> p h d", d=HD)
                    act.activation(eneg[0:T], o3, ACT.Exp, scale=-1.0).then_inc(exps, 1)
                    b.took(act.activation(einc[0:T], o3, ACT.Exp), "cinc", i)
                    take("cexc", i, eexc[0:T], 512, ACT.Exp)
                    take("dec", i, dec2[:, i % 2, :, :], 8, ACT.Exp)
                    b.wait_taken(act, "cs", i)
                    act.activation(ecs2[0:T, i % 2], csv[0:T], ACT.Exp).then_inc(cse, 1)
                    act.activation(hdec2[0:HD, i % 2, :], msmall[0:HD, 0, 0:4], ACT.Exp).then_inc(cse, 1)
                    act.activation(hdec2[HD:P, i % 2, :], msmall[HD:P, 0, 4:8], ACT.Exp).then_inc(cse, 1)
                    act.wait_ge(knorm_in, i + 1)
                    act.activation(small[0:T, 1, :], small[0:T, 0, :], ACT.Sqrt).then_inc(knorm, 1)

                def a4(i, tok, T, rc, xc):
                    for g in range(2):
                        b.wait_taken(act, f"cst{g}", i)
                        sg = seg2[0:T, i % 2, 4 * g:4 * g + 4, 0:T]
                        act.activation(sg, sg, ACT.Exp).then_inc(seg_exp, 1)

                def b1(i, tok, T, rc, xc):
                    b_fence(act, i)
                    for name, dst in (("bT", bT), ("kT", kT), ("aT", aT), ("rT", rT)):
                        take(name, i, dst[:, :, 0:T], 4 * T)

                def level(n):
                    def run(i, tok, T, rc, xc):
                        for e in range(2):
                            if n < last_level(i):
                                take(f"x{n}{e}", i, xx[0:T, e, :, 0:T], 4 * T)
                            take(f"t{n}{e}", i, xt[0:T, e, :, 0:T], 4 * T)
                        if n == 4:
                            act.wait_ge(mnorm_in, i + 1)
                            act.activation(msmall[0:T, 3, 0:2], msmall[0:T, 2, 0:2], ACT.Sqrt).then_inc(mnorm, 1)
                    return run

                def b5(i, tok, T, rc, xc):
                    for e in range(2):
                        take(f"y{e}", i, ys[0:T, e], 4 * HD)
                    for e in range(2):
                        take(f"u{e}", i, us[0:T, e], 4 * HD)
                    for e in range(2):
                        take(f"o{e}", i, os_[0:T, e::2, :], 4 * HD)
                    if i:
                        act.wait_ge(sent, 16 * i)
                    take("om", i, oT[:, 4:8, 0:T], 4 * T)

                def c2(i, tok, T, rc, xc):
                    act.wait_ge(gnorm_in, i + 1)
                    act.activation(small_b[0:T, 5, :], small_b[0:T, 4, :], ACT.Sqrt).then_inc(gnorm, 1)

                def c4(i, tok, T, rc, xc):
                    take("or", i, oT[:, 0:4, 0:T], 4 * T)

                run_parts({"A1": a1, "A2": a2, "A4": a4, "B1": b1, "B5": b5, "C2": c2, "C4": c4,
                           **{f"L{n}": level(n) for n in range(1, LEVELS)}})

            @block.gpsimd
            def _(pool):
                pool.memset(st[:, 0, :, :], 0.0).then_inc(zeroed, 1)
                pool.memset(ht[:, 0, :, :], 0.0).then_inc(zeroed, 1)
                pool.wait_ge(par_in, 7 * 16)
                link = core.chains["pool"].on(pool)

                TT = pool.tensor_tensor

                def row(n, T):
                    return rows[0:T, n, :].rearrange("p (h d) -> p h d", d=HD)

                def per_head(ap, T):
                    return bc(ap, 2, [T, HEADS, HD])

                def a1(i, tok, T, rc, xc):
                    a_fence(pool, i)
                    b.wait_taken(pool, "k", i)
                    link(TT(kk[0:T], kt[0:T], row(2, T), ALU.mult))
                    TT(t0[0:T], kk[0:T], kk[0:T], ALU.mult).then_inc(ksq, 1)

                def a2(i, tok, T, rc, xc):
                    b.wait_taken(pool, "mb", i)
                    pool.tensor_copy(dab[0:T, :, 0:T], bc(mbt2[0:T, i % 2, P + 8:P + 16], 2, [T, HEADS, T])).then_inc(dab_rdy, 1)
                    b.wait_taken(pool, "mx", i)
                    TT(xdt2[0:T, i % 2], mxt2[0:T, i % 2], per_head(mbt2[0:T, i % 2, P:P + 8], T), ALU.mult).then_inc(xdt_rdy, 1)

                def a3(i, tok, T, rc, xc):
                    pool.wait_ge(kmod, i + 1)
                    b.wait_taken(pool, "r", i)
                    link(TT(t1[0:T], rt[0:T], km[0:T], ALU.mult))
                    TT(t1[0:T], t1[0:T], row(4, T), ALU.mult).then_inc(bonus, 1)
                    pool.wait_ge(cse, 3 * (i + 1))
                    pool.wait_ge(xdt_rdy, 2 * i + 1)
                    TT(xw2[0:T, i % 2], xdt2[0:T, i % 2], per_head(ecs2[0:T, i % 2, 1, :], T), ALU.mult).then_inc(xdt_rdy, 1)

                def l1(i, tok, T, rc, xc):
                    b_fence(pool, i)
                    TT(t2[0:T], mxt2[0:T, i % 2], per_head(heads_row[0:T, :], T), ALU.mult).then_inc(skip, 1)

                def l2(i, tok, T, rc, xc):
                    b.wait_taken(pool, "yd", i)
                    b.wait_taken(pool, "mz", i)
                    pool.wait_ge(skip, i + 1)
                    link(TT(ym[0:T], ym[0:T], t2[0:T], ALU.add))
                    link(TT(ym[0:T], ym[0:T], mzt2[0:T, i % 2], ALU.mult))
                    TT(t2[0:T], ym[0:T], ym[0:T], ALU.mult).then_inc(ysq, 1)

                def l5(i, tok, T, rc, xc):
                    pool.wait_ge(yinv, i + 1)
                    y2 = ym[0:T].rearrange("p (g h) d -> p g (h d)", g=2)
                    link(TT(y2, y2, bc(msmall[0:T, 1, 0:2], 2, [T, 2, 4 * HD]), ALU.mult))
                    TT(ym[0:T], ym[0:T], row(7, T), ALU.mult).then_inc(om_rdy, 1)

                def b5(i, tok, T, rc, xc):
                    if i:
                        pool.wait_ge(or_rdy, i)
                    pool.wait_ge(bonus_sum, i + 1)
                    TT(t4[0:T], vt2[0:T, i % 2], per_head(bonus2[0:T, i % 2, :], T), ALU.mult).then_inc(bonus_v, 1)

                def c3(i, tok, T, rc, xc):
                    pool.wait_ge(ginv, i + 1)
                    pool.wait_ge(bonus_v, i + 1)
                    link(TT(os_[0:T], os_[0:T], per_head(small_b[0:T, 6, :], T), ALU.mult))
                    link(TT(os_[0:T], os_[0:T], row(5, T), ALU.mult))
                    link(TT(os_[0:T], os_[0:T], row(6, T), ALU.add))
                    link(TT(os_[0:T], os_[0:T], t4[0:T], ALU.add))
                    TT(os_[0:T], os_[0:T], gt3[0:T, i % 3], ALU.mult).then_inc(or_rdy, 1)

                run_parts({"A1": a1, "A2": a2, "A3": a3, "L1": l1, "L2": l2, "L5": l5, "B5": b5, "C3": c3})

            @block.vector
            def _(dve):
                link = core.chains["dve"].on(dve)
                dve.wait_ge(par_in, 7 * 16)
                dve.wait_ge(zeroed, 2)
                TT, STT, TS = dve.tensor_tensor, dve.scalar_tensor_tensor, dve.tensor_scalar

                def row(n, T):
                    return rows[0:T, n, :].rearrange("p (h d) -> p h d", d=HD)

                def h3(ap):
                    return ap.rearrange("p (h d) -> p h d", d=HD)

                def per_head(ap, T):
                    return bc(ap, 2, [T, HEADS, HD])

                def mask4(c, T):
                    return bc(cst[0:T, c:c + T], 1, [T, 4, T])

                def q4(o, T):
                    return o[0:T, 0:4 * T].rearrange("p (q t) -> p q t", t=T)

                def a1(i, tok, T, rc, xc):
                    a_fence(dve, i)
                    for n, name in enumerate(("w", "a")):
                        o = b.get(dve, name, i)[0:T, :]
                        b.took(TT(wa[0:T, n, :], o, rows[0:T, n, :], ALU.add), name, i)

                def a2(i, tok, T, rc, xc):
                    dve.wait_ge(ksq, i + 1)
                    dve.tensor_reduce(small[0:T, 0, :], t0[0:T], AX_X, ALU.add).then_inc(knorm_in, 1)
                    o = b.get(dve, "cs", i)
                    dve.tensor_copy(csv[0:T], o[0:T, 0:16].rearrange("p (a h) -> p a h", h=HEADS))
                    b.took(dve.tensor_copy(msmall[:, 0, :], o[:, 16:24]), "cs", i)
                    for g in range(2):
                        o = b.get(dve, f"cb{g}", i)
                        b.took(TT(cb[0:T, g, 0:T], o[0:T, 0:T], cst[0:T, C_TRI:C_TRI + T], ALU.mult), f"cb{g}", i)
                    dve.wait_ge(tanhs, 2 * (i + 1))
                    dve.wait_ge(knorm_in, i + 1)
                    b.wait_taken(dve, "k", i)
                    link(STT(out=t0[0:T], in0=h3(wa[0:T, 1, :]), scalar=1.0, in1=row(3, T), op0=ALU.subtract, op1=ALU.mult))
                    STT(out=km[0:T], in0=t0[0:T], scalar=1.0, in1=kt[0:T], op0=ALU.add, op1=ALU.mult).then_inc(kmod, 1)
                    dve.wait_ge(kmod, i + 1)

                def a3(i, tok, T, rc, xc):
                    dve.wait_ge(knorm, i + 1)
                    link(TS(small[0:T, 2, :], small[0:T, 1, :], 1e-12, None, ALU.max))
                    link(dve.reciprocal(small[0:T, 3, :], small[0:T, 2, :]))
                    link(TT(kk[0:T], kk[0:T], per_head(small[0:T, 3, :], T), ALU.mult))
                    link(TT(t0[0:T], kk[0:T], h3(wa[0:T, 1, :]), ALU.mult))
                    b.wait_taken(dve, "dec", i)
                    b.wait_taken(dve, "r", i)
                    if i:
                        b.wait_taken(dve, "rT", i - 1)
                    TT(h3(bh2[0:T, i % 2, :]), t0[0:T], eneg[0:T], ALU.mult).then_inc(hats, 1)
                    TT(h3(kh2[0:T, i % 2, :]), km[0:T], eneg[0:T], ALU.mult).then_inc(hats, 1)
                    STT(out=h3(ah[0:T, :]), in0=kk[0:T], scalar=-1.0, in1=eexc[0:T], op0=ALU.mult, op1=ALU.mult).then_inc(hats, 1)
                    TT(h3(rh[0:T, :]), rt[0:T], einc[0:T], ALU.mult).then_inc(hats, 1)

                def a4(i, tok, T, rc, xc):
                    b.wait_taken(dve, "cs", i)
                    for g in range(2):
                        o = b.get(dve, f"cst{g}", i)
                        for h in range(4):
                            ins = TS(seg2[0:T, i % 2, 4 * g + h, 0:T], o[0:T, h * T:(h + 1) * T],
                                     csv[0:T, 0, 4 * g + h:4 * g + h + 1], 0.0, ALU.subtract, ALU.min)
                        b.took(ins, f"cst{g}", i)
                    dve.wait_ge(bonus, i + 1)
                    dve.tensor_reduce(bonus2[0:T, i % 2, :], t1[0:T], AX_X, ALU.add).then_inc(bonus_sum, 1)

                def a5(i, tok, T, rc, xc):
                    for g in range(2):
                        dve.wait_ge(seg_exp, 2 * i + g + 1)
                        b.wait_taken(dve, f"cb{g}", i)
                        sg = seg2[0:T, i % 2, 4 * g:4 * g + 4, 0:T]
                        TT(sg, sg, bc(cb[0:T, g, 0:T], 1, [T, 4, T]), ALU.mult).then_inc(l_rdy, 1)

                def b1(i, tok, T, rc, xc):
                    b_fence(dve, i)
                    TT(s0m[:], st[:, frm[i]], bc(dec2[:, i % 2, :, 0], 2, [P, 4, HD]), ALU.mult).then_inc(s0_rdy, 1)

                    def masked(name, e, dst, mask):
                        o = q4(b.get(dve, f"{name}{e}", i), T)
                        b.took(TT(dst[0:T, e, :, 0:T], o, mask4(mask, T), ALU.mult), f"{name}{e}", i)

                    one = bc(core.ident[0:T, 0:T], 1, [T, 4, T])
                    for e in range(2):
                        masked("ab", e, mT, C_MS)
                    for e in range(2):
                        masked("m", e, xx, C_LEV)
                    for e in range(2):
                        b.wait_taken(dve, f"m{e}", i)
                        link(TT(mT[0:T, e, :, 0:T], mT[0:T, e, :, 0:T], one, ALU.add))
                        TT(xt[0:T, e, :, 0:T], mT[0:T, e, :, 0:T], mask4(C_LT0, T), ALU.mult).then_inc(x_rdy, 1)
                        TT(xx[0:T, e, :, 0:T], xx[0:T, e, :, 0:T], one, ALU.add).then_inc(x_rdy, 1)
                    for e in range(2):
                        masked("ak", e, ak, C_MS)
                        masked("rb", e, rb, C_TRI)
                        masked("rk", e, rk, C_TRI)

                def level(n):
                    def run(i, tok, T, rc, xc):
                        ecs, hdec = ecs2[:, i % 2], hdec2[:, i % 2]
                        for e in range(2):
                            o = q4(b.get(dve, f"q{n}{e}", i), T)
                            b.took(TT(pq[0:T, e, :, 0:T], o, mask4(C_LEV + n * P, T), ALU.mult), f"q{n}{e}", i)
                        if n == 1:
                            for g in range(2):
                                o = b.get(dve, f"yo{g}", i)[0:T, 0:4 * HD]
                                b.took(TT(ym[0:T, 4 * g:4 * g + 4, :], h3(o),
                                          bc(ecs[0:T, 0, 4 * g:4 * g + 4], 2, [T, 4, HD]), ALU.mult), f"yo{g}", i)
                        if n == 2:
                            o = b.get(dve, "yd", i)[0:T, :]
                            b.wait_taken(dve, "yo1", i)
                            b.took(TT(ym[0:T], h3(o), ym[0:T], ALU.add), "yd", i)
                        if n == 3:
                            link(TT(t5[:], ht[:, frm[i]], bc(hdec[:, :], 2, [P, 4, HD]), ALU.mult))
                            o = b.get(dve, "st", i)[:, 0:4 * HD]
                            b.took(TT(ht[:, into[i]], h3(o), t5[:], ALU.add), "st", i)
                            b.wait_taken(dve, "st", i)
                        if n == 4:
                            dve.wait_ge(ysq, i + 1)
                            link(dve.tensor_reduce(msmall[0:T, 1, 0:2],
                                                   t2[0:T].rearrange("p (g h) d -> p g (h d)", g=2), AX_X, ALU.add))
                            TS(msmall[0:T, 2, 0:2], msmall[0:T, 1, 0:2], 1.0 / 256, NORM_EPS, ALU.mult,
                               ALU.add).then_inc(mnorm_in, 1)
                        if n == 5:
                            dve.wait_ge(mnorm, i + 1)
                            dve.reciprocal(msmall[0:T, 1, 0:2], msmall[0:T, 3, 0:2]).then_inc(yinv, 1)
                    return run

                def b5(i, tok, T, rc, xc):
                    o = b.get(dve, "s", i)[:, 0:4 * HD]
                    b.took(TT(t5[:], h3(o), s0m[:], ALU.add), "s", i)
                    b.wait_taken(dve, "s", i)
                    TT(st[:, into[i]], t5[:], bc(dec2[:, i % 2, :, 1], 2, [P, 4, HD]), ALU.mult).then_inc(states, 1)

                def c1(i, tok, T, rc, xc):
                    b.wait_taken(dve, "o1", i)
                    if i:
                        dve.wait_ge(or_rdy, i)
                    link(dve.tensor_reduce(small_b[0:T, 0, :], os_[0:T], AX_X, ALU.add))
                    link(TS(small_b[0:T, 1, :], small_b[0:T, 0, :], 1.0 / HD, None, ALU.mult))
                    link(TT(os_[0:T], os_[0:T], per_head(small_b[0:T, 1, :], T), ALU.subtract))
                    link(TT(t3[0:T], os_[0:T], os_[0:T], ALU.mult))
                    link(dve.tensor_reduce(small_b[0:T, 2, :], t3[0:T], AX_X, ALU.add))
                    TS(small_b[0:T, 4, :], small_b[0:T, 2, :], 1.0 / HD, GN_EPS, ALU.mult, ALU.add).then_inc(gnorm_in, 1)

                def c3(i, tok, T, rc, xc):
                    dve.wait_ge(gnorm, i + 1)
                    dve.reciprocal(small_b[0:T, 6, :], small_b[0:T, 5, :]).then_inc(ginv, 1)

                run_parts({"A1": a1, "A2": a2, "A3": a3, "A4": a4, "A5": a5, "B1": b1, "B5": b5, "C1": c1, "C3": c3,
                           **{f"L{n}": level(n) for n in range(1, LEVELS)}})


def project_out(core, acts):
    nc, a = core.nc, core.a
    with ExitStack() as ctx:
        norm = Norm(core, ctx, "n2", acts, 1, True, 4)
        gemm = Gemm(core, ctx, "wout", acts, DT, a["w_out"])
        om = core.sb("mixed_o", [P, DT, TOK], ctx=ctx)
        x_in, o_in = core.sem("res_in"), core.sem("o_in")
        high, low, added = core.sem("o_high"), core.sem("o_low"), core.sem("res_added")

        with nc.Block() as block:
            @block.sync
            def _(sp):
                sp.dma_start(om[:, :, :], a["o"]).then_inc(o_in, 16)
                sp.dma_start(acts.x[:, :, :], a["x"]).then_inc(x_in, 16)
                for c in range(DT):
                    gemm.load(sp, c)

            @block.gpsimd
            def _(pool):
                for c in range(DT):
                    gemm.split_low(pool, c)

            @block.tensor
            def _(pe):
                pe.wait_ge(low, DT)
                for c in range(DT):
                    gemm.multiply(pe, c)
                norm.pe_sums(pe)

            @block.scalar
            def _(act):
                act.wait_ge(o_in, 16)
                for dt in range(DT):
                    act.activation(acts.hi[:, dt, :], om[:, dt, :], ACT.Copy).then_inc(high, 1)
                for c in range(DT):
                    gemm.split_high(act, c)
                norm.act_squares(act, ready=lambda dt: (gemm.taken, dt + 1))
                norm.act_root(act)
                norm.act_high(act)

            @block.vector
            def _(dve):
                for dt in range(DT):
                    dve.wait_ge(high, dt + 1)
                    dve.tensor_tensor(acts.lo[:, dt, :], om[:, dt, :], acts.hi[:, dt, :].bitcast(F32),
                                      ALU.subtract).then_inc(low, 1)
                dve.wait_ge(x_in, 16)
                for c in range(DT):
                    dve.wait_ge(gemm.done, c + 1)
                    for half in range(2):
                        x = acts.x[:, c, half * HALF:(half + 1) * HALF]
                        ins = dve.tensor_tensor(x, gemm.out(c, half), x, ALU.add)
                        ins.then_inc((added, gemm.taken)[half], 1)
                dve.wait_ge(gemm.taken, DT)
                norm.dve(dve)


def route_jobs(nq):
    jobs, h = [], 0
    for c in range(nq):
        for _ in range(2 if c >= 4 else 0):
            jobs.append(("hidden", h))
            h += 1
        jobs.append(("q", c))
    return jobs + [("hidden", n) for n in range(h, AHEAD4)]


def route(core, acts, sel):
    nc, a = core.nc, core.a
    with ExitStack() as ctx:
        def sb(name, *shape, dt=F32):
            return core.sb(name, list(shape), dt, ctx)

        NC = 2 * P_HEADS
        jobs = route_jobs(NC)
        tiles = [a["w_q"][n] if kind == "q" else a["u"][KEY4 + n] for kind, n in jobs]
        job_of_q = {n: j for j, (kind, n) in enumerate(jobs) if kind == "q"}
        exp_after = {job_of_q[2 * h + 4] if h < P_HEADS - 2 else len(jobs) - 4: h for h in range(P_HEADS - 1)}
        match_after = {j - 1: h for j, h in exp_after.items()}
        gemm = Gemm(core, ctx, "q", acts, len(jobs), tiles)
        gelu = sb("gelu_ahead", P, 2, TOK)
        gelu_sent = [core.sem(f"gelu_ahead_sent{n}") for n in range(2)]
        keys = sb("sub_keysT", P, 2, N_KEYS)
        ranks = sb("ranks", P, TOPK)
        qT = sb("qT", P, 2, TOK)
        sc = sb("scores", P, 2, NT, N_KEYS)
        left = sb("scores_left", P, NT, N_KEYS)
        val = sb("top_values", P, 2, NT, TOPK)
        idx = sb("top_index", P, 2, NT, TOPK, dt=U32)
        idf = sb("top_index_f", P, 2, 2, NT, TOPK)
        match = sb("rank_match", P, 2, NT, TOPK * TOPK)
        cand = sb("candidates", P, NT, TOPK * TOPK)
        cleft = sb("candidates_left", P, NT, TOPK * TOPK)
        tv = sb("pick_values", P, 2, NT, TOPK)
        tp = sb("pick_pos", P, NT, TOPK, dt=U32)
        rk = sb("pick_rank", P, 2, NT, TOPK, dt=U32)
        rkf = sb("pick_rank_f", P, 2, NT, TOPK)
        gsum = sb("gate_sum", P, NT, 2)
        picks = sb("picks", P, NT, 3, SEL)
        par_in = core.sem("route_in")
        s_done, s_taken = core.sem("scores_done"), core.sem("scores_taken")
        ranked, zeroed = core.sem("ranked"), core.sem("scores_zeroed")
        e_in, e_out = core.sem("gate_args"), core.sem("gate_exps")
        picked, turned, sel_out = core.sem("picked"), core.sem("picks_turned"), core.sem("picks_out")
        matched, keyed = core.sem("ranks_matched"), core.sem("keys_matched")

        with nc.Block() as block:
            @block.sync
            def _(sp):
                sp.dma_start(keys[:, :, :], a["keysT"]).then_inc(par_in, 16)
                sp.dma_start(ranks[:, :], a["ranks"][:, 0:TOPK]).then_inc(par_in, 16)
                def send(j):
                    kind, n = jobs[j]
                    if kind == "hidden":
                        sp.wait_ge(gemm.taken, j + 1)
                        sp.dma_start(a["hidden"][n], gelu[:, n % 2, :]).then_inc(gelu_sent[n % 2], 16)

                LAG = 4
                for j in range(len(jobs)):
                    gemm.load(sp, j)
                    if j >= LAG:
                        send(j - LAG)
                for j in range(len(jobs) - LAG, len(jobs)):
                    send(j)
                for n in range(2):
                    sp.wait_ge(gelu_sent[n], 16 * (AHEAD4 // 2))

            @block.gpsimd
            def _(pool):
                pool.memset(sc[:, :, NT - 1, :], 0.0).then_inc(zeroed, 1)
                def match_keys(h):
                    grid = [P, NT, TOPK, TOPK]
                    for side in range(2):
                        pool.wait_ge(matched, 2 * h + side + 1)
                        e4 = match[:, side].rearrange("p n (a b) -> p n a b", a=TOPK)
                        pool.tensor_tensor(e4, e4, bc(idf[:, h % 2, side], 2, grid), ALU.mult).then_inc(keyed, 1)

                for j in range(len(jobs)):
                    gemm.split_low(pool, j)
                    if j in match_after:
                        match_keys(match_after[j])
                match_keys(P_HEADS - 1)

            @block.tensor
            def _(pe):
                def scores(c):
                    pe.wait_ge(gemm.taken, job_of_q[c] + 1)
                    if c >= 2:
                        pe.wait_ge(s_taken, c - 1)
                    for n, (tok, T, _, _) in enumerate(TILES):
                        bank = core.bank(4 + 2 * (c % 2) + n // 4)
                        ins = pe.matmul(bank[0:T, (n % 4) * P:(n % 4 + 1) * P], qT[:, c % 2, tok:tok + T],
                                        keys[:, c % 2, :], start=True, stop=True)
                    ins.then_inc(s_done, 1)

                pe.wait_ge(par_in, 32)
                for j, (kind, n) in enumerate(jobs):
                    gemm.multiply(pe, j)
                    if j and jobs[j - 1][0] == "q":
                        scores(jobs[j - 1][1])
                for n, (tok, T, _, _) in enumerate(TILES):
                    pe.wait_ge(picked, 3 * P_HEADS)
                    if n >= 2:
                        pe.wait_ge(sel_out, n - 1)
                    for k in range(3):
                        ins = pe.transpose(core.psum[:, n % 2, k * P:k * P + T], picks[0:T, n, k, :],
                                           core.ident[0:T, 0:T])
                    ins.then_inc(turned, 1)

            @block.scalar
            def _(act):
                def take_scores(c):
                    act.wait_ge(s_done, c + 1)
                    act.wait_ge(zeroed, 1)
                    if c >= 2:
                        act.wait_ge(ranked, c - 1)
                    bank = core.bank(4 + 2 * (c % 2))
                    act.activation(sc[:, c % 2, 0:4, :], bank.rearrange("p (n k) -> p n k", n=4), ACT.Copy)
                    bank = core.bank(5 + 2 * (c % 2))
                    act.activation(sc[0:DEC_SEQ, c % 2, 4, :], bank[0:DEC_SEQ, 0:P], ACT.Copy).then_inc(s_taken, 1)

                def gate_exp(h):
                    act.wait_ge(e_in, h + 1)
                    act.activation(tv[:, h % 2], tv[:, h % 2], ACT.Exp).then_inc(e_out, 1)

                gemm.split_high(act, 0)
                for j, (kind, n) in enumerate(jobs):
                    if j + 1 < len(jobs):
                        gemm.split_high(act, j + 1)
                    act.wait_ge(gemm.done, j + 1)
                    if kind == "q":
                        if n >= 2:
                            act.wait_ge(s_done, n - 1)
                        act.activation(qT[:, n % 2, 0:HALF], gemm.out(j, 0), ACT.Copy)
                        act.activation(qT[:, n % 2, HALF:], gemm.out(j, 1), ACT.Copy).then_inc(gemm.taken, 1)
                    else:
                        if n >= 2:
                            act.wait_ge(gelu_sent[n % 2], 16 * (n // 2))
                        act.activation(gelu[:, n % 2, 0:HALF], gemm.out(j, 0), ACT.Gelu)
                        act.activation(gelu[:, n % 2, HALF:], gemm.out(j, 1), ACT.Gelu).then_inc(gemm.taken, 1)
                    if j and jobs[j - 1][0] == "q":
                        take_scores(jobs[j - 1][1])
                    if j in exp_after:
                        gate_exp(exp_after[j])
                gate_exp(P_HEADS - 1)
                for n, (tok, T, _, _) in enumerate(TILES):
                    act.wait_ge(turned, n + 1)
                    act.activation(sel[:, :, tok:tok + T],
                                   core.psum[:, n % 2, 0:3 * P].rearrange("p (k t) -> p k t", k=3)[:, :, 0:T],
                                   ACT.Copy).then_inc(sel_out, 1)

            @block.vector
            def _(dve):
                link = core.chains["dve"].on(dve)

                def top16(values, index, source, rest, read=None):
                    for n in range(NT):
                        ins = dve.max(values[:, n, 0:8], source[:, n, :])
                    link(ins)
                    for n in range(NT):
                        dve.match_replace(rest[:, n, :], values[:, n, 0:8], source[:, n, :], LOWEST)
                        ins = dve.max_index(index[:, n, 0:8], values[:, n, 0:8], source[:, n, :])
                    if read is None:
                        link(ins)
                    else:
                        ins.then_inc(read[0], 1)
                        dve.wait_ge(*read)
                    for n in range(NT):
                        ins = dve.max(values[:, n, 8:16], rest[:, n, :])
                    link(ins)
                    for n in range(NT):
                        ins = dve.max_index(index[:, n, 8:16], values[:, n, 8:16], rest[:, n, :])
                    link(ins)

                def finish_picks(h):
                    hs = slice(h * TOPK, (h + 1) * TOPK)
                    for side in range(2):
                        dve.wait_ge(keyed, 2 * h + side + 1)
                        e4 = match[:, side].rearrange("p n (a b) -> p n a b", a=TOPK)
                        dve.tensor_reduce(picks[:, :, side, hs], e4, AX_X, ALU.add).then_inc(picked, 1)
                    dve.wait_ge(e_out, h + 1)
                    link(dve.tensor_reduce(gsum[:, :, 0], tv[:, h % 2], AX_X, ALU.add))
                    link(dve.reciprocal(gsum[:, :, 1], gsum[:, :, 0]))
                    dve.tensor_tensor(picks[:, :, 2, hs], tv[:, h % 2], gsum[:, :, 1:2].broadcast_to([P, NT, TOPK]),
                                      ALU.mult).then_inc(picked, 1)
                    dve.wait_ge(picked, 3 * h + 3)

                for h in range(P_HEADS):
                    for side in range(2):
                        c = 2 * h + side
                        dve.wait_ge(s_taken, c + 1)
                        top16(val[:, side], idx[:, side], sc[:, side], left, read=(ranked, c + 1))
                        if side == 0 and h:
                            finish_picks(h - 1)
                    link(dve.tensor_copy(idf[:, h % 2], idx[:, :, :, :]))
                    c4 = cand[:, :, :].rearrange("p n (a b) -> p n a b", a=TOPK)
                    grid = [P, NT, TOPK, TOPK]
                    link(dve.tensor_tensor(c4, bc(val[:, 0], 3, grid), bc(val[:, 1], 2, grid), ALU.add))
                    top16(tv[:, h % 2], tp, cand, cleft)
                    dve.tensor_scalar(rk[:, 0], tp[:, :, :], 4, None, ALU.logical_shift_right)
                    link(dve.tensor_scalar(rk[:, 1], tp[:, :, :], TOPK - 1, None, ALU.bitwise_and))
                    dve.tensor_copy(gsum[:, :, 1:2], tv[:, h % 2, :, 0:1])
                    link(dve.tensor_copy(rkf[:, :, :, :], rk[:, :, :, :]))
                    for side in range(2):
                        dve.tensor_tensor(match[:, side].rearrange("p n (a b) -> p n a b", a=TOPK), bc(rkf[:, side], 3, grid),
                                          ranks[:, :].unsqueeze(1).unsqueeze(1).broadcast_to(grid),
                                          ALU.is_equal).then_inc(matched, 1)
                    dve.tensor_tensor(tv[:, h % 2], tv[:, h % 2], gsum[:, :, 1:2].broadcast_to([P, NT, TOPK]),
                                      ALU.subtract).then_inc(e_in, 1)
                    dve.wait_ge(e_in, h + 1)
                    dve.wait_ge(matched, 2 * h + 2)
                finish_picks(P_HEADS - 1)


def spread_gates(core, acts, sel):
    nc, a = core.nc, core.a
    with ExitStack() as ctx:
        FOUR, SLOTS, PER = 4, 4, 2 * TB // 4
        iota = core.sb("iota", [P, N_KEYS], ctx=ctx)
        cur = core.sb("cur_picks", [P, 3, 2 * TB], ctx=ctx)
        onea = core.sb("onehot_first", [P, SLOTS * FOUR, N_KEYS], ctx=ctx)
        oneb = core.sb("gated_second", [P, SLOTS * FOUR, N_KEYS], ctx=ctx)
        stage = core.sb("gate_stage", [P, 2, NG, TB, JJ], ctx=ctx)
        iota_in = core.sem("iota_in")
        onehots = core.sem("onehots_ready")
        bank_done = core.sem("gates_done")
        staged = core.sem("gates_staged")
        sent = [core.sem(f"gates_sent{n}") for n in range(2)]
        copied = core.sem("picks_copied")
        steps = G_STEPS
        BANKS = 4
        AFTER = {9: (0, 0), 11: (0, 1), 13: (1, 0), 15: (1, 1)}
        SPLIT = {5: 0, 7: 1}
        u_raw = core.sb("u_ahead", [P, 2, DT * P], ctx=ctx)
        uh = core.sb("u_ahead_high", [P, 2, DT * P], F32R, ctx=ctx)
        ul = core.sb("u_ahead_low", [P, 2, DT * P], F32R, ctx=ctx)
        gelu = core.sb("gelu_ahead5", [P, 2, TOK], ctx=ctx)
        u_in = [core.sem(f"u_ahead_in{n}") for n in range(2)]
        u_high = core.sem("u_ahead_high_done")
        u_low = core.sem("u_ahead_low_done")
        hid_done = core.sem("ahead_done")
        gelu_done = core.sem("gelu_ahead_done")
        gelu_sent = [core.sem(f"gelu_ahead5_sent{n}") for n in range(2)]

        def hid_bank(s, half):
            return core.psum[:, 4 + 2 * s + half, 0:HALF]

        with nc.Block() as block:
            @block.sync
            def _(sp):
                sp.dma_start(iota[:, :], a["ranks"]).then_inc(iota_in, 16)
                with sp.Fori(0, steps) as it:
                    def send_gates(b):
                        sp.wait_ge(staged, it * PER + 8 * (b + 1) + BANKS)
                        dst = a["gates"][:, :, bass.ds(it * (2 * TB) + b * TB, TB), :].rearrange("g p t j -> p g (t j)")
                        sp.dma_start(dst, stage[:, b].rearrange("p g t j -> p g (t j)")).then_inc(sent[b], 16)

                    for s in range(2):
                        sp.wait_ge(u_low, it * 2 + s + 1)
                        sp.dma_start(u_raw[:, s], a["u"][bass.ds(it * 2 + (KEY5 + s), 1)].rearrange(
                            "o p n -> p (o n)")).then_inc(u_in[s], 16)
                    send_gates(0)
                    for s in range(2):
                        sp.wait_ge(gelu_done, it * 4 + 2 * s + 2 + 4)
                        sp.dma_start(a["hidden"][bass.ds(it * 2 + (AHEAD4 + s), 1)].rearrange("o p t -> p (o t)"),
                                     gelu[:, s, :]).then_inc(gelu_sent[s], 16)
                        if s == 0:
                            send_gates(1)
                for b in range(2):
                    sp.wait_ge(sent[b], 16 * (steps + 1))
                    sp.wait_ge(gelu_sent[b], 16 * (steps + 1))

            @block.gpsimd
            def _(pool):
                pool.sem_inc(u_low, 2)
                with pool.Fori(0, steps) as it:
                    for s in range(2):
                        pool.wait_ge(u_high, it * 2 + s + 1)
                        pool.tensor_tensor(ul[:, s], u_raw[:, s], uh[:, s].bitcast(F32), ALU.subtract).then_inc(u_low, 1)

            @block.tensor
            def _(pe):
                pe.sem_inc(hid_done, 4)
                with pe.Fori(0, steps) as it:
                    for g in range(PER):
                        pe.wait_ge(onehots, it * PER + g + 2)
                        pe.wait_ge(staged, it * PER + g + 1)
                        for t in range(FOUR):
                            s = (g % SLOTS) * FOUR + t
                            ins = pe.matmul(core.psum[:, g % BANKS, t * P:(t + 1) * P], onea[:, s, :], oneb[:, s, :],
                                            start=True, stop=True)
                        ins.then_inc(bank_done, 1)
                        if g in AFTER:
                            s, half = AFTER[g]
                            pe.wait_ge(u_low, it * 2 + s + 1 + 2)
                            pe.wait_ge(gelu_done, it * 4 + 2 * s + half + 1)
                            cols = slice(half * HALF, (half + 1) * HALF)
                            for dt in range(DT):
                                w = slice(dt * P, (dt + 1) * P)
                                ins = three_products(pe, hid_bank(s, half), uh[:, s, w], ul[:, s, w],
                                                     acts.hi[:, dt, cols], acts.lo[:, dt, cols], dt == 0, dt == DT - 1)
                            ins.then_inc(hid_done, 1)

            @block.scalar
            def _(act):
                act.sem_inc(staged, BANKS)
                act.sem_inc(gelu_done, 4)
                for n in range(2):
                    act.sem_inc(sent[n], 16)
                    act.sem_inc(gelu_sent[n], 16)
                with act.Fori(0, steps) as it:
                    for g in range(PER):
                        b, r = g // 8, g % 8
                        if r == 0:
                            act.wait_ge(sent[b], 16 * it + 16)
                        act.wait_ge(bank_done, it * PER + g + 1 + SLOTS)
                        src = core.psum[:, g % BANKS, :].rearrange("p (t g j) -> p g t j", t=FOUR, j=JJ)
                        act.activation(stage[:, b, :, r * FOUR:(r + 1) * FOUR, :], src, ACT.Copy).then_inc(staged, 1)
                        if g in SPLIT:
                            s = SPLIT[g]
                            act.wait_ge(u_in[s], 16 * it + 16)
                            act.wait_ge(hid_done, it * 4 + 2 * s + 2)
                            act.activation(uh[:, s], u_raw[:, s], ACT.Copy).then_inc(u_high, 1)
                        if g in AFTER:
                            s, half = AFTER[g]
                            act.wait_ge(hid_done, it * 4 + 2 * s + half + 1 + 4)
                            if half == 0:
                                act.wait_ge(gelu_sent[s], 16 * it + 16)
                            act.activation(gelu[:, s, half * HALF:(half + 1) * HALF], hid_bank(s, half),
                                           ACT.Gelu).then_inc(gelu_done, 1)

            @block.vector
            def _(dve):
                dve.wait_ge(iota_in, 16)
                dve.sem_inc(onehots, 1)
                dve.sem_inc(bank_done, SLOTS)
                with dve.Fori(0, steps) as it:
                    dve.wait_ge(onehots, it * PER + 1)
                    dve.tensor_copy(cur[:, :, :], sel[:, :, bass.ds(it * (2 * TB), 2 * TB)]).then_inc(copied, 1)
                    dve.wait_ge(copied, it + 1)
                    for g in range(PER):
                        dve.wait_ge(bank_done, it * PER + g + 1)
                        s0, k0 = (g % SLOTS) * FOUR, g * FOUR
                        dve.tensor_tensor(onea[:, s0:s0 + FOUR, :], bc(iota[:, :], 1, [P, FOUR, N_KEYS]),
                                          bc(cur[:, 0, k0:k0 + FOUR], 2, [P, FOUR, N_KEYS]), ALU.is_equal)
                        for t in range(FOUR):
                            s, k = s0 + t, k0 + t
                            ins = dve.tensor_scalar(oneb[:, s, :], iota[:, :], cur[:, 1, k:k + 1], cur[:, 2, k:k + 1],
                                                    ALU.is_equal, ALU.mult)
                        ins.then_inc(onehots, 1)


def experts(core, acts):
    nc, a = core.nc, core.a
    with ExitStack() as ctx:
        def sb(name, *shape, dt=F32):
            return core.sb(name, list(shape), dt, ctx)

        OUTS = 2 * DT
        QW = D_MODEL // 4
        u_raw = sb("u_raw", P, 2, 2, DT * P)
        v_raw = sb("v_raw", P, 4, JJ * QW)
        gates = sb("gates_in", P, 2, TOK, JJ)
        uh, ul = sb("u_high", P, 2, DT * P, dt=F32R), sb("u_low", P, 2, DT * P, dt=F32R)
        vh, vl = sb("v_high", P, 4, JJ * QW, dt=F32R), sb("v_low", P, 4, JJ * QW, dt=F32R)
        gelu = sb("gelu_out", P, 2, TOK)
        prod = sb("gated", P, 2, TOK)
        wh, wl = sb("w_high", P, 2, JJ, TOK, dt=F32R), sb("w_low", P, 2, JJ, TOK, dt=F32R)
        u_in = [core.sem(f"u_in{n}") for n in range(2)]
        g_in = [core.sem(f"gates_in{n}") for n in range(2)]
        v_in = [core.sem(f"v_in{n}") for n in range(4)]
        h_in = [core.sem(f"hidden_in{n}") for n in range(2)]
        u_high, u_low = core.sem("u_high_done"), core.sem("u_low_done")
        v_high, v_low = core.sem("v_high_done"), core.sem("v_low_done")
        hid_done = core.sem("hidden_done")
        gelu_done = core.sem("gelu_done")
        prod_done = core.sem("gated_done")
        w_high = core.sem("w_high_done")
        w_low = core.sem("w_low_done")
        out_done = core.sem("out_done")
        out_added = core.sem("out_added")
        O2 = 2 * OUTS

        def groups(whole, loaded, before=None, after=None):
            def run(eng):
                if before:
                    before(eng)
                whole(eng, 0, 0, first=True, last=False)
                with eng.Fori(0, NH // 2 - 1) as it:
                    whole(eng, it * 2 + 1, 1, first=False, last=False)
                    whole(eng, it * 2 + 2, 0, first=False, last=False)
                whole(eng, NH - 1, 1, first=False, last=True)
                with eng.Fori(0, (NG - NH) // 2) as it:
                    loaded(eng, it * 2 + NH, 0)
                    loaded(eng, it * 2 + (NH + 1), 1)
                if after:
                    after(eng)
            return run

        def load_u(sp, g, s):
            sp.dma_start(u_raw[:, s], a["u"][bass.ds(g * JJ + 2 * s, 2)].rearrange("c p n -> p c n")).then_inc(u_in[s], 16)

        def load_gates(sp, g, par):
            sp.dma_start(gates[:, par], a["gates"][bass.ds(g, 1)].rearrange("o p t j -> p (o t) j")).then_inc(g_in[par], 16)

        def load_v(sp, g, first):
            for q in range(4):
                if not first:
                    sp.wait_ge(v_low, (g - 1) * 4 + q + 1)
                sp.dma_start(v_raw[:, q], a["v"][bass.ds(g, 1), :, q].rearrange("o p n -> p (o n)")).then_inc(v_in[q], 16)

        def sp_whole(sp, g, par, first, last):
            for s in range(2):
                if not first:
                    sp.wait_ge(u_low, (g - 1) * JJ + 2 * s + 2)
                load_u(sp, g, s)
            if not first:
                sp.wait_ge(prod_done, g * JJ - 2)
            load_gates(sp, g, par)
            load_v(sp, g, first)

        def sp_loaded(sp, g, par):
            def load_hidden(jj):
                sp.wait_ge(prod_done, g * JJ + jj + 1)
                sp.dma_start(gelu[:, jj % 2], a["hidden"][bass.ds(g * JJ + (jj - NH * JJ), 1)].rearrange(
                    "o p t -> p (o t)")).then_inc(h_in[jj % 2], 16)

            sp.wait_ge(prod_done, g * JJ - 2)
            load_gates(sp, g, par)
            load_hidden(0)
            load_hidden(1)
            load_v(sp, g, False)
            load_hidden(2)
            load_hidden(3)

        def split_u_high(act, n, g, jj):
            act.wait_ge(u_in[jj // 2], g * 16 + 16)
            act.activation(uh[:, jj % 2], u_raw[:, jj // 2, jj % 2], ACT.Copy).then_inc(u_high, 1)

        def split_v_high(act, g, q):
            act.wait_ge(v_in[q], g * 16 + 16)
            act.wait_ge(out_done, g * OUTS + 4 * q + 4 + OUTS)
            act.activation(vh[:, q], v_raw[:, q], ACT.Copy).then_inc(v_high, 1)

        def split_v_low(dve, g, q):
            dve.wait_ge(v_high, g * 4 + q + 1)
            dve.tensor_tensor(vl[:, q], v_raw[:, q], vh[:, q].bitcast(F32), ALU.subtract).then_inc(v_low, 1)

        def hidden(pe, g):
            for jj in range(JJ):
                n = g * JJ + jj
                pe.wait_ge(u_low, n + 1)
                pe.wait_ge(gelu_done, n + 1)
                for half in range(2):
                    o = core.psum[:, 2 * (jj % 2) + half, 0:HALF]
                    cols = slice(half * HALF, (half + 1) * HALF)
                    for dt in range(DT):
                        w = slice(dt * P, (dt + 1) * P)
                        ins = three_products(pe, o, uh[:, jj % 2, w], ul[:, jj % 2, w],
                                             acts.hi[:, dt, cols], acts.lo[:, dt, cols], dt == 0, dt == DT - 1)
                ins.then_inc(hid_done, 1)

        def out(pe, g, par):
            for k in range(OUTS):
                dt, half, q = k // 2, k % 2, k // 4
                if k % 4 == 0:
                    pe.wait_ge(v_low, g * 4 + q + 1)
                pe.wait_ge(out_added, g * OUTS + k + 1)
                o = core.psum[:, 4 + k % 4, 0:HALF]
                for jj in range(JJ):
                    if k == 0:
                        pe.wait_ge(w_low, g * JJ + jj + 1 + 2)
                    w = slice(jj * QW + dt % 2 * P, jj * QW + dt % 2 * P + P)
                    cols = slice(half * HALF, (half + 1) * HALF)
                    ins = three_products(pe, o, vh[:, q, w], vl[:, q, w], wh[:, par, jj, cols],
                                         wl[:, par, jj, cols], jj == 0, jj == JJ - 1)
                ins.then_inc(out_done, 1)

        def pe_whole(pe, g, par, first, last):
            hidden(pe, g)
            if not first:
                out(pe, g - 1, 1 - par)

        def pe_loaded(pe, g, par):
            out(pe, g - 1, 1 - par)

        def gated_high(act, g, par, jj):
            act.wait_ge(prod_done, g * JJ + jj + 3)
            if jj == 0:
                act.wait_ge(out_done, g * OUTS + OUTS)
            act.activation(wh[:, par, jj, :], prod[:, jj % 2, :], ACT.Copy).then_inc(w_high, 1)

        def act_whole(act, g, par, first, last):
            for jj in range(JJ):
                n = g * JJ + jj
                act.wait_ge(hid_done, n + 1)
                act.wait_ge(prod_done, n + 1)
                for half in range(2):
                    ins = act.activation(gelu[:, jj % 2, half * HALF:(half + 1) * HALF],
                                         core.psum[:, 2 * (jj % 2) + half, 0:HALF], ACT.Gelu)
                ins.then_inc(gelu_done, 1)
                if not (last and jj >= 2):
                    split_u_high(act, n + 2, g + (jj + 2) // JJ, (jj + 2) % JJ)
                gated_high(act, g, par, jj)
            for q in range(4):
                split_v_high(act, g, q)

        def act_loaded(act, g, par):
            for q in range(4):
                gated_high(act, g, par, q)
                split_v_high(act, g, q)

        def gate(dve, g, par, jj, made):
            dve.wait_ge(*made)
            if jj == 0:
                dve.wait_ge(g_in[par], 8 * (g - par) + 16)
            dve.wait_ge(w_low, g * JJ + jj + 1)
            dve.tensor_tensor(prod[:, jj % 2, :], gelu[:, jj % 2, :], gates[:, par, :, jj],
                              ALU.mult).then_inc(prod_done, 1)

        def gated_low(dve, g, par, jj):
            dve.wait_ge(w_high, g * JJ + jj + 1)
            dve.tensor_tensor(wl[:, par, jj, :], prod[:, jj % 2, :], wh[:, par, jj, :].bitcast(F32),
                              ALU.subtract).then_inc(w_low, 1)

        def dve_whole(dve, g, par, first, last):
            for jj in range(JJ):
                gate(dve, g, par, jj, (gelu_done, g * JJ + jj + 3))
                gated_low(dve, g, par, jj)
            for q in range(4):
                if not first:
                    add_out(dve, g - 1, q)
                split_v_low(dve, g, q)

        def dve_loaded(dve, g, par):
            for q in range(4):
                gate(dve, g, par, q, (h_in[q % 2], g * 32 + (16 * (q // 2 + 1) - 32 * NH)))
                add_out(dve, g - 1, q)
                gated_low(dve, g, par, q)
                split_v_low(dve, g, q)

        def add_out(dve, g, q):
            for k in range(4 * q, 4 * q + 4):
                x = acts.x[:, k // 2, (k % 2) * HALF:(k % 2 + 1) * HALF]
                dve.wait_ge(out_done, g * OUTS + k + 1 + O2)
                dve.tensor_tensor(x, core.psum[:, 4 + k % 4, 0:HALF], x, ALU.add).then_inc(out_added, 1)

        def act_before(act):
            act.sem_inc(gelu_done, 2)
            split_u_high(act, 0, 0, 0)
            split_u_high(act, 1, 0, 1)

        def dve_before(dve):
            dve.sem_inc(prod_done, 2)
            dve.sem_inc(w_low, 2)
            dve.sem_inc(out_added, 4)

        def dve_after(dve):
            for q in range(4):
                add_out(dve, NG - 1, q)

        with nc.Block() as block:
            @block.sync
            def _(sp):
                groups(sp_whole, sp_loaded)(sp)

            @block.gpsimd
            def _(pool):
                with pool.Fori(0, NH) as g:
                    for jj in range(JJ):
                        pool.wait_ge(u_high, g * JJ + jj + 1)
                        pool.tensor_tensor(ul[:, jj % 2], u_raw[:, jj // 2, jj % 2], uh[:, jj % 2].bitcast(F32),
                                           ALU.subtract).then_inc(u_low, 1)

            @block.tensor
            def _(pe):
                pe.sem_inc(out_done, O2)
                groups(pe_whole, pe_loaded)(pe)
                out(pe, NG - 1, 1)

            @block.scalar
            def _(act):
                groups(act_whole, act_loaded, act_before)(act)

            @block.vector
            def _(dve):
                groups(dve_whole, dve_loaded, dve_before, dve_after)(dve)


def finish(core, acts):
    nc, a = core.nc, core.a
    with ExitStack() as ctx:
        norm = Norm(core, ctx, "n3", acts, 2, False, 0)
        stored = core.sem("y_stored")
        with nc.Block() as block:
            @block.sync
            def _(sp):
                for dt in range(DT):
                    sp.wait_ge(norm.scaled, dt + 2)
                    sp.dma_start(a["y"][:, dt, :], norm.y[:, dt, :]).then_inc(stored, 16)
                sp.wait_ge(stored, 16 * DT)

            @block.tensor
            def _(pe):
                norm.pe_sums(pe)

            @block.scalar
            def _(act):
                norm.act_squares(act)
                norm.act_root(act)

            @block.vector
            def _(dve):
                norm.dve(dve)


def build(nc, a):
    with ExitStack() as ctx:
        core = Core(nc, ctx, a)
        project_in(core)
        mix(core)
        acts = Acts(core, ctx, "res")
        with ExitStack() as inner:
            sel = core.sb("picks_by_token", [P, 3, TOK], ctx=inner)
            project_out(core, acts)
            route(core, acts, sel)
            spread_gates(core, acts, sel)
        experts(core, acts)
        finish(core, acts)



_OUT = {
    "y": (P, DT, TOK), "shift_out": (P, RT, 2), "conv_out": (P, XT_, 2, CONV_W - 1),
    "wkv_out": (P, 2, 4, HD), "ssm_out": (P, 2, 4, HD),
}
_SCRATCH = {
    "pm": (P, RT, RWIN), "xbc": (P, XT_, XWIN), "z": (P, ZT, TOK), "dt": (8, 2, TOK), "o": (P, DT, TOK),
    "gates": (NG, P, TOK, JJ), "hidden": (AHEAD4 + AHEAD5, P, TOK),
}


def lay_out(inp):
    f = {k: np.asarray(v) for k, v in inp.items()}

    def chan(x):
        x = np.asarray(x)
        x = x.reshape(x.shape[:-1] + (x.shape[-1] // P, P))
        return np.ascontiguousarray(np.moveaxis(np.moveaxis(x, -1, 0), -1, 1))

    def weight_tiles(w):
        r, c = w.shape
        return np.ascontiguousarray(w.reshape(r // P, P, c // P, P).transpose(2, 1, 0, 3).reshape(c // P, P, r))

    def rows(x):
        return np.broadcast_to(np.asarray(x).reshape(-1), (P, np.asarray(x).size))

    x = np.concatenate([f["x_prompt"][0], f["x_sample"][0]], 0)
    w_in = f["w_in"][0]
    z0, x0, d0 = R_PROJ, R_PROJ + M_WIDTH, R_PROJ + M_WIDTH + CONV_DIM
    pad = np.zeros((D_MODEL, P - HEADS), w_in.dtype)
    w_in = np.concatenate([w_in[:, :R_PROJ], w_in[:, x0:d0], w_in[:, z0:x0], w_in[:, d0:], pad], 1)
    shift = f["state_rwkv_shift"][0, 0]
    par1 = np.concatenate([
        chan(f["rwkv_mu"][0]), chan(shift), np.zeros((P, RT), np.float32),
        chan(f["mamba_conv_w"][0]).reshape(P, -1), chan(f["mamba_conv_b"][0]),
        chan(f["state_mamba_conv"][0, 0]).reshape(P, -1)], 1)

    def pair_states(s):
        return np.ascontiguousarray(s.reshape(4, 2, HD, HD).transpose(1, 3, 0, 2).reshape(P, 4, HD))

    def group_states(s):
        return np.ascontiguousarray(s.reshape(2, 4, HD, HD).transpose(0, 3, 1, 2).reshape(P, 4, HD))

    u = f["peer_u"][0].reshape(N_KEYS, N_KEYS, DT, P).transpose(1, 3, 2, 0).reshape(N_KEYS, P, DT * P)
    v = f["peer_v"][0].reshape(N_KEYS, NG, JJ, 4, D_MODEL // 4).transpose(1, 0, 3, 2, 4).reshape(NG, P, 4, D_MODEL)
    return {
        "x": chan(x), "w_in": weight_tiles(w_in), "w_out": weight_tiles(f["w_out"][0]),
        "w_q": weight_tiles(f["peer_w_q"][0]), "consts": shape_constants(),
        "ranks": np.broadcast_to(np.arange(P, dtype=np.float32), (P, P)),
        "norms": np.stack([chan(f["norm1_w"][0]), chan(f["norm2_w"][0]), chan(f["final_norm_w"])], 1),
        "par1": par1, "dtp": np.stack([f["mamba_dt_bias"][0], f["mamba_A_log"][0]], 1),
        "rows": np.stack([rows(f[k]) for k in ("rwkv_w0", "rwkv_a0", "rwkv_k_k", "rwkv_k_a", "rwkv_r_k",
                                               "rwkv_ln_w", "rwkv_ln_b", "mamba_norm_w")], 1),
        "mamba_D": rows(f["mamba_D"]), "w2": np.concatenate([f["rwkv_w2"][0], f["rwkv_a2"][0]], 0),
        "g2": f["rwkv_g2"][0], "wkv_in": pair_states(f["state_rwkv_wkv"][0, 0]),
        "ssm_in": group_states(f["state_mamba_ssm"][0, 0]),
        "keysT": np.ascontiguousarray(f["peer_sub_keys"][0].transpose(2, 0, 1)),
        "u": u, "v": v,
    }


def kernel(**inputs):
    import concourse.bacc as bacc
    from concourse.bass_utils import run_bass_kernel_spmd

    nc = bacc.Bacc("TRN2", target_bir_lowering=False, num_devices=1)
    arrays = {"arg_" + k: np.ascontiguousarray(v) for k, v in lay_out(inputs).items()}
    a = {k[4:]: nc.dram_tensor(k, v.shape, F32, kind="ExternalInput").ap() for k, v in arrays.items()}
    a.update({k: nc.dram_tensor("out_" + k, s, F32, kind="ExternalOutput").ap() for k, s in _OUT.items()})
    a.update({k: nc.dram_tensor("scratch_" + k, s, F32, kind="Internal").ap() for k, s in _SCRATCH.items()})
    build(nc, a)
    r = run_bass_kernel_spmd(nc, [arrays], core_ids=[0]).results[0]
    y = np.asarray(r["out_y"]).transpose(2, 1, 0).reshape(TOK, D_MODEL)
    shift = np.asarray(r["out_shift_out"]).transpose(2, 1, 0).reshape(2, R_PROJ)
    conv = np.asarray(r["out_conv_out"]).transpose(2, 3, 1, 0).reshape(2, CONV_W - 1, CONV_DIM)
    wkv = np.asarray(r["out_wkv_out"]).reshape(2, HD, 2, 4, HD).transpose(2, 3, 0, 4, 1).reshape(2, HEADS, HD, HD)
    ssm = np.asarray(r["out_ssm_out"]).reshape(2, HD, 2, 4, HD).transpose(2, 0, 3, 4, 1).reshape(2, HEADS, HD, HD)
    outs = [y[None, :SEQ], y[None, SEQ:]]
    for n in range(2):
        outs += [shift[None, n:n + 1], wkv[None, n:n + 1], conv[None, n:n + 1], ssm[None, n:n + 1]]
    return tuple(np.ascontiguousarray(o) for o in outs)
```

```python
from contextlib import ExitStack

import numpy as np

import concourse.bass as bass
from concourse import mybir

F32 = mybir.dt.float32
F32R = mybir.dt.float32r
U32 = mybir.dt.uint32
ALU = mybir.AluOpType
ACT = mybir.ActivationFunctionType
AX_X = mybir.AxisListType.X

P = 128
D_MODEL = 1024
SEQ = 512
DEC_SEQ = 64
TOK = SEQ + DEC_SEQ
HALF = TOK // 2
DT = D_MODEL // P
R_WIDTH = 512
M_WIDTH = 512
HEADS = 8
HD = 64
R_PROJ = 1792
CONV_DIM = 768
CONV_W = 4
RT = R_PROJ // P
XT_ = CONV_DIM // P
ZT = M_WIDTH // P
NCT = RT + XT_ + ZT + 1
N_KEYS = 128
P_HEADS = 8
TOPK = 16
SEL = P_HEADS * TOPK
NORM_EPS = 1e-6
GN_EPS = HD * 1e-5
DECAY_SCALE = -float(np.exp(-0.5))
LOWEST = -3.0e38
RWIN = SEQ + 1 + DEC_SEQ
XWIN = SEQ + CONV_W - 1 + DEC_SEQ
TILES = [(0, P, 0, 0), (P, P, P, P), (2 * P, P, 2 * P, 2 * P), (3 * P, P, 3 * P, 3 * P),
         (SEQ, DEC_SEQ, SEQ + 1, SEQ + CONV_W - 1)]
NT = len(TILES)
LEVELS = 7
JJ = 4
NG = N_KEYS // JJ
TB = 32
G_STEPS = TOK // (2 * TB)
AHEAD5 = 2 * G_STEPS
AHEAD4 = 38
NH = NG - (AHEAD4 + AHEAD5) // JJ
KEY4, KEY5 = NH * JJ, NH * JJ + AHEAD4

C_ID, C_ONE, C_TRI, C_REV, C_DINC, C_DEXC = (P * n for n in range(6))
C_MS, C_LT0, C_LEV = (P * n for n in range(6, 9))
C_DCOL = C_LEV + P * LEVELS
C_N = C_DCOL + 2


def shape_constants():
    c = np.zeros((P, C_N), np.float32)
    s = np.arange(P)[:, None]
    t = np.arange(P)[None, :]
    c[:, C_ID:C_ID + P] = s == t
    c[:, C_ONE:C_ONE + P] = 1
    c[:, C_TRI:C_TRI + P] = s <= t
    c[:, C_REV:C_REV + P] = s > t
    mid = (s <= HD - 1)
    c[:, C_DINC:C_DINC + P] = DECAY_SCALE * ((s <= t).astype(np.float32) - mid)
    c[:, C_DEXC:C_DEXC + P] = DECAY_SCALE * ((s < t).astype(np.float32) - mid)
    c[:, C_MS:C_MS + P] = s < t
    for n in range(LEVELS):
        b = 1 << n
        m = ((s // (2 * b) == t // (2 * b)) & (s // b > t // b)) | (s == t)
        c[:, C_LEV + P * n:C_LEV + P * (n + 1)] = m if n else m & (s != t)
        if n == 0:
            c[:, C_LT0:C_LT0 + P] = m.T
    c[:, C_DCOL] = DECAY_SCALE * mid[:, 0]
    c[:, C_DCOL + 1] = DECAY_SCALE * (~mid[:, 0])
    return c


def bc(ap, axis, shape):
    return ap.unsqueeze(axis).broadcast_to(shape)


def three_products(pe, out, ah, al, bh, bl, first, last):
    pe.matmul(out, ah, bh, start=first, stop=False)
    pe.matmul(out, ah, bl, start=False, stop=False)
    return pe.matmul(out, al, bh, start=False, stop=last)


class Acts:

    def __init__(self, core, ctx, name, x=None):
        self.x = core.sb(name + "_x", [P, DT, TOK], ctx=ctx) if x is None else x
        self.hi = core.sb(name + "_hi", [P, DT, TOK], F32R, ctx=ctx)
        self.lo = core.sb(name + "_lo", [P, DT, TOK], F32R, ctx=ctx)


class Core:

    def __init__(self, nc, ctx, a):
        self.nc, self.ctx, self.a = nc, ctx, a
        self.psum = ctx.enter_context(nc.psum_tensor("banks", [P, 8, 512], F32))
        self.ident = self.sb("ident", [P, P])
        self.ones = self.sb("ones", [P, P])
        self.norms = self.sb("norms", [P, 3, DT])
        self.norm_sems = [self.sem("norm_" + n) for n in
                          ("squared", "summed", "meaned", "rooted", "scaled", "high", "low")]
        self.chains = {name: Chain(self.sem(name + "_chain")) for name in ("pe", "act", "pool", "dve")}

    def sb(self, name, shape, dt=F32, ctx=None):
        return (ctx or self.ctx).enter_context(self.nc.sbuf_tensor(name, shape, dt))

    def sem(self, name):
        return self.ctx.enter_context(self.nc.semaphore(name))

    def bank(self, n):
        return self.psum[:, n % 8, :]


class Chain:

    def __init__(self, sem):
        self.sem, self.n = sem, 0

    def on(self, eng):
        self.eng = eng
        return self

    def __call__(self, ins):
        ins.then_inc(self.sem, 1)
        self.n += 1
        self.eng.wait_ge(self.sem, self.n)


class Gemm:

    def __init__(self, core, ctx, name, acts, count, dram, banks=(0, 1, 2, 3)):
        self.acts = acts
        self.core, self.count, self.dram, self.banks = core, count, dram, banks
        self.raw = core.sb(name + "_raw", [P, 3, DT * P], ctx=ctx)
        self.wh = core.sb(name + "_wh", [P, 2, DT * P], F32R, ctx=ctx)
        self.wl = core.sb(name + "_wl", [P, 2, DT * P], F32R, ctx=ctx)
        self.loaded = [core.sem(f"{name}_loaded{n}") for n in range(3)]
        self.high = core.sem(name + "_high")
        self.low = core.sem(name + "_low")
        self.done = core.sem(name + "_done")
        self.taken = core.sem(name + "_taken")

    def load(self, sp, c):
        if c >= 3:
            sp.wait_ge(self.low, c - 2)
        sp.dma_start(self.raw[:, c % 3, :], self.dram[c]).then_inc(self.loaded[c % 3], 16)

    def split_high(self, act, c):
        act.wait_ge(self.loaded[c % 3], 16 * (c // 3 + 1))
        if c >= 2:
            act.wait_ge(self.done, c - 1)
        act.activation(self.wh[:, c % 2, :], self.raw[:, c % 3, :], ACT.Copy).then_inc(self.high, 1)

    def split_low(self, pool, c):
        pool.wait_ge(self.high, c + 1)
        pool.tensor_tensor(self.wl[:, c % 2, :], self.raw[:, c % 3, :],
                           self.wh[:, c % 2, :].bitcast(F32), ALU.subtract).then_inc(self.low, 1)

    def multiply(self, pe, c, ready=None):
        pe.wait_ge(self.low, c + 1)
        if c >= 2:
            pe.wait_ge(self.taken, c - 1)
        halves, dts = range(2), range(DT)
        order = [(half, dt) for half in halves for dt in dts] if ready is None else [
            (half, dt) for dt in dts for half in halves]
        for half, dt in order:
            if ready is not None and half == 0:
                pe.wait_ge(ready[0], ready[1] + dt + 1)
            cols, w = slice(half * HALF, (half + 1) * HALF), slice(dt * P, (dt + 1) * P)
            ins = three_products(pe, self.out(c, half), self.wh[:, c % 2, w], self.wl[:, c % 2, w],
                                 self.acts.hi[:, dt, cols], self.acts.lo[:, dt, cols], dt == 0, dt == DT - 1)
        ins.then_inc(self.done, 1)

    def out(self, c, half):
        return self.core.psum[:, self.banks[2 * (c % 2) + half], 0:HALF]


class Norm:

    def __init__(self, core, ctx, name, acts, which, halves, bank, sq=None):
        self.acts = acts
        self.core, self.which, self.halves, self.b = core, which, halves, bank
        self.sq = core.sb(name + "_sq", [P, 2, TOK], ctx=ctx) if sq is None else sq
        self.ctx, self.name = ctx, name
        self.ny = 2 if halves else DT
        if halves:
            self.make_room()

        self.squared, self.summed, self.meaned, self.rooted, self.scaled, self.high, self.low = core.norm_sems
        self.b8, self.b9 = which * DT, which * (DT + 1)

    def make_room(self):
        core, ctx, name = self.core, self.ctx, self.name
        self.mean = core.sb(name + "_mean", [P, TOK], ctx=ctx)
        self.root = core.sb(name + "_root", [P, TOK], ctx=ctx)
        self.inv = core.sb(name + "_inv", [P, TOK], ctx=ctx)
        self.y = core.sb(name + "_y", [P, self.ny, TOK], ctx=ctx)

    def act_squares(self, act, ready=None):
        for dt in range(DT):
            if ready is not None:
                act.wait_ge(*ready(dt))
            if dt >= 2:
                act.wait_ge(self.summed, self.b8 + dt - 1)
            act.activation(self.sq[:, dt % 2, :], self.acts.x[:, dt, :], ACT.Square).then_inc(self.squared, 1)

    def pe_sums(self, pe):
        for dt in range(DT):
            pe.wait_ge(self.squared, self.b8 + dt + 1)
            for half in range(2):
                ins = pe.matmul(self.core.psum[:, self.b + half, 0:HALF], self.core.ones[:, :],
                                self.sq[:, dt % 2, half * HALF:(half + 1) * HALF],
                                start=dt == 0, stop=dt == DT - 1)
            ins.then_inc(self.summed, 1)

    def act_root(self, act):
        act.wait_ge(self.meaned, 2 * (self.which + 1))
        act.activation(self.root[:, :], self.mean[:, :], ACT.Sqrt).then_inc(self.rooted, 1)

    def act_high(self, act):
        for dt in range(DT):
            act.wait_ge(self.scaled, self.b9 + dt + 2)
            act.activation(self.acts.hi[:, dt, :], self.y[:, dt % 2, :], ACT.Copy).then_inc(self.high, 1)

    def dve(self, dve):
        dve.wait_ge(self.summed, self.b8 + DT)
        for half in range(2):
            cols = slice(half * HALF, (half + 1) * HALF)
            dve.tensor_scalar(self.mean[:, cols], self.core.psum[:, self.b + half, 0:HALF],
                              1.0 / D_MODEL, NORM_EPS, ALU.mult, ALU.add).then_inc(self.meaned, 1)
        dve.wait_ge(self.rooted, self.which + 1)
        dve.reciprocal(self.inv[:, :], self.root[:, :]).then_inc(self.scaled, 1)
        dve.wait_ge(self.scaled, self.b9 + 1)
        for dt in range(DT + 1):
            if dt < DT:
                if dt >= self.ny:
                    dve.wait_ge(self.low, self.b8 + dt - 1)
                dve.scalar_tensor_tensor(out=self.y[:, dt % self.ny, :], in0=self.acts.x[:, dt, :],
                                         scalar=self.core.norms[:, self.which, dt:dt + 1],
                                         in1=self.inv[:, :], op0=ALU.mult, op1=ALU.mult).then_inc(self.scaled, 1)
            if self.halves and dt:
                dve.wait_ge(self.high, self.b8 + dt)
                dve.tensor_tensor(self.acts.lo[:, dt - 1, :], self.y[:, (dt - 1) % 2, :],
                                  self.acts.hi[:, dt - 1, :].bitcast(F32), ALU.subtract).then_inc(self.low, 1)


class MixParams:

    def __init__(self, core, ctx):
        self.cst = core.sb("shape_constants", [P, C_N], ctx=ctx)
        self.rows = core.sb("param_rows", [P, 8, R_WIDTH], ctx=ctx)
        self.heads_row = core.sb("mamba_D", [P, HEADS], ctx=ctx)
        self.w2 = core.sb("w2", [P, R_WIDTH], ctx=ctx)
        self.g2 = core.sb("g2", [P, R_WIDTH], ctx=ctx)
        self.loaded = core.sem("mix_params_in")

    def load(self, sp, a):
        for dst, src in ((self.cst[:, :], a["consts"]), (self.rows[:, :, :], a["rows"]),
                         (self.heads_row[:, :], a["mamba_D"]), (self.w2[:, :], a["w2"]), (self.g2[:, :], a["g2"])):
            sp.dma_start(dst, src).then_inc(self.loaded, 16)


def project_in(core, following):
    nc, a = core.nc, core.a
    with ExitStack() as ctx:
        acts = Acts(core, ctx, "in")
        norm = Norm(core, ctx, "n1", acts, 0, True, 4)
        gemm = Gemm(core, ctx, "in", acts, NCT, a["w_in"])
        out = core.sb("row_out", [P, 3, XWIN], ctx=ctx)
        pr = core.sb("pr", [P, 2, RWIN + 1], ctx=ctx)
        px = core.sb("px", [P, 2, XWIN + CONV_W - 1], ctx=ctx)
        tmp = core.sb("tmp1", [P, 2, XWIN], ctx=ctx)
        par = core.sb("par1", [P, 3 * RT + XT_ * (CONV_W + 1 + CONV_W - 1)], ctx=ctx)
        mu, shift_in, = par[:, 0:RT], par[:, RT:2 * RT]
        cw = par[:, 3 * RT:3 * RT + XT_ * CONV_W].rearrange("p (x k) -> p x k", k=CONV_W)
        cb = par[:, 3 * RT + XT_ * CONV_W:3 * RT + XT_ * (CONV_W + 1)]
        cst = par[:, 3 * RT + XT_ * (CONV_W + 1):].rearrange("p (x k) -> p x k", k=CONV_W - 1)
        shift_out = core.sb("shift_out", [P, RT, 2], ctx=ctx)
        conv_out = core.sb("conv_out", [P, XT_, 2, CONV_W - 1], ctx=ctx)
        dtp = core.sb("dtp", [8, 4], ctx=ctx)
        dts = core.sb("dts", [8, 3, TOK], ctx=ctx)
        dto = core.sb("dt_out", [8, 2, TOK], ctx=ctx)
        x_in = [core.sem(f"x_in{n}") for n in range(4)]
        ones_in, norms_in = core.sem("ones_in"), core.sem("norms_in")
        par_in = core.sem("par_in")
        zeroed = core.sem("pads_zeroed")
        mixed = core.sem("row_mixed")
        conved = core.sem("row_conved")
        tails = core.sem("tails_copied")
        silued = core.sem("row_silued")
        dtc = core.sem("dt_act")
        dtv = core.sem("dt_dve")
        stored = core.sem("tails_stored")
        sent = [core.sem(f"row_sent{n}") for n in range(3)]

        with nc.Block() as block:
            @block.sync
            def _(sp):
                for n in range(4):
                    sp.dma_start(acts.x[:, 2 * n:2 * n + 2, :], a["x"][:, 2 * n:2 * n + 2]).then_inc(x_in[n], 16)
                    if n == 0:
                        sp.dma_start(core.ones[:, :], a["consts"][:, C_ONE:C_ONE + P]).then_inc(ones_in, 16)
                sp.dma_start(core.norms[:, :, :], a["norms"]).then_inc(norms_in, 16)
                for c in range(3):
                    gemm.load(sp, c)
                sp.dma_start(core.ident[:, :], a["consts"][:, C_ID:C_ID + P]).then_inc(par_in, 16)
                sp.dma_start(par[:, :], a["par1"]).then_inc(par_in, 16)
                sp.dma_start(dtp[:, 0:2], a["dtp"]).then_inc(par_in, 16)
                for c in range(NCT - 1):
                    if c + 3 < NCT:
                        gemm.load(sp, c + 3)
                    if c == 2:
                        following.load(sp, a)
                    if c < RT:
                        sp.wait_ge(mixed, c + 1)
                        dst = a["pm"][:, c, :]
                    elif c < RT + XT_:
                        sp.wait_ge(silued, c - RT + 1)
                        dst = a["xbc"][:, c - RT, :]
                    else:
                        sp.wait_ge(gemm.taken, c + 1)
                        dst = a["z"][:, c - RT - XT_, :]
                    sp.dma_start(dst, out[:, c % 3, 0:dst.shape[1]]).then_inc(sent[c % 3], 16)
                sp.wait_ge(dtv, 1)
                sp.dma_start(a["dt"], dto[:, :, :]).then_inc(stored, 16)
                sp.wait_ge(tails, RT + XT_)
                sp.wait_ge(mixed, RT + XT_)
                sp.dma_start(a["shift_out"], shift_out[:, :, :]).then_inc(stored, 16)
                sp.dma_start(a["conv_out"], conv_out[:, :, :, :]).then_inc(stored, 16)
                sp.wait_ge(stored, 48)
                for n in range(3):
                    sp.wait_ge(sent[n], 16 * ((NCT - 1) // 3))

            @block.gpsimd
            def _(pool):
                pool.memset(pr[:, :, 0:1], 0.0).then_inc(zeroed, 1)
                pool.memset(px[:, :, 0:CONV_W - 1], 0.0).then_inc(zeroed, 1)
                for c in range(NCT):
                    gemm.split_low(pool, c)

            @block.tensor
            def _(pe):
                pe.wait_ge(ones_in, 16)
                norm.pe_sums(pe)
                for c in range(NCT):
                    gemm.multiply(pe, c, ready=(norm.low, norm.b8) if c == 0 else None)

            @block.scalar
            def _(act):
                link = core.chains["act"].on(act)
                norm.act_squares(act, ready=lambda dt: (x_in[dt // 2], 16))
                norm.act_root(act)
                gemm.split_high(act, 0)
                gemm.split_high(act, 1)
                norm.act_high(act)
                act.wait_ge(par_in, 48)
                act.wait_ge(zeroed, 2)

                def row_free(c):
                    if c >= 3:
                        act.wait_ge(sent[c % 3], 16 * (c // 3))

                link(act.activation(dtp[:, 2:3], dtp[:, 1:2], ACT.Exp))

                def silu(x):
                    act.wait_ge(conved, x + 1)
                    row_free(RT + x)
                    act.activation(out[:, (RT + x) % 3, :], tmp[:, 1, :], ACT.Silu, bias=cb[:, x:x + 1]).then_inc(silued, 1)

                for c in range(NCT):
                    act.wait_ge(gemm.done, c + 1)
                    a0, a1 = gemm.out(c, 0), gemm.out(c, 1)
                    n1 = SEQ - HALF
                    if c < RT:
                        if c >= 2:
                            act.wait_ge(mixed, c - 1)
                        row = pr[:, c % 2, :]
                        act.activation(row[:, SEQ + 1:SEQ + 2], shift_in[:, c:c + 1], ACT.Copy)
                        act.activation(row[:, 1:1 + HALF], a0, ACT.Copy)
                        act.activation(row[:, 1 + HALF:1 + SEQ], a1[:, 0:n1], ACT.Copy)
                        act.activation(row[:, SEQ + 2:], a1[:, n1:], ACT.Copy).then_inc(gemm.taken, 1)
                    elif c < RT + XT_:
                        x = c - RT
                        if x >= 2:
                            act.wait_ge(mixed, c - 1)
                        row = px[:, x % 2, :]
                        g = CONV_W - 1
                        act.activation(row[:, g + SEQ:g + SEQ + g], cst[:, x, :], ACT.Copy)
                        act.activation(row[:, g:g + HALF], a0, ACT.Copy)
                        act.activation(row[:, g + HALF:g + SEQ], a1[:, 0:n1], ACT.Copy)
                        act.activation(row[:, g + SEQ + g:], a1[:, n1:], ACT.Copy).then_inc(gemm.taken, 1)
                        if x >= 1:
                            silu(x - 1)
                    elif c < RT + XT_ + ZT:
                        if c == RT + XT_:
                            silu(XT_ - 1)
                        row_free(c)
                        act.activation(out[:, c % 3, 0:HALF], a0, ACT.Silu)
                        act.activation(out[:, c % 3, HALF:TOK], a1, ACT.Silu).then_inc(gemm.taken, 1)
                    else:
                        act.activation(dts[:, 0, 0:HALF], a0[0:8, :], ACT.Identity, bias=dtp[:, 0:1]).then_inc(dtc, 1)
                        act.activation(dts[:, 0, HALF:], a1[0:8, :], ACT.Identity, bias=dtp[:, 0:1]).then_inc(gemm.taken, 1)
                        act.wait_ge(gemm.taken, NCT)
                        link(act.activation(dts[:, 1, :], dts[:, 0, :], ACT.Abs))
                        link(act.activation(dts[:, 2, :], dts[:, 1, :], ACT.Exp, scale=-1.0))
                        act.activation(dts[:, 1, :], dts[:, 2, :], ACT.Ln, bias=1.0).then_inc(dtc, 1)
                    if c + 2 < NCT:
                        gemm.split_high(act, c + 2)

            @block.vector
            def _(dve):
                link = core.chains["dve"].on(dve)
                dve.wait_ge(norms_in, 16)
                norm.dve(dve)
                dve.wait_ge(par_in, 48)
                dve.wait_ge(zeroed, 2)
                for c in range(RT):
                    dve.wait_ge(gemm.taken, c + 1)
                    row = pr[:, c % 2, :]
                    link(dve.tensor_tensor(tmp[:, 0, 0:RWIN], row[:, 0:RWIN], row[:, 1:], ALU.subtract))
                    dve.tensor_copy(shift_out[:, c, :], row[:, SEQ:SEQ + 2 + DEC_SEQ:DEC_SEQ + 1]).then_inc(tails, 1)
                    if c >= 3:
                        dve.wait_ge(sent[c % 3], 16 * (c // 3))
                    dve.scalar_tensor_tensor(out=out[:, c % 3, 0:RWIN], in0=tmp[:, 0, 0:RWIN], scalar=mu[:, c:c + 1],
                                             in1=row[:, 1:], op0=ALU.mult, op1=ALU.add).then_inc(mixed, 1)
                    dve.wait_ge(mixed, c + 1)
                for x in range(XT_):
                    c = RT + x
                    dve.wait_ge(gemm.taken, c + 1)
                    row = px[:, x % 2, :]
                    dve.tensor_copy(conv_out[:, x, 0, :], row[:, SEQ:SEQ + CONV_W - 1]).then_inc(tails, 1)
                    link(dve.tensor_scalar(tmp[:, 0, :], row[:, 0:XWIN], cw[:, x, 0:1], None, ALU.mult))
                    if x >= 1:
                        dve.wait_ge(silued, x)
                    link(dve.scalar_tensor_tensor(out=tmp[:, 1, :], in0=row[:, 1:1 + XWIN], scalar=cw[:, x, 1:2],
                                                  in1=tmp[:, 0, :], op0=ALU.mult, op1=ALU.add))
                    link(dve.scalar_tensor_tensor(out=tmp[:, 0, :], in0=row[:, 2:2 + XWIN], scalar=cw[:, x, 2:3],
                                                  in1=tmp[:, 1, :], op0=ALU.mult, op1=ALU.add))
                    dve.scalar_tensor_tensor(out=tmp[:, 1, :], in0=row[:, 3:3 + XWIN], scalar=cw[:, x, 3:4],
                                             in1=tmp[:, 0, :], op0=ALU.mult, op1=ALU.add).then_inc(conved, 1)
                    dve.wait_ge(conved, x + 1)
                    dve.tensor_copy(conv_out[:, x, 1, :], row[:, XWIN:XWIN + CONV_W - 1]).then_inc(mixed, 1)
                dve.wait_ge(mixed, RT + XT_)
                dve.wait_ge(dtc, 2)
                link(dve.tensor_scalar(dts[:, 0, :], dts[:, 0, :], 0.0, None, ALU.max))
                link(dve.tensor_tensor(dto[:, 0, :], dts[:, 0, :], dts[:, 1, :], ALU.add))
                dve.tensor_scalar(dto[:, 1, :], dto[:, 0, :], dtp[:, 2:3], -1.0, ALU.mult, ALU.mult).then_inc(dtv, 1)


def tile_parts():
    parts = [(name, 0) for name in ("A1", "A2", "A2b", "A3", "A4", "A5")]
    between = {1: ("C1", "Y1", "A1"), 2: ("C2", "A2", "Y2", "A2b"), 3: ("C3", "A3", "Y3"), 4: ("A4", "C4"), 5: ("A5",)}
    for i in range(NT):
        parts.append(("B1", i))
        for n in range(1, last_level(i) + 1):
            parts.append((f"L{n}", i))
            for name in between.get(n, ()):
                j = i + {"A": 1, "Y": 0, "C": -1}[name[0]]
                if 0 <= j < NT:
                    parts.append((name, j))
        parts.append(("B5", i))
    return parts + [(f"C{n}", NT - 1) for n in range(1, 5)]


def last_level(i):
    return LEVELS - 1 if TILES[i][1] == P else LEVELS - 2


def mixer_jobs():
    jobs = []
    for part, i in tile_parts():
        one = {
            "A1": [("k", "act"), ("w", "dve"), ("a", "dve"), ("r", "act"), ("v", "act"), ("g", "act"),
                   ("mb", "act"), ("mx", "act"), ("mz", "act")],
            "A2": [("cinc", "act"), ("cexc", "act"), ("dec", "act"), ("cs", "dve"), ("cb0", "dve"), ("cb1", "dve")],
            "A4": [("cst0", "dve"), ("cst1", "dve")],
            "B1": [("bT", "act"), ("kT", "act"), ("aT", "act"), ("rT", "act")]
                  + [(f"{name}{e}", "dve") for name in ("ab", "m") for e in range(2)]
                  + [(f"{name}{e}", "dve") for e in range(2) for name in ("ak", "rb")]
                  + [("rk0", "act"), ("rk1", "act")],
            "B5": [("y0", "act"), ("y1", "act"), ("om", "act"), ("u0", "act"), ("u1", "act"), ("o0", "act"),
                   ("o1", "act"), ("s", "dve")],
            "C4": [("or", "act")],
        }.get(part, [])
        if part[0] == "L":
            n = int(part[1])
            one = [(f"q{n}{e}", "dve") for e in range(2)]
            for e in range(2):
                one += [(f"x{n}{e}", "act")] * (n < last_level(i)) + [(f"t{n}{e}", "act")]
            one += {1: [("yo0", "dve"), ("yo1", "dve")], 2: [("yd", "dve")], 3: [("st", "dve")]}.get(n, [])
        jobs += [(name, i, taker) for name, taker in one]
    return jobs


class Banks:

    def __init__(self, core, jobs):
        self.core = core
        self.done = core.sem("banks_done")
        self.taken = {"act": core.sem("banks_taken_act"), "dve": core.sem("banks_taken_dve")}
        self.number, self.order, count = {}, [], {"act": 0, "dve": 0}
        for n, (name, i, taker) in enumerate(jobs):
            count[taker] += 1
            self.number[name, i] = n
            self.order.append((self.taken[taker], count[taker]))

    def start(self, pe, name, i):
        n = self.number[name, i]
        if n >= 8:
            pe.wait_ge(*self.order[n - 8])
        return self.core.bank(n)

    def finish(self, ins):
        ins.then_inc(self.done, 1)

    def get(self, eng, name, i):
        n = self.number[name, i]
        eng.wait_ge(self.done, n + 1)
        return self.core.bank(n)

    def took(self, ins, name, i):
        ins.then_inc(self.order[self.number[name, i]][0], 1)

    def wait_taken(self, eng, name, i):
        eng.wait_ge(*self.order[self.number[name, i]])


def mix(core, params, om):
    nc, a = core.nc, core.a
    with ExitStack() as ctx:
        def sb(name, *shape, dt=F32):
            return core.sb(name, list(shape), dt, ctx)

        cst, rows, heads_row, w2, g2 = params.cst, params.rows, params.heads_row, params.w2, params.g2
        kt, rt = (sb(n, P, HEADS, HD) for n in ("k_tok", "r_tok"))
        vt2, gt3 = sb("v_tok", P, 2, HEADS, HD), sb("g_tok", P, 3, HEADS, HD)
        wa = sb("wa_sigmoid", P, 2, R_WIDTH)
        einc, eneg, eexc = (sb(n, P, HEADS, HD) for n in ("e_inc", "e_neg", "e_exc"))
        dec2 = sb("decay_cols", P, 2, 4, 2)
        kk, km = sb("kk", P, HEADS, HD), sb("k_mod", P, HEADS, HD)
        bh2, kh2 = (sb(n, P, 2, R_WIDTH) for n in ("b_hat", "k_hat"))
        ah, rh = (sb(n, P, R_WIDTH) for n in ("a_hat", "r_hat"))
        bT, kT, aT, rT = (sb(n, P, 4, P) for n in ("b_hatT", "k_hatT", "a_hatT", "r_hatT"))
        mT, ak, rb, rk = (sb(n, P, 2, 4, P) for n in ("mT", "akT", "rbT", "rkT"))
        xx, xt = sb("inv", P, 2, 4, P), sb("invT", P, 2, 4, P)
        pq = sb("level", P, 2, 4, P)
        s0m = sb("s_mid", P, 4, HD)
        st = sb("wkv_states", P, 5, 4, HD)
        ys, us = sb("y_sol", P, 2, 4, HD), sb("u_sol", P, 2, 4, HD)
        os_ = sb("o_tok", P, HEADS, HD)
        t0, t1, t4 = (sb(n, P, HEADS, HD) for n in ("tmp_a", "bonus_prod", "bonus_v"))
        small, small_b = sb("small", P, 4, HEADS), sb("small_b", P, 8, HEADS)
        bonus2 = sb("bonus", P, 2, HEADS)
        mxt2, mzt2 = sb("mx_tok", P, 2, HEADS, HD), sb("mz_tok", P, 2, HEADS, HD)
        mbt2 = sb("mb_tok", P, 2, P + 2 * HEADS)
        dab = sb("dA_rows", P, HEADS, P)
        cb = sb("cb_masked", P, 2, P)
        csv = sb("cs_cols", P, 2, HEADS)
        ecs2 = sb("cs_exp", P, 2, 2, HEADS)
        hdec2 = sb("h_decay", P, 2, 4)
        seg2 = sb("segments", P, 2, HEADS, P)
        xdt2, xw2 = sb("xdt", P, 2, HEADS, HD), sb("xw", P, 2, HEADS, HD)
        ht = sb("ssm_states", P, 5, 4, HD)
        ym, t2 = sb("y_mamba", P, HEADS, HD), sb("tmp_c", P, HEADS, HD)
        t5 = sb("state_tmp", P, 4, HD)
        msmall = sb("msmall", P, 4, HEADS)

        pm_in, xbc_in = sb("pm_in", P, 2, RT, P), sb("xbc_in", P, 2, XT_, P)
        z_in, dt_in = sb("z_in", P, 2, ZT, P), sb("dt_in", 8, 2, 2, P)
        b = Banks(core, mixer_jobs())
        rows_in = [core.sem(f"tile_rows_in{n}") for n in range(2)]
        inner = core.sem("inner_acts")
        par_in = params.loaded
        zeroed = core.sem("states_zeroed")
        tanhs = core.sem("wa_sigmoids")
        states = core.sem("states_ready")
        hats = core.sem("hats")
        mt_rdy = core.sem("mT_ready")
        x_rdy, xt_rdy = core.sem("inv_first"), core.sem("invT_first")
        s0_rdy = core.sem("s_mid_ready")
        exps = core.sem("exps_ready")
        dab_rdy = core.sem("dA_rows_ready")
        seg_exp = core.sem("segments_exp")
        l_rdy = core.sem("weights_ready")
        cse = core.sem("cs_exps")
        xdt_rdy = core.sem("xdt_ready")
        rk_rdy = core.sem("rkT_ready")
        kmod = core.sem("k_mod_ready")
        knorm_in, knorm = core.sem("key_norm_arg"), core.sem("key_norm")
        mnorm_in, mnorm = core.sem("mamba_norm_arg"), core.sem("mamba_norm")
        gnorm_in, gnorm = core.sem("group_norm_arg"), core.sem("group_norm")
        bonus_sum = core.sem("bonus_summed")
        ksq = core.sem("key_squared")
        skip = core.sem("skip_ready")
        ysq = core.sem("mamba_squared")
        om_rdy, or_rdy = core.sem("mamba_out_ready"), core.sem("rwkv_out_ready")
        bonus, bonus_v = core.sem("bonus_products"), core.sem("bonus_times_v")
        yinv, ginv = core.sem("mamba_inverse_root"), core.sem("group_inverse_root")
        stored = core.sem("states_stored")
        into = [1, 0, 1, 2, 4]
        frm = [0, 1, 0, 1, 3]

        def b_over(eng, i):
            b.wait_taken(eng, "s", i)
            b.wait_taken(eng, "om", i)
            eng.wait_ge(states, i + 1)
            eng.wait_ge(bonus_v, i + 1)

        def a_over(eng, i):
            eng.wait_ge(hats, 4 * (i + 1))
            eng.wait_ge(l_rdy, 2 * (i + 1))
            eng.wait_ge(xdt_rdy, 2 * (i + 1))
            eng.wait_ge(bonus_sum, i + 1)

        def a_fence(eng, i):
            if i:
                a_over(eng, i - 1)
            if i >= 2:
                b_over(eng, i - 2)
            if i >= 3:
                b.wait_taken(eng, "or", i - 3)

        def b_fence(eng, i):
            if i:
                b_over(eng, i - 1)

        def run_parts(parts):
            for part, i in tile_parts():
                if part in parts:
                    parts[part](i, *TILES[i])

        def scale_outputs(eng, link, i, T):
            ln_w, ln_b = (rows[0:T, n, :].rearrange("p (h d) -> p h d", d=HD) for n in (5, 6))
            o = os_[0:T]
            eng.wait_ge(ginv, i + 1)
            eng.wait_ge(bonus_v, i + 1)
            link(eng.tensor_tensor(o, o, bc(small_b[0:T, 6, :], 2, [T, HEADS, HD]), ALU.mult))
            link(eng.tensor_tensor(o, o, ln_w, ALU.mult))
            link(eng.tensor_tensor(o, o, ln_b, ALU.add))
            link(eng.tensor_tensor(o, o, t4[0:T], ALU.add))
            eng.tensor_tensor(o, o, gt3[0:T, i % 3], ALU.mult).then_inc(or_rdy, 1)

        with nc.Block() as block:
            @block.sync
            def _(sp):
                def load(i):
                    tok, T, rc, xc = TILES[i]
                    for dst, src in ((pm_in[:, i % 2, :, 0:T], a["pm"][:, :, rc:rc + T]),
                                     (xbc_in[:, i % 2, :, 0:T], a["xbc"][:, :, xc:xc + T]),
                                     (z_in[:, i % 2, :, 0:T], a["z"][:, :, tok:tok + T]),
                                     (dt_in[:, i % 2, :, 0:T], a["dt"][:, :, tok:tok + T])):
                        sp.dma_start(dst, src).then_inc(rows_in[i % 2], 16)

                load(0)
                sp.dma_start(st[:, 3, :, :], a["wkv_in"]).then_inc(par_in, 16)
                sp.dma_start(ht[:, 3, :, :], a["ssm_in"]).then_inc(par_in, 16)
                load(1)
                for i, (tok, T, rc, xc) in enumerate(TILES):
                    b_over(sp, i)
                    if i + 2 < NT:
                        load(i + 2)
                sp.dma_start(a["wkv_out"][:, 0], st[:, 2, :, :]).then_inc(stored, 16)
                sp.dma_start(a["ssm_out"][:, 0], ht[:, 2, :, :]).then_inc(stored, 16)
                sp.dma_start(a["wkv_out"][:, 1], st[:, 4, :, :]).then_inc(stored, 16)
                sp.dma_start(a["ssm_out"][:, 1], ht[:, 4, :, :]).then_inc(stored, 16)
                sp.wait_ge(stored, 64)

            @block.tensor
            def _(pe):
                pe.wait_ge(par_in, 7 * 16)
                pe.wait_ge(zeroed, 2)
                ident = core.ident
                link = core.chains["pe"].on(pe)

                def apart(ins, e, T):
                    if T < P and e == 1:
                        link(ins)

                def rows_of(i, T):
                    return (x[:, i % 2, :, 0:T] for x in (pm_in, xbc_in, z_in, dt_in))

                def turned(name, i, T, srcs):
                    o = b.start(pe, name, i)
                    for n, src in enumerate(srcs):
                        ins = pe.transpose(o[0:T, n * P:n * P + src.shape[0]], src,
                                           ident[0:src.shape[0], 0:src.shape[0]])
                    b.finish(ins)

                def four(name, i, T, lhs, rhs):
                    o = b.start(pe, name, i)
                    for q in range(4):
                        ins = pe.matmul(o[0:T, q * T:(q + 1) * T], lhs(q), rhs(q), start=True, stop=True)
                    b.finish(ins)

                def a1(i, tok, T, rc, xc):
                    a_fence(pe, i)
                    pmi, xbi, zi, dti = rows_of(i, T)
                    pe.wait_ge(rows_in[i % 2], 64 * (i // 2 + 1))
                    turned("k", i, T, [pmi[:, 4 + n] for n in range(4)])
                    pe.wait_ge(inner, 2 * (i + 1))
                    for name, lhs, rhs in (("w", pmi[0:HD, RT - 2], w2[0:HD, :]), ("a", pmi[HD:P, RT - 2], w2[HD:P, :])):
                        o = b.start(pe, name, i)
                        b.finish(pe.matmul(o[0:T, :], lhs, rhs, start=True, stop=True))
                    turned("r", i, T, [pmi[:, n] for n in range(4)])
                    turned("v", i, T, [pmi[:, 8 + n] for n in range(4)])
                    o = b.start(pe, "g", i)
                    b.finish(pe.matmul(o[0:T, :], pmi[:, RT - 1], g2[:, :], start=True, stop=True))
                    o = b.start(pe, "mb", i)
                    pe.transpose(o[0:T, 0:P], xbi[:, 4], ident[:, :])
                    pe.transpose(o[0:T, P:P + 8], dti[:, 0], ident[0:8, 0:8])
                    b.finish(pe.transpose(o[0:T, P + 8:P + 16], dti[:, 1], ident[0:8, 0:8]))
                    turned("mx", i, T, [xbi[:, n] for n in range(4)])
                    turned("mz", i, T, [zi[:, n] for n in range(4)])

                def a2(i, tok, T, rc, xc):
                    pmi, xbi, zi, dti = rows_of(i, T)
                    mbt = mbt2[:, i % 2]
                    pe.wait_ge(tanhs, 2 * (i + 1))
                    for name, m in (("cinc", C_DINC), ("cexc", C_DEXC)):
                        o = b.start(pe, name, i)
                        b.finish(pe.matmul(o[0:T, :], cst[0:T, m:m + T], wa[0:T, 0, :], start=True, stop=True))
                    o = b.start(pe, "dec", i)
                    for n in range(4):
                        ins = pe.matmul(o[:, 2 * n:2 * n + 2], wa[0:T, 0, n * P:(n + 1) * P],
                                        cst[0:T, C_DCOL:C_DCOL + 2], start=True, stop=True)
                    b.finish(ins)
                    b.wait_taken(pe, "mb", i)
                    o = b.start(pe, "cs", i)
                    da = mbt[0:T, P + 8:P + 16]
                    pe.matmul(o[0:T, 0:8], cst[0:T, C_TRI:C_TRI + T], da, start=True, stop=True)
                    pe.matmul(o[0:T, 8:16], cst[0:T, C_REV:C_REV + T], da, start=True, stop=True)
                    b.finish(pe.matmul(o[:, 16:24], core.ones[0:T, :], da, start=True, stop=True))
                    for g in range(2):
                        o = b.start(pe, f"cb{g}", i)
                        gs = slice(g * HD, (g + 1) * HD)
                        b.finish(pe.matmul(o[0:T, 0:T], xbi[gs, 4], xbi[gs, 5], start=True, stop=True))

                def a4(i, tok, T, rc, xc):
                    pe.wait_ge(dab_rdy, i + 1)
                    for g in range(2):
                        four(f"cst{g}", i, T, lambda h: dab[0:T, 4 * g + h, 0:T], lambda h: cst[0:T, C_TRI:C_TRI + T])

                def b1(i, tok, T, rc, xc):
                    b_fence(pe, i)
                    for n, (name, src) in enumerate((("bT", bh2[:, i % 2]), ("kT", kh2[:, i % 2]), ("aT", ah), ("rT", rh))):
                        pe.wait_ge(hats, 4 * i + n + 1)
                        o = b.start(pe, name, i)
                        for q in range(4):
                            ins = pe.transpose(o[:, q * T:(q + 1) * T], src[0:T, q * P:(q + 1) * P], ident[0:T, 0:T])
                        b.finish(ins)
                    b.wait_taken(pe, "aT", i)

                    def score(name, e, lhs, rhs):
                        es = slice(e * HD, (e + 1) * HD)
                        four(f"{name}{e}", i, T, lambda q: lhs[es, q, 0:T], lambda q: rhs[es, q, 0:T])

                    for name, lhs, rhs in (("ab", bT, aT), ("m", aT, bT)):
                        for e in range(2):
                            score(name, e, lhs, rhs)
                    b.wait_taken(pe, "rT", i)
                    for e in range(2):
                        for name, lhs, rhs in (("ak", kT, aT), ("rb", bT, rT)):
                            score(name, e, lhs, rhs)
                    for e in range(2):
                        score("rk", e, kT, rT)

                def level(n):
                    def run(i, tok, T, rc, xc):
                        last = last_level(i)
                        xbi = xbc_in[:, i % 2, :, 0:T]
                        for e in range(2):
                            if n == 1:
                                pe.wait_ge(x_rdy, 2 * i + e + 1)
                                pe.wait_ge(xt_rdy, 2 * i + e + 1)
                            else:
                                b.wait_taken(pe, f"x{n - 1}{e}", i)
                            four(f"q{n}{e}", i, T, lambda q: mT[0:T, e, q, 0:T], lambda q: xx[0:T, e, q, 0:T])
                        for e in range(2):
                            b.wait_taken(pe, f"q{n}{e}", i)
                            if n > 1:
                                b.wait_taken(pe, f"t{n - 1}{e}", i)
                            if n < last:
                                four(f"x{n}{e}", i, T, lambda q: xt[0:T, e, q, 0:T], lambda q: pq[0:T, e, q, 0:T])
                            four(f"t{n}{e}", i, T, lambda q: pq[0:T, e, q, 0:T], lambda q: xt[0:T, e, q, 0:T])
                        if n == 1:
                            if i not in (0, 4):
                                b.wait_taken(pe, "st", i - 1)
                            for g in range(2):
                                gs = slice(g * HD, (g + 1) * HD)
                                o = b.start(pe, f"yo{g}", i)
                                b.finish(pe.matmul(o[0:T, 0:4 * HD], xbi[gs, 5], ht[gs, frm[i], :, :],
                                                   start=True, stop=True))
                        if n == 2:
                            pe.wait_ge(l_rdy, 2 * (i + 1))
                            pe.wait_ge(xdt_rdy, 2 * (i + 1))
                            o = b.start(pe, "yd", i)
                            for h in range(HEADS):
                                ins = pe.matmul(o[0:T, h * HD:(h + 1) * HD], seg2[0:T, i % 2, h, 0:T],
                                                xdt2[0:T, i % 2, h, :], start=True, stop=True)
                            b.finish(ins)
                        if n == 3:
                            o = b.start(pe, "st", i)
                            for g in range(2):
                                gs = slice(g * HD, (g + 1) * HD)
                                ins = pe.matmul(o[gs, 0:4 * HD], mbt2[0:T, i % 2, gs], xw2[0:T, i % 2, 4 * g:4 * g + 4, :],
                                                start=True, stop=True)
                            b.finish(ins)
                    return run

                def b5(i, tok, T, rc, xc):
                    vt, bh, kh = vt2[:, i % 2], bh2[:, i % 2], kh2[:, i % 2]
                    last = last_level(i)
                    pe.wait_ge(s0_rdy, i + 1)
                    for e in range(2):
                        es = slice(e * HD, (e + 1) * HD)
                        b.wait_taken(pe, f"ak{e}", i)
                        o = b.start(pe, f"y{e}", i)
                        for q in range(4):
                            oo = o[0:T, q * HD:(q + 1) * HD]
                            apart(pe.matmul(oo, aT[es, q, 0:T], s0m[es, q, :], start=True, stop=False), e, T)
                            ins = pe.matmul(oo, ak[0:T, e, q, 0:T], vt[0:T, 2 * q + e, :], start=False, stop=True)
                            if q < 3:
                                apart(ins, e, T)
                        b.finish(ins)
                    pe.wait_ge(om_rdy, i + 1)
                    outs("om", i, T, ym)
                    for e in range(2):
                        b.wait_taken(pe, f"y{e}", i)
                        b.wait_taken(pe, f"t{last}{e}", i)
                        o = b.start(pe, f"u{e}", i)
                        for q in range(4):
                            ins = pe.matmul(o[0:T, q * HD:(q + 1) * HD], xt[0:T, e, q, 0:T], ys[0:T, e, q, :],
                                            start=True, stop=True)
                        b.finish(ins)
                    for e in range(2):
                        es = slice(e * HD, (e + 1) * HD)
                        b.wait_taken(pe, f"u{e}", i)
                        pe.wait_ge(rk_rdy, 2 * i + e + 1)
                        o = b.start(pe, f"o{e}", i)
                        for q in range(4):
                            oo = o[0:T, q * HD:(q + 1) * HD]
                            apart(pe.matmul(oo, rT[es, q, 0:T], s0m[es, q, :], start=True, stop=False), e, T)
                            pe.matmul(oo, rk[0:T, e, q, 0:T], vt[0:T, 2 * q + e, :], start=False, stop=False)
                            ins = pe.matmul(oo, rb[0:T, e, q, 0:T], us[0:T, e, q, :], start=False, stop=True)
                            if q < 3:
                                apart(ins, e, T)
                        b.finish(ins)
                    o = b.start(pe, "s", i)
                    for h in range(HEADS):
                        q, e = h // 2, h % 2
                        hs = slice(h * HD, (h + 1) * HD)
                        oo = o[e * HD:(e + 1) * HD, q * HD:(q + 1) * HD]
                        pe.matmul(oo, bh[0:T, hs], us[0:T, e, q, :], start=True, stop=False)
                        ins = pe.matmul(oo, kh[0:T, hs], vt[0:T, h, :], start=False, stop=True)
                    b.finish(ins)

                def outs(name, i, T, src):
                    flat = src[:, :, :].rearrange("p h d -> p (h d)")
                    o = b.start(pe, name, i)
                    for q in range(4):
                        ins = pe.transpose(o[:, q * T:(q + 1) * T], flat[0:T, q * P:(q + 1) * P], ident[0:T, 0:T])
                    b.finish(ins)

                def c4(i, tok, T, rc, xc):
                    pe.wait_ge(or_rdy, i + 1)
                    outs("or", i, T, os_)

                run_parts({"A1": a1, "A2": a2, "A4": a4, "B1": b1, "B5": b5, "C4": c4,
                           **{f"L{n}": level(n) for n in range(1, LEVELS)}})

            @block.scalar
            def _(act):
                act.wait_ge(par_in, 7 * 16)

                def take(name, i, dst, cols, func=ACT.Copy, **kw):
                    src = b.get(act, name, i)[0:dst.shape[0], 0:cols]
                    if len(dst.shape) == 3:
                        src = src.rearrange("p (h d) -> p h d", d=dst.shape[2])
                    b.took(act.activation(dst, src, func, **kw), name, i)

                def a1(i, tok, T, rc, xc):
                    a_fence(act, i)
                    vt, gt, mxt, mzt, mbt = vt2[:, i % 2], gt3[:, i % 3], mxt2[:, i % 2], mzt2[:, i % 2], mbt2[:, i % 2]
                    act.wait_ge(rows_in[i % 2], 64 * (i // 2 + 1))
                    wd, gd = pm_in[0:HD, i % 2, RT - 2, 0:T], pm_in[:, i % 2, RT - 1, 0:T]
                    act.activation(wd, wd, ACT.Tanh).then_inc(inner, 1)
                    act.activation(gd, gd, ACT.Sigmoid).then_inc(inner, 1)
                    take("k", i, kt[0:T], 512)
                    for n in range(2):
                        b.wait_taken(act, ("w", "a")[n], i)
                        act.activation(wa[0:T, n, :], wa[0:T, n, :], ACT.Sigmoid).then_inc(tanhs, 1)
                    take("r", i, rt[0:T], 512)
                    take("v", i, vt[0:T], 512)
                    take("g", i, gt[0:T], 512)
                    take("mb", i, mbt[0:T, :], P + 16)
                    take("mx", i, mxt[0:T], 512)
                    take("mz", i, mzt[0:T], 512)

                def a2(i, tok, T, rc, xc):
                    o = b.get(act, "cinc", i)
                    o3 = o[0:T, :].rearrange("p (h d) -> p h d", d=HD)
                    act.activation(eneg[0:T], o3, ACT.Exp, scale=-1.0).then_inc(exps, 1)
                    b.took(act.activation(einc[0:T], o3, ACT.Exp), "cinc", i)
                    take("cexc", i, eexc[0:T], 512, ACT.Exp)
                    take("dec", i, dec2[:, i % 2, :, :], 8, ACT.Exp)
                    b.wait_taken(act, "cs", i)
                    act.activation(ecs2[0:T, i % 2], csv[0:T], ACT.Exp).then_inc(cse, 1)
                    act.activation(hdec2[0:HD, i % 2, :], msmall[0:HD, 0, 0:4], ACT.Exp).then_inc(cse, 1)
                    act.activation(hdec2[HD:P, i % 2, :], msmall[HD:P, 0, 4:8], ACT.Exp).then_inc(cse, 1)
                    act.wait_ge(knorm_in, i + 1)
                    act.activation(small[0:T, 1, :], small[0:T, 0, :], ACT.Sqrt).then_inc(knorm, 1)

                def a4(i, tok, T, rc, xc):
                    for g in range(2):
                        b.wait_taken(act, f"cst{g}", i)
                        sg = seg2[0:T, i % 2, 4 * g:4 * g + 4, 0:T]
                        act.activation(sg, sg, ACT.Exp).then_inc(seg_exp, 1)

                def b1(i, tok, T, rc, xc):
                    b_fence(act, i)
                    for name, dst in (("bT", bT), ("kT", kT), ("aT", aT), ("rT", rT)):
                        take(name, i, dst[:, :, 0:T], 4 * T)
                    for e in range(2):
                        take(f"rk{e}", i, rk[0:T, e, :, 0:T], 4 * T)

                def level(n):
                    def run(i, tok, T, rc, xc):
                        for e in range(2):
                            if n < last_level(i):
                                take(f"x{n}{e}", i, xx[0:T, e, :, 0:T], 4 * T)
                            take(f"t{n}{e}", i, xt[0:T, e, :, 0:T], 4 * T)
                        if n == 4:
                            act.wait_ge(mnorm_in, i + 1)
                            act.activation(msmall[0:T, 3, 0:2], msmall[0:T, 2, 0:2], ACT.Sqrt).then_inc(mnorm, 1)
                    return run

                def b5(i, tok, T, rc, xc):
                    for e in range(2):
                        take(f"y{e}", i, ys[0:T, e], 4 * HD)
                    take("om", i, om[:, 4:8, tok:tok + T], 4 * T)
                    for e in range(2):
                        take(f"u{e}", i, us[0:T, e], 4 * HD)
                    for e in range(2):
                        take(f"o{e}", i, os_[0:T, e::2, :], 4 * HD)
                def c2(i, tok, T, rc, xc):
                    act.wait_ge(gnorm_in, i + 1)
                    act.activation(small_b[0:T, 5, :], small_b[0:T, 4, :], ACT.Sqrt).then_inc(gnorm, 1)

                def c4(i, tok, T, rc, xc):
                    take("or", i, om[:, 0:4, tok:tok + T], 4 * T)

                run_parts({"A1": a1, "A2": a2, "A4": a4, "B1": b1, "B5": b5, "C2": c2, "C4": c4,
                           **{f"L{n}": level(n) for n in range(1, LEVELS)}})

            @block.gpsimd
            def _(pool):
                pool.memset(st[:, 0, :, :], 0.0).then_inc(zeroed, 1)
                pool.memset(ht[:, 0, :, :], 0.0).then_inc(zeroed, 1)
                pool.wait_ge(par_in, 7 * 16)
                link = core.chains["pool"].on(pool)

                TT = pool.tensor_tensor

                def row(n, T):
                    return rows[0:T, n, :].rearrange("p (h d) -> p h d", d=HD)

                def per_head(ap, T):
                    return bc(ap, 2, [T, HEADS, HD])

                def a1(i, tok, T, rc, xc):
                    a_fence(pool, i)
                    b.wait_taken(pool, "k", i)
                    link(TT(kk[0:T], kt[0:T], row(2, T), ALU.mult))
                    TT(t0[0:T], kk[0:T], kk[0:T], ALU.mult).then_inc(ksq, 1)

                def a2(i, tok, T, rc, xc):
                    b.wait_taken(pool, "mb", i)
                    pool.tensor_copy(dab[0:T, :, 0:T], bc(mbt2[0:T, i % 2, P + 8:P + 16], 2, [T, HEADS, T])).then_inc(dab_rdy, 1)
                    b.wait_taken(pool, "mx", i)
                    TT(xdt2[0:T, i % 2], mxt2[0:T, i % 2], per_head(mbt2[0:T, i % 2, P:P + 8], T), ALU.mult).then_inc(xdt_rdy, 1)

                def a3(i, tok, T, rc, xc):
                    pool.wait_ge(kmod, i + 1)
                    b.wait_taken(pool, "r", i)
                    link(TT(t1[0:T], rt[0:T], km[0:T], ALU.mult))
                    TT(t1[0:T], t1[0:T], row(4, T), ALU.mult).then_inc(bonus, 1)
                    pool.wait_ge(cse, 3 * (i + 1))
                    pool.wait_ge(xdt_rdy, 2 * i + 1)
                    TT(xw2[0:T, i % 2], xdt2[0:T, i % 2], per_head(ecs2[0:T, i % 2, 1, :], T), ALU.mult).then_inc(xdt_rdy, 1)

                def b1(i, tok, T, rc, xc):
                    b_fence(pool, i)
                    for e in range(2):
                        b.wait_taken(pool, f"m{e}", i)
                        x = xx[0:T, e, :, 0:T]
                        TT(x, x, bc(core.ident[0:T, 0:T], 1, [T, 4, T]), ALU.add).then_inc(x_rdy, 1)
                    for e in range(2):
                        b.wait_taken(pool, f"rk{e}", i)
                        x = rk[0:T, e, :, 0:T]
                        TT(x, x, bc(cst[0:T, C_TRI:C_TRI + T], 1, [T, 4, T]), ALU.mult).then_inc(rk_rdy, 1)

                def l1(i, tok, T, rc, xc):
                    TT(t2[0:T], mxt2[0:T, i % 2], per_head(heads_row[0:T, :], T), ALU.mult).then_inc(skip, 1)

                def y2(i, tok, T, rc, xc):
                    b.wait_taken(pool, "yd", i)
                    b.wait_taken(pool, "mz", i)
                    pool.wait_ge(skip, i + 1)
                    link(TT(ym[0:T], ym[0:T], t2[0:T], ALU.add))
                    link(TT(ym[0:T], ym[0:T], mzt2[0:T, i % 2], ALU.mult))
                    TT(t2[0:T], ym[0:T], ym[0:T], ALU.mult).then_inc(ysq, 1)

                def l5(i, tok, T, rc, xc):
                    pool.wait_ge(yinv, i + 1)
                    yg = ym[0:T].rearrange("p (g h) d -> p g (h d)", g=2)
                    link(TT(yg, yg, bc(msmall[0:T, 1, 0:2], 2, [T, 2, 4 * HD]), ALU.mult))
                    TT(ym[0:T], ym[0:T], row(7, T), ALU.mult).then_inc(om_rdy, 1)

                def b5(i, tok, T, rc, xc):
                    if i:
                        pool.wait_ge(or_rdy, i)
                    pool.wait_ge(bonus_sum, i + 1)
                    TT(t4[0:T], vt2[0:T, i % 2], per_head(bonus2[0:T, i % 2, :], T), ALU.mult).then_inc(bonus_v, 1)

                def c3(i, tok, T, rc, xc):
                    if i < NT - 1:
                        scale_outputs(pool, link, i, T)

                run_parts({"A1": a1, "A2": a2, "A3": a3, "B1": b1, "L1": l1, "Y2": y2, "L5": l5, "B5": b5, "C3": c3})

            @block.vector
            def _(dve):
                link = core.chains["dve"].on(dve)
                dve.wait_ge(par_in, 7 * 16)
                dve.wait_ge(zeroed, 2)
                TT, STT, TS = dve.tensor_tensor, dve.scalar_tensor_tensor, dve.tensor_scalar

                def row(n, T):
                    return rows[0:T, n, :].rearrange("p (h d) -> p h d", d=HD)

                def h3(ap):
                    return ap.rearrange("p (h d) -> p h d", d=HD)

                def per_head(ap, T):
                    return bc(ap, 2, [T, HEADS, HD])

                def mask4(c, T):
                    return bc(cst[0:T, c:c + T], 1, [T, 4, T])

                def q4(o, T):
                    return o[0:T, 0:4 * T].rearrange("p (q t) -> p q t", t=T)

                def a1(i, tok, T, rc, xc):
                    a_fence(dve, i)
                    for n, name in enumerate(("w", "a")):
                        o = b.get(dve, name, i)[0:T, :]
                        b.took(TT(wa[0:T, n, :], o, rows[0:T, n, :], ALU.add), name, i)

                def a2(i, tok, T, rc, xc):
                    dve.wait_ge(ksq, i + 1)
                    dve.tensor_reduce(small[0:T, 0, :], t0[0:T], AX_X, ALU.add).then_inc(knorm_in, 1)
                    dve.wait_ge(tanhs, 2 * (i + 1))
                    dve.wait_ge(knorm_in, i + 1)
                    b.wait_taken(dve, "k", i)
                    link(STT(out=t0[0:T], in0=h3(wa[0:T, 1, :]), scalar=1.0, in1=row(3, T), op0=ALU.subtract, op1=ALU.mult))
                    STT(out=km[0:T], in0=t0[0:T], scalar=1.0, in1=kt[0:T], op0=ALU.add, op1=ALU.mult).then_inc(kmod, 1)
                    dve.wait_ge(kmod, i + 1)

                def a2b(i, tok, T, rc, xc):
                    o = b.get(dve, "cs", i)
                    dve.tensor_copy(csv[0:T], o[0:T, 0:16].rearrange("p (a h) -> p a h", h=HEADS))
                    b.took(dve.tensor_copy(msmall[:, 0, :], o[:, 16:24]), "cs", i)
                    for g in range(2):
                        o = b.get(dve, f"cb{g}", i)
                        b.took(TT(cb[0:T, g, 0:T], o[0:T, 0:T], cst[0:T, C_TRI:C_TRI + T], ALU.mult), f"cb{g}", i)

                def a3(i, tok, T, rc, xc):
                    dve.wait_ge(knorm, i + 1)
                    link(TS(small[0:T, 2, :], small[0:T, 1, :], 1e-12, None, ALU.max))
                    link(dve.reciprocal(small[0:T, 3, :], small[0:T, 2, :]))
                    link(TT(kk[0:T], kk[0:T], per_head(small[0:T, 3, :], T), ALU.mult))
                    link(TT(t0[0:T], kk[0:T], h3(wa[0:T, 1, :]), ALU.mult))
                    b.wait_taken(dve, "cinc", i)
                    TT(h3(bh2[0:T, i % 2, :]), t0[0:T], eneg[0:T], ALU.mult).then_inc(hats, 1)
                    TT(h3(kh2[0:T, i % 2, :]), km[0:T], eneg[0:T], ALU.mult).then_inc(hats, 1)

                def a4(i, tok, T, rc, xc):
                    b.wait_taken(dve, "cs", i)
                    for g in range(2):
                        o = b.get(dve, f"cst{g}", i)
                        for h in range(4):
                            ins = TS(seg2[0:T, i % 2, 4 * g + h, 0:T], o[0:T, h * T:(h + 1) * T],
                                     csv[0:T, 0, 4 * g + h:4 * g + h + 1], 0.0, ALU.subtract, ALU.min)
                        b.took(ins, f"cst{g}", i)
                    dve.wait_ge(bonus, i + 1)
                    dve.tensor_reduce(bonus2[0:T, i % 2, :], t1[0:T], AX_X, ALU.add).then_inc(bonus_sum, 1)

                def a5(i, tok, T, rc, xc):
                    b.wait_taken(dve, "dec", i)
                    b.wait_taken(dve, "r", i)
                    if i:
                        b.wait_taken(dve, "rT", i - 1)
                    STT(out=h3(ah[0:T, :]), in0=kk[0:T], scalar=-1.0, in1=eexc[0:T], op0=ALU.mult, op1=ALU.mult).then_inc(hats, 1)
                    TT(h3(rh[0:T, :]), rt[0:T], einc[0:T], ALU.mult).then_inc(hats, 1)
                    for g in range(2):
                        dve.wait_ge(seg_exp, 2 * i + g + 1)
                        b.wait_taken(dve, f"cb{g}", i)
                        sg = seg2[0:T, i % 2, 4 * g:4 * g + 4, 0:T]
                        TT(sg, sg, bc(cb[0:T, g, 0:T], 1, [T, 4, T]), ALU.mult).then_inc(l_rdy, 1)

                def b1(i, tok, T, rc, xc):
                    b_fence(dve, i)
                    TT(s0m[:], st[:, frm[i]], bc(dec2[:, i % 2, :, 0], 2, [P, 4, HD]), ALU.mult).then_inc(s0_rdy, 1)

                    def masked(name, e, dst, mask):
                        o = q4(b.get(dve, f"{name}{e}", i), T)
                        b.took(TT(dst[0:T, e, :, 0:T], o, mask4(mask, T), ALU.mult), f"{name}{e}", i)

                    one = bc(core.ident[0:T, 0:T], 1, [T, 4, T])
                    for e in range(2):
                        masked("ab", e, mT, C_MS)
                    for e in range(2):
                        masked("m", e, xx, C_LEV)
                    b.wait_taken(dve, "ab1", i)
                    for e in range(2):
                        link(TT(mT[0:T, e, :, 0:T], mT[0:T, e, :, 0:T], one, ALU.add))
                        TT(xt[0:T, e, :, 0:T], mT[0:T, e, :, 0:T], mask4(C_LT0, T), ALU.mult).then_inc(xt_rdy, 1)
                    for e in range(2):
                        masked("ak", e, ak, C_MS)
                        masked("rb", e, rb, C_TRI)

                def level(n):
                    def run(i, tok, T, rc, xc):
                        for e in range(2):
                            o = q4(b.get(dve, f"q{n}{e}", i), T)
                            b.took(TT(pq[0:T, e, :, 0:T], o, mask4(C_LEV + n * P, T), ALU.mult), f"q{n}{e}", i)
                        if n == 4:
                            dve.wait_ge(ysq, i + 1)
                            link(dve.tensor_reduce(msmall[0:T, 1, 0:2],
                                                   t2[0:T].rearrange("p (g h) d -> p g (h d)", g=2), AX_X, ALU.add))
                            TS(msmall[0:T, 2, 0:2], msmall[0:T, 1, 0:2], 1.0 / 256, NORM_EPS, ALU.mult,
                               ALU.add).then_inc(mnorm_in, 1)
                        if n == 5:
                            dve.wait_ge(mnorm, i + 1)
                            dve.reciprocal(msmall[0:T, 1, 0:2], msmall[0:T, 3, 0:2]).then_inc(yinv, 1)
                    return run

                def y1(i, tok, T, rc, xc):
                    for g in range(2):
                        o = b.get(dve, f"yo{g}", i)[0:T, 0:4 * HD]
                        b.took(TT(ym[0:T, 4 * g:4 * g + 4, :], h3(o),
                                  bc(ecs2[0:T, i % 2, 0, 4 * g:4 * g + 4], 2, [T, 4, HD]), ALU.mult), f"yo{g}", i)

                def y2(i, tok, T, rc, xc):
                    o = b.get(dve, "yd", i)[0:T, :]
                    b.wait_taken(dve, "yo1", i)
                    b.took(TT(ym[0:T], h3(o), ym[0:T], ALU.add), "yd", i)

                def y3(i, tok, T, rc, xc):
                    link(TT(t5[:], ht[:, frm[i]], bc(hdec2[:, i % 2, :], 2, [P, 4, HD]), ALU.mult))
                    o = b.get(dve, "st", i)[:, 0:4 * HD]
                    b.took(TT(ht[:, into[i]], h3(o), t5[:], ALU.add), "st", i)
                    b.wait_taken(dve, "st", i)

                def b5(i, tok, T, rc, xc):
                    o = b.get(dve, "s", i)[:, 0:4 * HD]
                    b.took(TT(t5[:], h3(o), s0m[:], ALU.add), "s", i)
                    b.wait_taken(dve, "s", i)
                    TT(st[:, into[i]], t5[:], bc(dec2[:, i % 2, :, 1], 2, [P, 4, HD]), ALU.mult).then_inc(states, 1)

                def c1(i, tok, T, rc, xc):
                    b.wait_taken(dve, "o1", i)
                    if i:
                        dve.wait_ge(or_rdy, i)
                    link(dve.tensor_reduce(small_b[0:T, 0, :], os_[0:T], AX_X, ALU.add))
                    link(TS(small_b[0:T, 1, :], small_b[0:T, 0, :], 1.0 / HD, None, ALU.mult))
                    link(TT(os_[0:T], os_[0:T], per_head(small_b[0:T, 1, :], T), ALU.subtract))
                    link(TT(t1[0:T], os_[0:T], os_[0:T], ALU.mult))
                    link(dve.tensor_reduce(small_b[0:T, 2, :], t1[0:T], AX_X, ALU.add))
                    TS(small_b[0:T, 4, :], small_b[0:T, 2, :], 1.0 / HD, GN_EPS, ALU.mult, ALU.add).then_inc(gnorm_in, 1)

                def c3(i, tok, T, rc, xc):
                    dve.wait_ge(gnorm, i + 1)
                    dve.reciprocal(small_b[0:T, 6, :], small_b[0:T, 5, :]).then_inc(ginv, 1)
                    if i == NT - 1:
                        scale_outputs(dve, link, i, T)

                run_parts({"A1": a1, "A2": a2, "A2b": a2b, "A3": a3, "A4": a4, "A5": a5, "Y1": y1, "Y2": y2, "Y3": y3, "B1": b1, "B5": b5, "C1": c1, "C3": c3,
                           **{f"L{n}": level(n) for n in range(1, LEVELS)}})


def project_out(core, acts, norm, following):
    nc, a = core.nc, core.a
    with ExitStack() as ctx:
        gemm = Gemm(core, ctx, "wout", acts, DT, a["w_out"])
        om = acts.x
        x_in = [core.sem(f"res_in{n}") for n in range(4)]
        high, low, added = core.sem("o_high"), core.sem("o_low"), core.sem("res_added")

        with nc.Block() as block:
            @block.sync
            def _(sp):
                gemm.load(sp, 0)
                gemm.load(sp, 1)
                gemm.load(sp, 2)
                for n in range(4):
                    sp.wait_ge(low, 2 * n + 2)
                    sp.dma_start(acts.x[:, 2 * n:2 * n + 2, :], a["x"][:, 2 * n:2 * n + 2]).then_inc(x_in[n], 16)
                for c in range(3, DT):
                    gemm.load(sp, c)
                for c in range(3):
                    following.load(sp, c)

            @block.gpsimd
            def _(pool):
                for c in range(DT):
                    gemm.split_low(pool, c)
                for c in range(2):
                    following.split_low(pool, c)

            @block.tensor
            def _(pe):
                for c in range(DT):
                    gemm.multiply(pe, c, ready=(low, 0) if c == 0 else None)
                norm.pe_sums(pe)

            @block.scalar
            def _(act):
                for dt in range(DT):
                    if dt == 2:
                        gemm.split_high(act, 0)
                    act.activation(acts.hi[:, dt, :], om[:, dt, :], ACT.Copy).then_inc(high, 1)
                for c in range(1, DT):
                    gemm.split_high(act, c)
                for c in range(2):
                    following.split_high(act, c)
                norm.act_squares(act, ready=lambda dt: (gemm.taken, dt + 1))

            @block.vector
            def _(dve):
                for dt in range(DT):
                    dve.wait_ge(high, dt + 1)
                    dve.tensor_tensor(acts.lo[:, dt, :], om[:, dt, :], acts.hi[:, dt, :].bitcast(F32),
                                      ALU.subtract).then_inc(low, 1)
                for c in range(DT):
                    dve.wait_ge(x_in[c // 2], 16)
                    dve.wait_ge(gemm.done, c + 1)
                    for half in range(2):
                        x = acts.x[:, c, half * HALF:(half + 1) * HALF]
                        ins = dve.tensor_tensor(x, gemm.out(c, half), x, ALU.add)
                        ins.then_inc((added, gemm.taken)[half], 1)
                dve.wait_ge(gemm.taken, DT)


def route_jobs(nq):
    jobs, h = [], 0
    for c in range(nq):
        for _ in range(4 if c == 4 else 2 if c > 4 else 0):
            jobs.append(("hidden", h))
            h += 1
        jobs.append(("q", c))
    return jobs + [("hidden", n) for n in range(h, AHEAD4)]


def route(core, norm, gemm, jobs, sel, numbers):
    nc, a = core.nc, core.a
    with ExitStack() as ctx:
        def sb(name, *shape, dt=F32):
            return core.sb(name, list(shape), dt, ctx)

        NC = 2 * P_HEADS
        job_of_q = {n: j for j, (kind, n) in enumerate(jobs) if kind == "q"}
        exp_after = {job_of_q[2 * h + 4]: h for h in range(P_HEADS - 2)}
        exp_after.update({job_of_q[NC - 1] + 3: P_HEADS - 2, job_of_q[NC - 1] + 10: P_HEADS - 1})
        match_after = {j - 2 + side: (h, side) for j, h in exp_after.items() for side in range(2)}
        gelu = sb("gelu_ahead", P, 2, TOK)
        gelu_sent = [core.sem(f"gelu_ahead_sent{n}") for n in range(2)]
        keys = sb("sub_keysT", P, 2, N_KEYS)
        ranks = numbers[:, 0:TOPK]
        qT = sb("qT", P, 2, TOK)
        sc = sb("scores", P, 2, NT, N_KEYS)
        left = sb("scores_left", P, NT, N_KEYS)
        val = sb("top_values", P, 2, NT, TOPK)
        idx = sb("top_index", P, 2, NT, TOPK, dt=U32)
        idf = sb("top_index_f", P, 2, 2, NT, TOPK)
        match = sb("rank_match", P, 2, NT, TOPK * TOPK)
        cand = sb("candidates", P, NT, TOPK * TOPK)
        cleft = sb("candidates_left", P, NT, TOPK * TOPK)
        tv = sb("pick_values", P, 2, NT, TOPK)
        tp = sb("pick_pos", P, NT, TOPK, dt=U32)
        rk = sb("pick_rank", P, 2, NT, TOPK, dt=U32)
        rkf = sb("pick_rank_f", P, 2, NT, TOPK)
        gsum = sb("gate_sum", P, NT, 2)
        picks = sb("picks", P, NT, 3, SEL)
        par_in = core.sem("route_in")
        s_done, s_taken = core.sem("scores_done"), core.sem("scores_taken")
        ranked, zeroed = core.sem("ranked"), core.sem("scores_zeroed")
        e_in, e_out = core.sem("gate_args"), core.sem("gate_exps")
        picked, turned, sel_out = core.sem("picked"), core.sem("picks_turned"), core.sem("picks_out")
        matched, keyed = core.sem("ranks_matched"), core.sem("keys_matched")

        with nc.Block() as block:
            @block.sync
            def _(sp):
                sp.dma_start(keys[:, :, :], a["keysT"]).then_inc(par_in, 16)
                sp.dma_start(numbers[:, :], a["ranks"]).then_inc(par_in, 16)
                def send(j):
                    kind, n = jobs[j]
                    if kind == "hidden":
                        sp.wait_ge(gemm.taken, j + 1)
                        sp.dma_start(a["hidden"][n], gelu[:, n % 2, :]).then_inc(gelu_sent[n % 2], 16)

                LAG = 4
                for j in range(len(jobs)):
                    if j >= 3:
                        gemm.load(sp, j)
                    if j >= LAG:
                        send(j - LAG)
                for j in range(len(jobs) - LAG, len(jobs)):
                    send(j)
                for n in range(2):
                    sp.wait_ge(gelu_sent[n], 16 * (AHEAD4 // 2))

            @block.gpsimd
            def _(pool):
                pool.memset(sc[:, :, NT - 1, :], 0.0).then_inc(zeroed, 1)
                def match_keys(h, side):
                    pool.wait_ge(matched, 2 * h + side + 1)
                    e4 = match[:, side].rearrange("p n (a b) -> p n a b", a=TOPK)
                    pool.tensor_tensor(e4, e4, bc(idf[:, h % 2, side], 2, [P, NT, TOPK, TOPK]), ALU.mult).then_inc(keyed, 1)

                for j in range(2, len(jobs)):
                    gemm.split_low(pool, j)
                    if j in match_after:
                        match_keys(*match_after[j])

            @block.tensor
            def _(pe):
                def scores(c):
                    pe.wait_ge(gemm.taken, job_of_q[c] + 1)
                    if c >= 2:
                        pe.wait_ge(s_taken, c - 1)
                    for n, (tok, T, _, _) in enumerate(TILES):
                        bank = core.bank(4 + 2 * (c % 2) + n // 4)
                        ins = pe.matmul(bank[0:T, (n % 4) * P:(n % 4 + 1) * P], qT[:, c % 2, tok:tok + T],
                                        keys[:, c % 2, :], start=True, stop=True)
                    ins.then_inc(s_done, 1)

                pe.wait_ge(par_in, 32)
                for j, (kind, n) in enumerate(jobs):
                    gemm.multiply(pe, j, ready=(norm.low, norm.b8) if j == 0 else None)
                    if j and jobs[j - 1][0] == "q":
                        scores(jobs[j - 1][1])
                for n, (tok, T, _, _) in enumerate(TILES):
                    pe.wait_ge(picked, 3 * P_HEADS)
                    if n >= 2:
                        pe.wait_ge(sel_out, n - 1)
                    for k in range(3):
                        ins = pe.transpose(core.psum[:, 4 + n % 2, k * P:k * P + T], picks[0:T, n, k, :],
                                           core.ident[0:T, 0:T])
                    ins.then_inc(turned, 1)

            @block.scalar
            def _(act):
                def take_scores(c):
                    act.wait_ge(s_done, c + 1)
                    act.wait_ge(zeroed, 1)
                    if c >= 2:
                        act.wait_ge(ranked, c - 1)
                    bank = core.bank(4 + 2 * (c % 2))
                    act.activation(sc[:, c % 2, 0:4, :], bank.rearrange("p (n k) -> p n k", n=4), ACT.Copy)
                    bank = core.bank(5 + 2 * (c % 2))
                    act.activation(sc[0:DEC_SEQ, c % 2, 4, :], bank[0:DEC_SEQ, 0:P], ACT.Copy).then_inc(s_taken, 1)

                def gate_exp(h):
                    act.wait_ge(e_in, h + 1)
                    act.activation(tv[:, h % 2], tv[:, h % 2], ACT.Exp).then_inc(e_out, 1)

                norm.act_root(act)
                norm.act_high(act)
                for j, (kind, n) in enumerate(jobs):
                    if 2 <= j + 1 < len(jobs):
                        gemm.split_high(act, j + 1)
                    act.wait_ge(gemm.done, j + 1)
                    if kind == "q":
                        if n >= 2:
                            act.wait_ge(s_done, n - 1)
                        act.activation(qT[:, n % 2, 0:HALF], gemm.out(j, 0), ACT.Copy)
                        act.activation(qT[:, n % 2, HALF:], gemm.out(j, 1), ACT.Copy).then_inc(gemm.taken, 1)
                    else:
                        if n >= 2:
                            act.wait_ge(gelu_sent[n % 2], 16 * (n // 2))
                        act.activation(gelu[:, n % 2, 0:HALF], gemm.out(j, 0), ACT.Gelu)
                        act.activation(gelu[:, n % 2, HALF:], gemm.out(j, 1), ACT.Gelu).then_inc(gemm.taken, 1)
                    if j and jobs[j - 1][0] == "q":
                        take_scores(jobs[j - 1][1])
                    if j in exp_after:
                        gate_exp(exp_after[j])
                for n, (tok, T, _, _) in enumerate(TILES):
                    act.wait_ge(turned, n + 1)
                    act.activation(sel[:, :, tok:tok + T],
                                   core.psum[:, 4 + n % 2, 0:3 * P].rearrange("p (k t) -> p k t", k=3)[:, :, 0:T],
                                   ACT.Copy).then_inc(sel_out, 1)

            @block.vector
            def _(dve):
                link = core.chains["dve"].on(dve)

                def top16(values, index, source, rest, read=None):
                    for n in range(NT):
                        ins = dve.max(values[:, n, 0:8], source[:, n, :])
                    link(ins)
                    for n in range(NT):
                        dve.match_replace(rest[:, n, :], values[:, n, 0:8], source[:, n, :], LOWEST)
                        ins = dve.max_index(index[:, n, 0:8], values[:, n, 0:8], source[:, n, :])
                    if read is None:
                        link(ins)
                    else:
                        ins.then_inc(read[0], 1)
                        dve.wait_ge(*read)
                    for n in range(NT):
                        ins = dve.max(values[:, n, 8:16], rest[:, n, :])
                    link(ins)
                    for n in range(NT):
                        ins = dve.max_index(index[:, n, 8:16], values[:, n, 8:16], rest[:, n, :])
                    link(ins)

                def finish_picks(h):
                    hs = slice(h * TOPK, (h + 1) * TOPK)
                    for side in range(2):
                        dve.wait_ge(keyed, 2 * h + side + 1)
                        e4 = match[:, side].rearrange("p n (a b) -> p n a b", a=TOPK)
                        dve.tensor_reduce(picks[:, :, side, hs], e4, AX_X, ALU.add).then_inc(picked, 1)
                    dve.wait_ge(e_out, h + 1)
                    link(dve.tensor_reduce(gsum[:, :, 0], tv[:, h % 2], AX_X, ALU.add))
                    link(dve.reciprocal(gsum[:, :, 1], gsum[:, :, 0]))
                    dve.tensor_tensor(picks[:, :, 2, hs], tv[:, h % 2], gsum[:, :, 1:2].broadcast_to([P, NT, TOPK]),
                                      ALU.mult).then_inc(picked, 1)
                    dve.wait_ge(picked, 3 * h + 3)

                norm.dve(dve)
                dve.wait_ge(par_in, 32)
                for h in range(P_HEADS):
                    for side in range(2):
                        c = 2 * h + side
                        dve.wait_ge(s_taken, c + 1)
                        top16(val[:, side], idx[:, side], sc[:, side], left, read=(ranked, c + 1))
                        if side == 0 and h:
                            finish_picks(h - 1)
                    link(dve.tensor_copy(idf[:, h % 2], idx[:, :, :, :]))
                    c4 = cand[:, :, :].rearrange("p n (a b) -> p n a b", a=TOPK)
                    grid = [P, NT, TOPK, TOPK]
                    link(dve.tensor_tensor(c4, bc(val[:, 0], 3, grid), bc(val[:, 1], 2, grid), ALU.add))
                    top16(tv[:, h % 2], tp, cand, cleft)
                    dve.tensor_scalar(rk[:, 0], tp[:, :, :], 4, None, ALU.logical_shift_right)
                    link(dve.tensor_scalar(rk[:, 1], tp[:, :, :], TOPK - 1, None, ALU.bitwise_and))
                    dve.tensor_copy(gsum[:, :, 1:2], tv[:, h % 2, :, 0:1])
                    link(dve.tensor_copy(rkf[:, :, :, :], rk[:, :, :, :]))
                    for side in range(2):
                        dve.tensor_tensor(match[:, side].rearrange("p n (a b) -> p n a b", a=TOPK), bc(rkf[:, side], 3, grid),
                                          ranks[:, :].unsqueeze(1).unsqueeze(1).broadcast_to(grid),
                                          ALU.is_equal).then_inc(matched, 1)
                    dve.tensor_tensor(tv[:, h % 2], tv[:, h % 2], gsum[:, :, 1:2].broadcast_to([P, NT, TOPK]),
                                      ALU.subtract).then_inc(e_in, 1)
                    dve.wait_ge(e_in, h + 1)
                    dve.wait_ge(matched, 2 * h + 2)
                finish_picks(P_HEADS - 1)


class U:

    def __init__(self, core, ctx):
        self.dram = core.a["u"]
        self.raw = core.sb("u_raw", [P, 2, 2, DT * P], ctx=ctx)
        self.hi = core.sb("u_high", [P, 2, DT * P], F32R, ctx=ctx)
        self.lo = core.sb("u_low", [P, 2, DT * P], F32R, ctx=ctx)
        self.loaded = [core.sem(f"u_in{n}") for n in range(2)]
        self.high, self.low = core.sem("u_high_done"), core.sem("u_low_done")

    def load(self, sp, g, s):
        sp.dma_start(self.raw[:, s], self.dram[bass.ds(g * JJ + 2 * s, 2)].rearrange(
            "c p n -> p c n")).then_inc(self.loaded[s], 16)

    def split_high(self, act, g, jj):
        act.wait_ge(self.loaded[jj // 2], g * 16 + 16)
        act.activation(self.hi[:, jj % 2], self.raw[:, jj // 2, jj % 2], ACT.Copy).then_inc(self.high, 1)

    def split_low(self, pool, g, jj):
        pool.wait_ge(self.high, g * JJ + jj + 1)
        pool.tensor_tensor(self.lo[:, jj % 2], self.raw[:, jj // 2, jj % 2], self.hi[:, jj % 2].bitcast(F32),
                           ALU.subtract).then_inc(self.low, 1)


def spread_gates(core, acts, u, sel, iota):
    nc, a = core.nc, core.a
    with ExitStack() as ctx:
        FOUR, SLOTS, PER = 4, 4, 2 * TB // 4
        cur = core.sb("cur_picks", [P, 3, 2 * TB], ctx=ctx)
        onea = core.sb("onehot_first", [P, SLOTS * FOUR, N_KEYS], ctx=ctx)
        oneb = core.sb("gated_second", [P, SLOTS * FOUR, N_KEYS], ctx=ctx)
        stage = core.sb("gate_stage", [P, 2, NG, TB, JJ], ctx=ctx)
        onehots = core.sem("onehots_ready")
        bank_done = core.sem("gates_done")
        staged = core.sem("gates_staged")
        sent = [core.sem(f"gates_sent{n}") for n in range(2)]
        copied = core.sem("picks_copied")
        steps = G_STEPS
        BANKS = 4
        AFTER = {5: (0, 0), 8: (0, 1), 11: (1, 0), 14: (1, 1)}
        SPLIT = {1: 0, 3: 1}
        uh, ul = u.hi, u.lo
        gelu = core.sb("gelu_ahead5", [P, 2, TOK], ctx=ctx)
        u_in = [core.sem(f"u_ahead_in{n}") for n in range(2)]
        u_high = core.sem("u_ahead_high_done")
        u_low = core.sem("u_ahead_low_done")
        hid_done = core.sem("ahead_done")
        gelu_done = core.sem("gelu_ahead_done")
        gelu_sent = [core.sem(f"gelu_ahead5_sent{n}") for n in range(2)]

        def hid_bank(s, half):
            return core.psum[:, 4 + 2 * s + half, 0:HALF]

        with nc.Block() as block:
            @block.sync
            def _(sp):
                def load_u(it):
                    for s in range(2):
                        sp.wait_ge(u_low, it * 2 + s + 1)
                        sp.dma_start(u.raw[:, s, 0], a["u"][bass.ds(it * 2 + (KEY5 + s), 1)].rearrange(
                            "o p n -> p (o n)")).then_inc(u_in[s], 16)

                def send_gates(it, b):
                    sp.wait_ge(staged, it * PER + (8 * (b + 1) + BANKS))
                    dst = a["gates"][:, :, bass.ds(it * (2 * TB) + b * TB, TB), :].rearrange("g p t j -> p g (t j)")
                    sp.dma_start(dst, stage[:, b].rearrange("p g t j -> p g (t j)")).then_inc(sent[b], 16)

                def send_hidden(it):
                    for s in range(2):
                        sp.wait_ge(gelu_done, it * 4 + (2 * s + 2 + 4))
                        sp.dma_start(a["hidden"][bass.ds(it * 2 + (AHEAD4 + s), 1)].rearrange("o p t -> p (o t)"),
                                     gelu[:, s, :]).then_inc(gelu_sent[s], 16)

                def step(it, following):
                    send_gates(it, 0)
                    following()
                    send_hidden(it)
                    send_gates(it, 1)

                def load_first_group():
                    sp.wait_ge(u_low, 2 * steps + 2)
                    for s in range(2):
                        u.load(sp, 0, s)

                load_u(0)
                with sp.Fori(0, steps - 1) as it:
                    step(it, lambda: load_u(it + 1))
                step(steps - 1, load_first_group)
                for b in range(2):
                    sp.wait_ge(sent[b], 16 * (steps + 1))
                    sp.wait_ge(gelu_sent[b], 16 * (steps + 1))

            @block.gpsimd
            def _(pool):
                pool.sem_inc(u_low, 2)
                with pool.Fori(0, steps) as it:
                    for s in range(2):
                        pool.wait_ge(u_high, it * 2 + s + 1)
                        pool.tensor_tensor(ul[:, s], u.raw[:, s, 0], uh[:, s].bitcast(F32), ALU.subtract).then_inc(u_low, 1)
                for jj in range(2):
                    u.split_low(pool, 0, jj)

            @block.tensor
            def _(pe):
                pe.sem_inc(hid_done, 4)
                with pe.Fori(0, steps) as it:
                    for g in range(PER):
                        pe.wait_ge(onehots, it * PER + g + 2)
                        pe.wait_ge(staged, it * PER + g + 1)
                        for t in range(FOUR):
                            s = (g % SLOTS) * FOUR + t
                            ins = pe.matmul(core.psum[:, g % BANKS, t * P:(t + 1) * P], onea[:, s, :], oneb[:, s, :],
                                            start=True, stop=True)
                        ins.then_inc(bank_done, 1)
                        if g in AFTER:
                            s, half = AFTER[g]
                            pe.wait_ge(u_low, it * 2 + s + 1 + 2)
                            pe.wait_ge(gelu_done, it * 4 + 2 * s + half + 1)
                            cols = slice(half * HALF, (half + 1) * HALF)
                            for dt in range(DT):
                                w = slice(dt * P, (dt + 1) * P)
                                ins = three_products(pe, hid_bank(s, half), uh[:, s, w], ul[:, s, w],
                                                     acts.hi[:, dt, cols], acts.lo[:, dt, cols], dt == 0, dt == DT - 1)
                            ins.then_inc(hid_done, 1)

            @block.scalar
            def _(act):
                act.sem_inc(staged, BANKS)
                act.sem_inc(gelu_done, 4)
                for n in range(2):
                    act.sem_inc(sent[n], 16)
                    act.sem_inc(gelu_sent[n], 16)
                with act.Fori(0, steps) as it:
                    for g in range(PER):
                        b, r = g // 8, g % 8
                        if r == 0:
                            act.wait_ge(sent[b], 16 * it + 16)
                        act.wait_ge(bank_done, it * PER + g + 1 + SLOTS)
                        src = core.psum[:, g % BANKS, :].rearrange("p (t g j) -> p g t j", t=FOUR, j=JJ)
                        act.activation(stage[:, b, :, r * FOUR:(r + 1) * FOUR, :], src, ACT.Copy).then_inc(staged, 1)
                        if g in SPLIT:
                            s = SPLIT[g]
                            act.wait_ge(u_in[s], 16 * it + 16)
                            act.wait_ge(hid_done, it * 4 + 2 * s + 2)
                            act.activation(uh[:, s], u.raw[:, s, 0], ACT.Copy).then_inc(u_high, 1)
                        if g in AFTER:
                            s, half = AFTER[g]
                            act.wait_ge(hid_done, it * 4 + 2 * s + half + 1 + 4)
                            if half == 0:
                                act.wait_ge(gelu_sent[s], 16 * it + 16)
                            act.activation(gelu[:, s, half * HALF:(half + 1) * HALF], hid_bank(s, half),
                                           ACT.Gelu).then_inc(gelu_done, 1)
                act.wait_ge(hid_done, 4 * steps + 4)
                for jj in range(2):
                    u.split_high(act, 0, jj)

            @block.vector
            def _(dve):
                dve.sem_inc(onehots, 1)
                dve.sem_inc(bank_done, SLOTS)
                with dve.Fori(0, steps) as it:
                    dve.wait_ge(onehots, it * PER + 1)
                    dve.tensor_copy(cur[:, :, :], sel[:, :, bass.ds(it * (2 * TB), 2 * TB)]).then_inc(copied, 1)
                    dve.wait_ge(copied, it + 1)
                    for g in range(PER):
                        dve.wait_ge(bank_done, it * PER + g + 1)
                        s0, k0 = (g % SLOTS) * FOUR, g * FOUR
                        dve.tensor_tensor(onea[:, s0:s0 + FOUR, :], bc(iota[:, :], 1, [P, FOUR, N_KEYS]),
                                          bc(cur[:, 0, k0:k0 + FOUR], 2, [P, FOUR, N_KEYS]), ALU.is_equal)
                        for t in range(FOUR):
                            s, k = s0 + t, k0 + t
                            ins = dve.tensor_scalar(oneb[:, s, :], iota[:, :], cur[:, 1, k:k + 1], cur[:, 2, k:k + 1],
                                                    ALU.is_equal, ALU.mult)
                        ins.then_inc(onehots, 1)


def experts(core, acts, u, following):
    nc, a = core.nc, core.a
    with ExitStack() as ctx:
        def sb(name, *shape, dt=F32):
            return core.sb(name, list(shape), dt, ctx)

        OUTS = 2 * DT
        QW = D_MODEL // 4
        v_raw = sb("v_raw", P, 4, JJ * QW)
        gates = sb("gates_in", P, 2, TOK, JJ)
        vh, vl = sb("v_high", P, 4, JJ * QW, dt=F32R), sb("v_low", P, 4, JJ * QW, dt=F32R)
        gelu = sb("gelu_out", P, 2, TOK)
        prod = sb("gated", P, 2, TOK)
        wh, wl = sb("w_high", P, 2, JJ, TOK, dt=F32R), sb("w_low", P, 2, JJ, TOK, dt=F32R)
        g_in = [core.sem(f"gates_in{n}") for n in range(2)]
        v_in = [core.sem(f"v_in{n}") for n in range(4)]
        h_in = [core.sem(f"hidden_in{n}") for n in range(2)]
        v_high, v_low = core.sem("v_high_done"), core.sem("v_low_done")
        hid_done = core.sem("hidden_done")
        gelu_done = core.sem("gelu_done")
        prod_done = core.sem("gated_done")
        w_high = core.sem("w_high_done")
        w_low = core.sem("w_low_done")
        out_done = core.sem("out_done")
        out_added = core.sem("out_added")
        O2 = 2 * OUTS

        def groups(whole, loaded, before=None, after=None):
            def run(eng):
                if before:
                    before(eng)
                whole(eng, 0, 0, first=True, last=False)
                with eng.Fori(0, NH // 2 - 1) as it:
                    whole(eng, it * 2 + 1, 1, first=False, last=False)
                    whole(eng, it * 2 + 2, 0, first=False, last=False)
                whole(eng, NH - 1, 1, first=False, last=True)
                with eng.Fori(0, (NG - NH) // 2) as it:
                    loaded(eng, it * 2 + NH, 0)
                    loaded(eng, it * 2 + (NH + 1), 1)
                if after:
                    after(eng)
            return run

        def load_gates(sp, g, par):
            sp.dma_start(gates[:, par], a["gates"][bass.ds(g, 1)].rearrange("o p t j -> p (o t) j")).then_inc(g_in[par], 16)

        def load_v(sp, g, first):
            for q in range(4):
                if not first:
                    sp.wait_ge(v_low, (g - 1) * 4 + q + 1)
                sp.dma_start(v_raw[:, q], a["v"][bass.ds(g, 1), :, q].rearrange("o p n -> p (o n)")).then_inc(v_in[q], 16)

        def sp_whole(sp, g, par, first, last):
            for s in range(2):
                if not first:
                    sp.wait_ge(u.low, (g - 1) * JJ + 2 * s + 2)
                    u.load(sp, g, s)
            if not first:
                sp.wait_ge(prod_done, g * JJ - 2)
            load_gates(sp, g, par)
            load_v(sp, g, first)

        def sp_loaded(sp, g, par):
            def load_hidden(jj):
                sp.wait_ge(prod_done, g * JJ + jj + 1)
                sp.dma_start(gelu[:, jj % 2], a["hidden"][bass.ds(g * JJ + (jj - NH * JJ), 1)].rearrange(
                    "o p t -> p (o t)")).then_inc(h_in[jj % 2], 16)

            sp.wait_ge(prod_done, g * JJ - 2)
            load_gates(sp, g, par)
            load_hidden(0)
            load_hidden(1)
            load_v(sp, g, False)
            load_hidden(2)
            load_hidden(3)

        def split_v_high(act, g, q):
            act.wait_ge(v_in[q], g * 16 + 16)
            act.wait_ge(out_done, g * OUTS + 4 * q + 4 + OUTS)
            act.activation(vh[:, q], v_raw[:, q], ACT.Copy).then_inc(v_high, 1)

        def split_v_low(dve, g, q):
            dve.wait_ge(v_high, g * 4 + q + 1)
            dve.tensor_tensor(vl[:, q], v_raw[:, q], vh[:, q].bitcast(F32), ALU.subtract).then_inc(v_low, 1)

        def hidden(pe, g):
            for jj in range(JJ):
                n = g * JJ + jj
                pe.wait_ge(u.low, n + 1)
                pe.wait_ge(gelu_done, n + 1)
                for half in range(2):
                    o = core.psum[:, 2 * (jj % 2) + half, 0:HALF]
                    cols = slice(half * HALF, (half + 1) * HALF)
                    for dt in range(DT):
                        w = slice(dt * P, (dt + 1) * P)
                        ins = three_products(pe, o, u.hi[:, jj % 2, w], u.lo[:, jj % 2, w],
                                             acts.hi[:, dt, cols], acts.lo[:, dt, cols], dt == 0, dt == DT - 1)
                ins.then_inc(hid_done, 1)

        def out(pe, g, par):
            for k in range(OUTS):
                dt, half, q = k // 2, k % 2, k // 4
                if k % 4 == 0:
                    pe.wait_ge(v_low, g * 4 + q + 1)
                pe.wait_ge(out_added, g * OUTS + k + 1)
                o = core.psum[:, 4 + k % 4, 0:HALF]
                for jj in range(JJ):
                    if k == 0:
                        pe.wait_ge(w_low, g * JJ + jj + 1 + 2)
                    w = slice(jj * QW + dt % 2 * P, jj * QW + dt % 2 * P + P)
                    cols = slice(half * HALF, (half + 1) * HALF)
                    ins = three_products(pe, o, vh[:, q, w], vl[:, q, w], wh[:, par, jj, cols],
                                         wl[:, par, jj, cols], jj == 0, jj == JJ - 1)
                ins.then_inc(out_done, 1)

        def pe_whole(pe, g, par, first, last):
            hidden(pe, g)
            if not first:
                out(pe, g - 1, 1 - par)

        def pe_loaded(pe, g, par):
            out(pe, g - 1, 1 - par)

        def gated_high(act, g, par, jj):
            act.wait_ge(prod_done, g * JJ + jj + 3)
            if jj == 0:
                act.wait_ge(out_done, g * OUTS + OUTS)
            act.activation(wh[:, par, jj, :], prod[:, jj % 2, :], ACT.Copy).then_inc(w_high, 1)

        def act_whole(act, g, par, first, last):
            for jj in range(JJ):
                n = g * JJ + jj
                act.wait_ge(hid_done, n + 1)
                act.wait_ge(prod_done, n + 1)
                for half in range(2):
                    ins = act.activation(gelu[:, jj % 2, half * HALF:(half + 1) * HALF],
                                         core.psum[:, 2 * (jj % 2) + half, 0:HALF], ACT.Gelu)
                ins.then_inc(gelu_done, 1)
                if not (last and jj >= 2):
                    u.split_high(act, g + (jj + 2) // JJ, (jj + 2) % JJ)
                gated_high(act, g, par, jj)
            for q in range(4):
                split_v_high(act, g, q)

        def act_loaded(act, g, par):
            for q in range(4):
                gated_high(act, g, par, q)
                split_v_high(act, g, q)

        def gate(dve, g, par, jj, made):
            dve.wait_ge(*made)
            if jj == 0:
                dve.wait_ge(g_in[par], 8 * (g - par) + 16)
            dve.wait_ge(w_low, g * JJ + jj + 1)
            dve.tensor_tensor(prod[:, jj % 2, :], gelu[:, jj % 2, :], gates[:, par, :, jj],
                              ALU.mult).then_inc(prod_done, 1)

        def gated_low(dve, g, par, jj):
            dve.wait_ge(w_high, g * JJ + jj + 1)
            dve.tensor_tensor(wl[:, par, jj, :], prod[:, jj % 2, :], wh[:, par, jj, :].bitcast(F32),
                              ALU.subtract).then_inc(w_low, 1)

        def dve_whole(dve, g, par, first, last):
            for jj in range(JJ):
                gate(dve, g, par, jj, (gelu_done, g * JJ + jj + 3))
                gated_low(dve, g, par, jj)
            for q in range(4):
                if not first:
                    add_out(dve, g - 1, q)
                split_v_low(dve, g, q)

        def dve_loaded(dve, g, par):
            for q in range(4):
                gate(dve, g, par, q, (h_in[q % 2], g * 32 + (16 * (q // 2 + 1) - 32 * NH)))
                add_out(dve, g - 1, q)
                gated_low(dve, g, par, q)
                split_v_low(dve, g, q)

        def add_out(dve, g, q):
            for k in range(4 * q, 4 * q + 4):
                x = acts.x[:, k // 2, (k % 2) * HALF:(k % 2 + 1) * HALF]
                dve.wait_ge(out_done, g * OUTS + k + 1 + O2)
                dve.tensor_tensor(x, core.psum[:, 4 + k % 4, 0:HALF], x, ALU.add).then_inc(out_added, 1)

        norm = Norm(core, following, "n3", acts, 2, False, 0, sq=prod)

        def act_before(act):
            act.sem_inc(gelu_done, 2)

        def act_after(act):
            norm.act_squares(act, ready=lambda dt: (out_added, NG * OUTS + 4 - OUTS + 2 * dt + 2))

        def dve_before(dve):
            dve.sem_inc(prod_done, 2)
            dve.sem_inc(w_low, 2)
            dve.sem_inc(out_added, 4)

        def dve_after(dve):
            for q in range(4):
                add_out(dve, NG - 1, q)

        with nc.Block() as block:
            @block.sync
            def _(sp):
                groups(sp_whole, sp_loaded)(sp)

            @block.gpsimd
            def _(pool):
                for jj in range(2, JJ):
                    u.split_low(pool, 0, jj)
                with pool.Fori(0, NH - 1) as it:
                    for jj in range(JJ):
                        u.split_low(pool, it + 1, jj)

            @block.tensor
            def _(pe):
                pe.sem_inc(out_done, O2)
                groups(pe_whole, pe_loaded)(pe)
                out(pe, NG - 1, 1)
                norm.pe_sums(pe)

            @block.scalar
            def _(act):
                groups(act_whole, act_loaded, act_before, act_after)(act)

            @block.vector
            def _(dve):
                groups(dve_whole, dve_loaded, dve_before, dve_after)(dve)

        return norm


def finish(core, norm):
    nc, a = core.nc, core.a
    stored = core.sem("y_stored")
    norm.make_room()
    with nc.Block() as block:
        @block.sync
        def _(sp):
            for dt in range(DT):
                sp.wait_ge(norm.scaled, norm.b9 + dt + 2)
                sp.dma_start(a["y"][:, dt, :], norm.y[:, dt, :]).then_inc(stored, 16)
            sp.wait_ge(stored, 16 * DT)

        @block.scalar
        def _(act):
            norm.act_root(act)

        @block.vector
        def _(dve):
            norm.dve(dve)


def build(nc, a):
    with ExitStack() as ctx:
        core = Core(nc, ctx, a)
        x = core.sb("res_x", [P, DT, TOK])
        with ExitStack() as both:
            params = MixParams(core, both)
            project_in(core, params)
            mix(core, params, x)
        acts = Acts(core, ctx, "res", x)
        u = U(core, ctx)
        with ExitStack() as inner:
            sel = core.sb("picks_by_token", [P, 3, TOK], ctx=inner)
            numbers = core.sb("numbers", [P, N_KEYS], ctx=inner)
            with ExitStack() as both:
                jobs = route_jobs(2 * P_HEADS)
                tiles = [a["w_q"][n] if kind == "q" else a["u"][KEY4 + n] for kind, n in jobs]
                norm = Norm(core, both, "n2", acts, 1, True, 4)
                gemm = Gemm(core, both, "q", acts, len(jobs), tiles)
                project_out(core, acts, norm, gemm)
                route(core, norm, gemm, jobs, sel, numbers)
            spread_gates(core, acts, u, sel, numbers)
        norm = experts(core, acts, u, ctx)
        finish(core, norm)



_OUT = {
    "y": (P, DT, TOK), "shift_out": (P, RT, 2), "conv_out": (P, XT_, 2, CONV_W - 1),
    "wkv_out": (P, 2, 4, HD), "ssm_out": (P, 2, 4, HD),
}
_SCRATCH = {
    "pm": (P, RT, RWIN), "xbc": (P, XT_, XWIN), "z": (P, ZT, TOK), "dt": (8, 2, TOK),
    "gates": (NG, P, TOK, JJ), "hidden": (AHEAD4 + AHEAD5, P, TOK),
}


def lay_out(inp):
    f = {k: np.asarray(v) for k, v in inp.items()}

    def chan(x):
        x = np.asarray(x)
        x = x.reshape(x.shape[:-1] + (x.shape[-1] // P, P))
        return np.ascontiguousarray(np.moveaxis(np.moveaxis(x, -1, 0), -1, 1))

    def weight_tiles(w):
        r, c = w.shape
        return np.ascontiguousarray(w.reshape(r // P, P, c // P, P).transpose(2, 1, 0, 3).reshape(c // P, P, r))

    def rows(x):
        return np.broadcast_to(np.asarray(x).reshape(-1), (P, np.asarray(x).size))

    x = np.concatenate([f["x_prompt"][0], f["x_sample"][0]], 0)
    w_in = f["w_in"][0]
    z0, x0, d0 = R_PROJ, R_PROJ + M_WIDTH, R_PROJ + M_WIDTH + CONV_DIM
    pad = np.zeros((D_MODEL, P - HEADS), w_in.dtype)
    w_in = np.concatenate([w_in[:, :R_PROJ], w_in[:, x0:d0], w_in[:, z0:x0], w_in[:, d0:], pad], 1)
    shift = f["state_rwkv_shift"][0, 0]
    par1 = np.concatenate([
        chan(f["rwkv_mu"][0]), chan(shift), np.zeros((P, RT), np.float32),
        chan(f["mamba_conv_w"][0]).reshape(P, -1), chan(f["mamba_conv_b"][0]),
        chan(f["state_mamba_conv"][0, 0]).reshape(P, -1)], 1)

    def pair_states(s):
        return np.ascontiguousarray(s.reshape(4, 2, HD, HD).transpose(1, 3, 0, 2).reshape(P, 4, HD))

    def group_states(s):
        return np.ascontiguousarray(s.reshape(2, 4, HD, HD).transpose(0, 3, 1, 2).reshape(P, 4, HD))

    u = f["peer_u"][0].reshape(N_KEYS, N_KEYS, DT, P).transpose(1, 3, 2, 0).reshape(N_KEYS, P, DT * P)
    v = f["peer_v"][0].reshape(N_KEYS, NG, JJ, 4, D_MODEL // 4).transpose(1, 0, 3, 2, 4).reshape(NG, P, 4, D_MODEL)
    return {
        "x": chan(x), "w_in": weight_tiles(w_in), "w_out": weight_tiles(f["w_out"][0]),
        "w_q": weight_tiles(f["peer_w_q"][0]), "consts": shape_constants(),
        "ranks": np.broadcast_to(np.arange(P, dtype=np.float32), (P, P)),
        "norms": np.stack([chan(f["norm1_w"][0]), chan(f["norm2_w"][0]), chan(f["final_norm_w"])], 1),
        "par1": par1, "dtp": np.stack([f["mamba_dt_bias"][0], f["mamba_A_log"][0]], 1),
        "rows": np.stack([rows(f[k]) for k in ("rwkv_w0", "rwkv_a0", "rwkv_k_k", "rwkv_k_a", "rwkv_r_k",
                                               "rwkv_ln_w", "rwkv_ln_b", "mamba_norm_w")], 1),
        "mamba_D": rows(f["mamba_D"]), "w2": np.concatenate([f["rwkv_w2"][0], f["rwkv_a2"][0]], 0),
        "g2": f["rwkv_g2"][0], "wkv_in": pair_states(f["state_rwkv_wkv"][0, 0]),
        "ssm_in": group_states(f["state_mamba_ssm"][0, 0]),
        "keysT": np.ascontiguousarray(f["peer_sub_keys"][0].transpose(2, 0, 1)),
        "u": u, "v": v,
    }


def kernel(**inputs):
    import concourse.bacc as bacc
    from concourse.bass_utils import run_bass_kernel_spmd

    nc = bacc.Bacc("TRN2", target_bir_lowering=False, num_devices=1)
    arrays = {"arg_" + k: np.ascontiguousarray(v) for k, v in lay_out(inputs).items()}
    a = {k[4:]: nc.dram_tensor(k, v.shape, F32, kind="ExternalInput").ap() for k, v in arrays.items()}
    a.update({k: nc.dram_tensor("out_" + k, s, F32, kind="ExternalOutput").ap() for k, s in _OUT.items()})
    a.update({k: nc.dram_tensor("scratch_" + k, s, F32, kind="Internal").ap() for k, s in _SCRATCH.items()})
    build(nc, a)
    r = run_bass_kernel_spmd(nc, [arrays], core_ids=[0]).results[0]
    y = np.asarray(r["out_y"]).transpose(2, 1, 0).reshape(TOK, D_MODEL)
    shift = np.asarray(r["out_shift_out"]).transpose(2, 1, 0).reshape(2, R_PROJ)
    conv = np.asarray(r["out_conv_out"]).transpose(2, 3, 1, 0).reshape(2, CONV_W - 1, CONV_DIM)
    wkv = np.asarray(r["out_wkv_out"]).reshape(2, HD, 2, 4, HD).transpose(2, 3, 0, 4, 1).reshape(2, HEADS, HD, HD)
    ssm = np.asarray(r["out_ssm_out"]).reshape(2, HD, 2, 4, HD).transpose(2, 0, 3, 4, 1).reshape(2, HEADS, HD, HD)
    outs = [y[None, :SEQ], y[None, SEQ:]]
    for n in range(2):
        outs += [shift[None, n:n + 1], wkv[None, n:n + 1], conv[None, n:n + 1], ssm[None, n:n + 1]]
    return tuple(np.ascontiguousarray(o) for o in outs)
```
